# Optimizing a Trainium2 kernel written in Bass

```python
import math
import jax, jax.numpy as jnp
from jax import lax
import numpy as np

D_MODEL = 1024
BATCH = 1
SEQ = 512
DEPTH = 1

CONV_WIDTH = D_MODEL
CONV_K = 3
N_HEADS = 8
HEAD_DIM = D_MODEL // (2 * N_HEADS)
V_DIM = 2 * HEAD_DIM
ATTN_QK = N_HEADS * 2 * HEAD_DIM
ATTN_V = N_HEADS * V_DIM
ROT_DIM = HEAD_DIM // 4
ROPE_THETA = 500000.0
Q_BLOCK = 128
N_KEYS = 128
N_EXPERTS = N_KEYS * N_KEYS
PK_HEADS = 8
PK_DIM = 256
PK_HALF = PK_DIM // 2
PK_TOPK = 16
PEER_CHUNK = 128
ALPHA = (2 * DEPTH) ** 0.25
BETA = (8 * DEPTH) ** -0.25
LN_EPS = 1e-5
IN_WIDTHS = (CONV_WIDTH, CONV_WIDTH, CONV_WIDTH, ATTN_QK, ATTN_QK, ATTN_V, 2 * D_MODEL)

kernel_name = "hybrid_conv_diffattn_peer_deepnorm"

def _layernorm(x, g, b):
    xf = x.astype(jnp.float32)
    mu = jnp.mean(xf, axis=-1, keepdims=True)
    var = jnp.mean(jnp.square(xf - mu), axis=-1, keepdims=True)
    y = (xf - mu) * lax.rsqrt(var + LN_EPS) * g.astype(jnp.float32) + b.astype(jnp.float32)
    return y.astype(x.dtype)

def _rmsnorm(x, g):
    xf = x.astype(jnp.float32)
    y = xf * lax.rsqrt(jnp.mean(jnp.square(xf), axis=-1, keepdims=True) + LN_EPS)
    return y * g.astype(jnp.float32)

def _partial_rope(t, cos, sin):
    half = ROT_DIM // 2
    c = cos[:, :, None, None, :]
    s = sin[:, :, None, None, :]
    r1 = t[..., :half].astype(jnp.float32)
    r2 = t[..., half:ROT_DIM].astype(jnp.float32)
    rot = jnp.concatenate([r1 * c - r2 * s, r2 * c + r1 * s], axis=-1).astype(t.dtype)
    return jnp.concatenate([rot, t[..., ROT_DIM:]], axis=-1)

def _short_conv_mixer(h, b_gate, c_gate, conv_w, conv_b):
    z = c_gate * h
    seq = z.shape[1]
    zp = jnp.pad(z, ((0, 0), (CONV_K - 1, 0), (0, 0)))
    y = conv_b + sum(conv_w[j] * zp[:, j:j + seq] for j in range(CONV_K))
    return b_gate * y

def _diff_attention(q, k, v, lam):
    bsz, seq = q.shape[0], q.shape[1]
    nblk = seq // Q_BLOCK
    scale = HEAD_DIM ** -0.5
    kf = k.astype(jnp.float32)
    vf = v.astype(jnp.float32)
    qb = q.reshape(bsz, nblk, Q_BLOCK, N_HEADS, 2, HEAD_DIM).transpose(1, 0, 2, 3, 4, 5)
    kpos = jnp.arange(seq)

    def block(args):
        q_blk, start = args
        s = jnp.einsum('bqhcd,bkhcd->bhcqk', q_blk.astype(jnp.float32), kf) * scale
        qpos = start + jnp.arange(Q_BLOCK)
        mask = kpos[None, :] <= qpos[:, None]
        s = jnp.where(mask, s, -jnp.inf)
        p = jax.nn.softmax(s, axis=-1)
        a = p[:, :, 0] - lam * p[:, :, 1]
        return jnp.einsum('bhqk,bkhe->bqhe', a, vf)

    out = lax.map(block, (qb, jnp.arange(nblk) * Q_BLOCK))
    return out.transpose(1, 0, 2, 3, 4).reshape(bsz, seq, N_HEADS, V_DIM)

def _peer(x, w_pq, sub_keys, u_tab, v_tab):
    bsz, seq, dm = x.shape
    xt = x.reshape(-1, PEER_CHUNK, dm)

    def chunk(xc):
        q = (xc @ w_pq).reshape(PEER_CHUNK, PK_HEADS, 2, PK_HALF)
        s = jnp.einsum('thcd,hcnd->thcn', q.astype(jnp.float32), sub_keys.astype(jnp.float32))
        s1, i1 = lax.top_k(s[:, :, 0], PK_TOPK)
        s2, i2 = lax.top_k(s[:, :, 1], PK_TOPK)
        cand = (s1[..., :, None] + s2[..., None, :]).reshape(PEER_CHUNK, PK_HEADS, PK_TOPK * PK_TOPK)
        top_s, top_i = lax.top_k(cand, PK_TOPK)
        e_idx = (jnp.take_along_axis(i1, top_i // PK_TOPK, axis=-1) * N_KEYS
                 + jnp.take_along_axis(i2, top_i % PK_TOPK, axis=-1))
        g = jax.nn.softmax(top_s, axis=-1)
        u_sel = u_tab[e_idx]
        v_sel = v_tab[e_idx]
        act = jax.nn.gelu(jnp.einsum('thkd,td->thk', u_sel, xc).astype(jnp.float32), approximate=False)
        w = (g * act).astype(xc.dtype)
        return jnp.einsum('thk,thkd->td', w, v_sel)

    return lax.map(chunk, xt).reshape(bsz, seq, dm)

def setup_inputs(seed: int = 0) -> dict:
    key = jax.random.key(seed)
    ks = jax.random.split(key, 24)
    f32 = jnp.float32
    D = D_MODEL
    sd = D ** -0.5
    nrm = lambda k, shape, s: jax.random.normal(k, shape, f32) * s
    x = jax.random.normal(ks[0], (BATCH, SEQ, D), f32)
    offs = jax.random.randint(ks[1], (BATCH, 1), 0, 4096, dtype=jnp.int32)
    positions = offs + jnp.arange(SEQ, dtype=jnp.int32)[None, :]
    w_in = jnp.concatenate([
        nrm(ks[2], (DEPTH, D, 3 * CONV_WIDTH + 2 * ATTN_QK), sd),
        nrm(ks[3], (DEPTH, D, ATTN_V), sd * BETA),
        nrm(ks[4], (DEPTH, D, 2 * D), sd)], axis=-1)
    return {
        "x": x,
        "positions": positions,
        "w_in": w_in,
        "conv_w": nrm(ks[5], (DEPTH, CONV_K, CONV_WIDTH), CONV_K ** -0.5),
        "conv_b": nrm(ks[6], (DEPTH, CONV_WIDTH), 0.02),
        "gate_b": nrm(ks[7], (DEPTH, 2 * D), 0.1),
        "lambda_q1": nrm(ks[8], (DEPTH, HEAD_DIM), 0.1),
        "lambda_k1": nrm(ks[9], (DEPTH, HEAD_DIM), 0.1),
        "lambda_q2": nrm(ks[10], (DEPTH, HEAD_DIM), 0.1),
        "lambda_k2": nrm(ks[11], (DEPTH, HEAD_DIM), 0.1),
        "subln_g": 1.0 + nrm(ks[12], (DEPTH, V_DIM), 0.02),
        "w_conv_out": nrm(ks[13], (DEPTH, CONV_WIDTH, D), CONV_WIDTH ** -0.5),
        "w_attn_out": nrm(ks[14], (DEPTH, ATTN_V, D), ATTN_V ** -0.5),
        "w_o": nrm(ks[15], (DEPTH, D, D), sd * BETA),
        "ln1_g": 1.0 + nrm(ks[16], (DEPTH, D), 0.02),
        "ln1_b": nrm(ks[17], (DEPTH, D), 0.02),
        "w_pq": nrm(ks[18], (DEPTH, D, PK_HEADS * PK_DIM), sd),
        "sub_keys": nrm(ks[19], (DEPTH, PK_HEADS, 2, N_KEYS, PK_HALF), PK_HALF ** -0.5),
        "u_tab": nrm(ks[20], (DEPTH, N_EXPERTS, D), sd),
        "v_tab": nrm(ks[21], (DEPTH, N_EXPERTS, D), BETA),
        "ln2_g": 1.0 + nrm(ks[22], (DEPTH, D), 0.02),
        "ln2_b": nrm(ks[23], (DEPTH, D), 0.02),
    }

def reference(x, positions, w_in, conv_w, conv_b, gate_b, lambda_q1, lambda_k1, lambda_q2, lambda_k2,
              subln_g, w_conv_out, w_attn_out, w_o, ln1_g, ln1_b, w_pq, sub_keys, u_tab, v_tab,
              ln2_g, ln2_b):
    bsz, seq, _ = x.shape
    split_points = np.cumsum(IN_WIDTHS)[:-1].tolist()
    inv_freq = ROPE_THETA ** (-jnp.arange(0, ROT_DIM, 2, dtype=jnp.float32) / ROT_DIM)
    ang = positions.astype(jnp.float32)[..., None] * inv_freq
    cos, sin = jnp.cos(ang), jnp.sin(ang)
    for l in range(DEPTH):
        proj = x @ w_in[l]
        h, bg, cg, q, k, v, gates = jnp.split(proj, split_points, axis=-1)
        y_conv = _short_conv_mixer(h, bg, cg, conv_w[l], conv_b[l])
        q = _partial_rope(q.reshape(bsz, seq, N_HEADS, 2, HEAD_DIM), cos, sin)
        k = _partial_rope(k.reshape(bsz, seq, N_HEADS, 2, HEAD_DIM), cos, sin)
        lam_init = 0.8 - 0.6 * math.exp(-0.3 * l)
        lam = (jnp.exp(jnp.sum(lambda_q1[l].astype(jnp.float32) * lambda_k1[l].astype(jnp.float32)))
               - jnp.exp(jnp.sum(lambda_q2[l].astype(jnp.float32) * lambda_k2[l].astype(jnp.float32)))
               + lam_init)
        o = _diff_attention(q, k, v.reshape(bsz, seq, N_HEADS, V_DIM), lam)
        o = _rmsnorm(o, subln_g[l]) * (1.0 - lam_init)
        y_attn = o.reshape(bsz, seq, ATTN_V).astype(x.dtype)
        g = jax.nn.sigmoid(gates + gate_b[l])
        g_conv, g_attn = g[..., :D_MODEL], g[..., D_MODEL:]
        merged = g_conv * (y_conv @ w_conv_out[l]) + g_attn * (y_attn @ w_attn_out[l])
        x = _layernorm(ALPHA * x + merged @ w_o[l], ln1_g[l], ln1_b[l])
        x = _layernorm(ALPHA * x + _peer(x, w_pq[l], sub_keys[l], u_tab[l], v_tab[l]), ln2_g[l], ln2_b[l])
    return x


_drawn_inputs = setup_inputs


def setup_inputs(seed=0):
    import zlib

    import numpy as np

    out = dict(_drawn_inputs(seed))
    spreads = {}
    factors = {'conv_b': 2.79,
     'lambda_k1': 4.868,
     'lambda_q2': 5.317,
     'subln_g': 3.32,
     'ln2_g': 2.826,
     'ln2_b': 2.909}
    for name, (base, spread) in spreads.items():
        noise = np.random.default_rng([zlib.crc32(name.encode()), seed]).standard_normal(out[name].shape)
        drawn = base * np.exp(spread * noise) if base else spread * noise
        out[name] = __import__('jax').numpy.asarray(drawn.astype(out[name].dtype))
    for name, factor in factors.items():
        out[name] = (out[name] * factor).astype(out[name].dtype)
    return out
```

```python
import math
from contextlib import ExitStack

import concourse.bass as bass
import numpy as np
from concourse import mybir

F32 = mybir.dt.float32
F32R = mybir.dt.float32r
I32 = mybir.dt.int32
U32 = mybir.dt.uint32
ACT = mybir.ActivationFunctionType
ALU = mybir.AluOpType
AX = mybir.AxisListType

P = 128
D = 1024
T = 512
DT = D // P
TT = T // P
HEADS = 8
HD = 64
CW = 256
SLOTS = 2
PK_HEADS = 8
TOPK = 16
N_KEYS = 128
ALPHA = 2 ** 0.25
LAM_INIT = 0.8 - 0.6 * math.exp(0.0)
LN_EPS = 1e-5
SCALE = HD ** -0.5
ROT_DIM = HD // 4
ROPE_THETA = 500000.0
NEG = -3.0e38
GROUP = 4
TOK = 32
PER_TILE = T // N_KEYS

MIX_ROUNDS, MIX_CHUNKS = 4, 6
MERGE_ROUNDS, MERGE_CHUNKS = 4, 4
WO_ROUNDS, WO_CHUNKS = 2, 2
PQ_ROUNDS, PQ_CHUNKS = 4, 2
MIX_0 = 0
MERGE_0 = MIX_0 + MIX_ROUNDS * MIX_CHUNKS
WO_0 = MERGE_0 + MERGE_ROUNDS * MERGE_CHUNKS
PQ_0 = WO_0 + WO_ROUNDS * WO_CHUNKS
CHUNKS = PQ_0 + PQ_ROUNDS * PQ_CHUNKS


def f32(ap):
    return ap.bitcast(F32)


def row(ap, at):
    return ap[:, bass.ds(at, 1)].rearrange("p a n -> p (a n)")


class Chain:

    def __init__(self, engine, sem):
        self.engine, self.sem, self.n, self.base = engine, sem, 0, 0

    def step(self, instruction):
        self.n += 1
        instruction.then_inc(self.sem, 1)
        self.engine.wait_ge(self.sem, self.base + self.n)

    def round(self, i, per):
        self.start, self.per = self.base + self.n, per
        self.base, self.n = self.start + i * per, 0

    def done(self, rounds):
        assert self.n == self.per, (self.n, self.per)
        self.base, self.n = self.start + rounds * self.per, 0


class Stream:

    def __init__(self, nc, ctx, source):
        self.nc, self.source = nc, source
        self.raw, self.hi, self.lo = tiles(
            nc, ctx, ("w_raw", [P, SLOTS, DT, CW], F32), ("w_hi", [P, SLOTS, DT, CW], F32R),
            ("w_lo", [P, SLOTS, DT, CW], F32R), side="right")
        self.raw_loaded = [ctx.enter_context(nc.semaphore(f"w_raw_loaded{s}")) for s in range(SLOTS)]
        self.hi_ready = ctx.enter_context(nc.semaphore("w_hi_ready"))
        self.lo_ready = ctx.enter_context(nc.semaphore("w_lo_ready"))
        self.unit_done = ctx.enter_context(nc.semaphore("unit_done"))
        self.bank_free = ctx.enter_context(nc.semaphore("proj_bank_free"))

    def load(self, sp, n, m):
        sp.wait_ge(self.lo_ready, n + 1)
        sp.dma_start(self.raw[:, m], self.source[n]).then_inc(self.raw_loaded[m], 16)

    def load_stage(self, sp, first, last):
        with sp.Fori(0, (min(last, CHUNKS - 2) - first) // 2) as i:
            for m in range(2):
                self.load(sp, 2 * i + first + 2 + m, m)

    def take_hi(self, act, n, m):
        act.wait_ge(self.raw_loaded[m % 2], (n - m % 2) * 8 + 16)
        if not isinstance(n, int) or n >= 2:
            act.wait_ge(self.unit_done, 2 * n - 2)
        self.nc.scalar.activation(self.hi[:, m % 2], self.raw[:, m % 2], ACT.Copy).then_inc(self.hi_ready, 1)

    def take_lo(self, pool, n, m):
        pool.wait_ge(self.hi_ready, n + 1)
        self.nc.gpsimd.tensor_tensor(self.lo[:, m % 2], self.raw[:, m % 2], f32(self.hi[:, m % 2]),
                                     ALU.subtract).then_inc(self.lo_ready, 1)

    def columns(self, pe, out, n, m, half, right_hi, right_lo):
        if half == 0:
            pe.wait_ge(self.lo_ready, n + 1 + SLOTS)
        pe.wait_ge(self.bank_free, 2 * n + half + 1)
        for c in range(DT):
            hi = self.hi[:, m % 2, c, P * half:P * half + P]
            lo = self.lo[:, m % 2, c, P * half:P * half + P]
            self.nc.tensor.matmul(out, hi, right_hi[:, c, :], start=(c == 0), stop=False)
            self.nc.tensor.matmul(out, hi, right_lo[:, c, :], start=False, stop=False)
            last = self.nc.tensor.matmul(out, lo, right_hi[:, c, :], start=False, stop=(c == DT - 1))
        last.then_inc(self.unit_done, 1)

    def rows(self, pe, outs, n, m, left_hi, left_lo):
        pe.wait_ge(self.lo_ready, n + 1 + SLOTS)
        for half in range(2):
            pe.wait_ge(self.bank_free, 2 * n + half + 1)
            for k in range(2):
                tokens = slice(P * (2 * half + k), P * (2 * half + k) + P)
                to = outs[half][:, CW * k:CW * k + CW]
                for c in range(DT):
                    hi, lo = self.hi[:, m % 2, c], self.lo[:, m % 2, c]
                    self.nc.tensor.matmul(to, left_hi[:, c, tokens], hi, start=(c == 0), stop=False)
                    self.nc.tensor.matmul(to, left_hi[:, c, tokens], lo, start=False, stop=False)
                    last = self.nc.tensor.matmul(to, left_lo[:, c, tokens], hi, start=False, stop=(c == DT - 1))
            last.then_inc(self.unit_done, 1)

    def evacuate(self, act, n, half, to, bank, func=ACT.Copy, **kw):
        act.wait_ge(self.unit_done, 2 * n + half + 1)
        self.nc.scalar.activation(to, bank, func, **kw).then_inc(self.bank_free, 1)

    def wait_out(self, engine, n, half):
        engine.wait_ge(self.bank_free, SLOTS + 2 * n + half + 1)


def take_los(pool, stream, first, rounds, per, ahead):
    with pool.Fori(0, rounds if ahead else rounds - 1) as j:
        for m in range(per):
            stream.take_lo(pool, first + per * j + m + 1, m + 1)
    if not ahead:
        for m in range(per - 1):
            stream.take_lo(pool, first + per * (rounds - 1) + m + 1, m + 1)


def tiles(nc, ctx, *named, side="left"):
    return [ctx.enter_context(nc.sbuf_tensor(name, shape, dtype, side=side)) for name, shape, dtype in named]


def banks(nc, ctx, *named):
    return [ctx.enter_context(nc.psum_tensor(name, [P, n, 512], F32)) for name, n in named]


def sems(nc, ctx, names):
    return [ctx.enter_context(nc.semaphore(n)) for n in names.split()]


def mixers(nc, a, stream, identity, xT, conv, attn):
    MAGIC = 1.5 * 2.0 ** 23
    TURN = 2 * math.pi
    TURN_1, TURN_2 = 6.28125, float(np.float32(TURN - 6.28125))
    TURN_3 = TURN - TURN_1 - TURN_2
    HALF_TURN = float(np.nextafter(np.float32(math.pi), np.float32(0)))
    CONSTS = 12
    with ExitStack() as ctx:
        (raws, cosT, sinT, part, qT, kT, v, probs, diff, diffT, z, y, o, mask, swap, freq,
         conv_w, conv_b, subln, lam_in, lam, stat, o_stat) = tiles(
            nc, ctx, ("raws", [P, 8, T], F32),
            ("cosT", [P, T], F32), ("sinT", [P, T], F32), ("part", [P, T], F32),
            ("qT", [P, 2, T], F32), ("kT", [P, 2, T], F32), ("v", [P, TT, CW], F32),
            ("probs", [P, 2, 2, T], F32), ("diff", [P, 2, T], F32), ("diffT", [P, 10, P], F32),
            ("z", [P, T + 2], F32), ("y", [P, T], F32),
            ("o", [P, 2 * TT, P], F32), ("mask", [P, P], F32),
            ("swap", [P, P], F32), ("freq", [P, 1], F32), ("conv_w", [P, 3, DT], F32),
            ("conv_b", [P, DT], F32), ("subln", [P, P], F32), ("lam_in", [P, 4, HD], F32),
            ("lam", [P, 8], F32), ("stat", [P, 2, 10], F32), ("o_stat", [P, 3, 2 * TT], F32))
        position = kT[:, 1].bitcast(I32)
        proj, scores, turn, pv = banks(nc, ctx, ("proj", 2), ("scores", 4), ("turn", 1), ("pv", 1))
        (x_loaded, const_loaded, x_hi, x_split, tables_ready, sin_ready, lam_exp, swap_done, qk_ready,
         score_done, bias_ready, exp_done, diff_ready, turned, diffT_ready, pv_done, o_ready, sums_ready,
         root_ready, y_ready, y_turned, y_hi, y_split, conv_done, dve_step) = sems(
            nc, ctx, "x_loaded const_loaded x_hi x_split tables_ready sin_ready lam_exp swap_done "
            "qk_ready score_done bias_ready exp_done diff_ready turned diffT_ready pv_done o_ready "
            "sums_ready root_ready y_ready y_turned y_hi y_split conv_done dve_step")
        squares = raws[:, 6:8, :].rearrange("p a (t n) -> p (a t) n", n=P)
        RAW = {0: 0, 1: 2, 3: 4, 4: 0, 5: 2}
        block = ctx.enter_context(nc.Block())

        @block.sync
        def _(sp):
            sp.dma_start(raws[:], a["x_columns"]).then_inc(x_loaded, 16)
            for m in range(2):
                sp.dma_start(stream.raw[:, m], stream.source[m]).then_inc(stream.raw_loaded[m], 16)
            sp.dma_start(identity[:], a["identity"]).then_inc(const_loaded, 16)
            sp.dma_start(position, a["positions"].broadcast_to([P, T])).then_inc(const_loaded, 16)
            sp.dma_start(freq[:], a["freq"]).then_inc(const_loaded, 16)
            sp.dma_start(mask[:], a["mask"]).then_inc(const_loaded, 16)
            sp.dma_start(swap[:], a["swap"]).then_inc(const_loaded, 16)
            sp.dma_start(subln[:], a["subln_g"].broadcast_to([P, P])).then_inc(const_loaded, 16)
            for n, name in enumerate(("lambda_q1", "lambda_k1", "lambda_q2", "lambda_k2")):
                sp.dma_start(lam_in[:, n], a[name].broadcast_to([P, HD])).then_inc(const_loaded, 16)
            sp.dma_start(conv_b[:], a["conv_b_columns"]).then_inc(const_loaded, 16)
            sp.dma_start(conv_w[:], a["conv_w_columns"]).then_inc(const_loaded, 16)
            stream.load_stage(sp, MIX_0, MERGE_0)

        @block.gpsimd
        def _(pool):
            pool.sem_inc(stream.lo_ready, SLOTS)
            stream.take_lo(pool, 0, 0)
            take_los(pool, stream, MIX_0, MIX_ROUNDS, MIX_CHUNKS, True)

        @block.tensor
        def _(pe):
            pe.sem_inc(turned, 2)
            pe.wait_ge(const_loaded, 16 * CONSTS)
            pe.wait_ge(x_split, DT)

            def project(j, m, half):
                stream.columns(pe, proj[:, half], MIX_0 + MIX_CHUNKS * j + m, m, half, *xT)

            def rotate_halves(j, m):
                for half in range(2):
                    stream.wait_out(pe, MIX_0 + MIX_CHUNKS * j + m, half)
                    if m == 0 and half == 0:
                        pe.wait_ge(y_split, 2 * j)
                    pe.wait_ge(qk_ready, 4 * j + 2 * m + half)
                    nc.tensor.matmul(turn[:, 0], swap[:], raws[:, RAW[m] + half], start=True,
                                     stop=True).then_inc(swap_done, 1)

            def score(j, head, tile):
                u = 8 * j + 4 * head + tile
                n = P * (tile + 1)
                pe.wait_ge(qk_ready, 4 * j + 4)
                pe.wait_ge(exp_done, 2 * u)
                for c in range(2):
                    rows = slice(HD * c, HD * c + HD)
                    last = nc.tensor.matmul(scores[:, 2 * (tile % 2) + c, 0:n],
                                            qT[rows, head, P * tile:P * tile + P], kT[rows, head, 0:n],
                                            start=True, stop=True)
                last.then_inc(score_done, 1)

            def turn_diff(j, head, tile):
                u = 8 * j + 4 * head + tile
                pe.wait_ge(diff_ready, u + 3)
                pe.wait_ge(diffT_ready, u)
                for b in range(tile + 1):
                    last = nc.tensor.transpose(turn[:, 0, P * b:P * b + P], diff[:, tile % 2, P * b:P * b + P],
                                               identity[:])
                last.then_inc(turned, 1)

            def values(j, head):
                pe.wait_ge(diffT_ready, 8 * j + 4 * head + 4)
                stream.wait_out(pe, MIX_0 + MIX_CHUNKS * j + 2, 1)
                pe.wait_ge(o_ready, 2 * j + head)
                for tile in range(TT):
                    at = tile * (tile + 1) // 2
                    for b in range(tile + 1):
                        last = nc.tensor.matmul(pv[:, 0, P * tile:P * tile + P], diffT[:, at + b],
                                                v[:, b, P * head:P * head + P], start=(b == 0), stop=(b == tile))
                last.then_inc(pv_done, 1)

            def turn_y(j, head):
                pe.wait_ge(y_ready, j + 1)
                pe.wait_ge(diffT_ready, 8 * j + 8)
                pe.wait_ge(y_split, 2 * j + head)
                for tile in range(TT):
                    last = nc.tensor.transpose(turn[:, 0, P * tile:P * tile + P], o[:, TT * head + tile],
                                               identity[:])
                last.then_inc(y_turned, 1)

            def round_of(j, first):
                project(j, 0, 0)
                project(j, 0, 1)
                project(j, 1, 0)
                if not first:
                    turn_y(j - 1, 0)
                project(j, 1, 1)
                if not first:
                    turn_y(j - 1, 1)
                rotate_halves(j, 0)
                stream.rows(pe, [proj[:, half] for half in range(2)], MIX_0 + MIX_CHUNKS * j + 2, 2, *xT)
                rotate_halves(j, 1)
                project(j, 3, 0)
                score(j, 0, 0)
                score(j, 0, 1)
                project(j, 3, 1)
                score(j, 0, 2)
                score(j, 0, 3)
                project(j, 4, 0)
                for tile in range(2):
                    turn_diff(j, 0, tile)
                score(j, 1, 0)
                score(j, 1, 1)
                project(j, 4, 1)
                for tile in range(2, TT):
                    turn_diff(j, 0, tile)
                values(j, 0)
                score(j, 1, 2)
                score(j, 1, 3)
                project(j, 5, 0)
                for tile in range(TT):
                    turn_diff(j, 1, tile)
                values(j, 1)
                project(j, 5, 1)

            round_of(0, True)
            with pe.Fori(1, MIX_ROUNDS) as j:
                round_of(j, False)
            turn_y(MIX_ROUNDS - 1, 0)
            turn_y(MIX_ROUNDS - 1, 1)

        @block.scalar
        def _(act):
            act.sem_inc(stream.bank_free, SLOTS)
            act.sem_inc(exp_done, 2)
            stream.take_hi(act, 0, 0)
            act.wait_ge(x_loaded, 16)
            for c in range(DT):
                nc.scalar.activation(xT[0][:, c], raws[:, c], ACT.Copy).then_inc(x_hi, 1)
            act.wait_ge(tables_ready, 1)
            nc.scalar.activation(sinT[:], sinT[:], ACT.Sin).then_inc(sin_ready, 1)
            nc.scalar.activation(cosT[:], cosT[:], ACT.Sin).then_inc(sin_ready, 1)
            nc.scalar.activation(lam[:, 2:4], lam[:, 0:2], ACT.Exp).then_inc(lam_exp, 1)

            def bring(j, m, half, free, value):
                act.wait_ge(free, value)
                stream.evacuate(act, MIX_0 + MIX_CHUNKS * j + m, half, raws[:, RAW[m] + half], proj[:, half])

            def exponentials(j, head, tile):
                n = P * (tile + 1)
                u = 8 * j + 4 * head + tile
                act.wait_ge(bias_ready, u + 1)
                act.wait_ge(diff_ready, u + 1)
                for c in range(2):
                    nc.scalar.activation(probs[:, tile % 2, c, 0:n], scores[:, 2 * (tile % 2) + c, 0:n], ACT.Exp,
                                         bias=stat[:, tile % 2, 2 + c:3 + c], scale=SCALE,
                                         accum_out=stat[:, tile % 2, 4 + c:5 + c]).then_inc(exp_done, 1)

            def bring_diffT(j, head, tile):
                u = 8 * j + 4 * head + tile
                act.wait_ge(turned, u + 3)
                act.wait_ge(pv_done, 2 * j + head)
                at = tile * (tile + 1) // 2
                nc.scalar.activation(diffT[:, at:at + tile + 1],
                                     turn[:, 0, 0:P * (tile + 1)].rearrange("p (b n) -> p b n", n=P),
                                     ACT.Copy).then_inc(diffT_ready, 1)

            def bring_o(j, head):
                act.wait_ge(pv_done, 2 * j + head + 1)
                act.wait_ge(y_turned, 2 * j)
                nc.scalar.activation(o[:, TT * head:TT * head + TT], pv[:, 0].rearrange("p (t n) -> p t n", n=P),
                                     ACT.Copy).then_inc(o_ready, 1)

            def bring_y_hi(j, head):
                act.wait_ge(y_turned, 2 * j + head + 1)
                nc.scalar.activation(row(attn[0], 2 * j + head), turn[:, 0], ACT.Copy).then_inc(y_hi, 1)

            def round_of(j, first):
                def ahead(m):
                    stream.take_hi(act, MIX_0 + MIX_CHUNKS * j + m + 1, m + 1)

                for m in range(2):
                    ahead(m)
                    for half in range(2):
                        bring(j, m, half, conv_done, 2 * j)
                        if m == 1 and not first:
                            bring_y_hi(j - 1, half)
                ahead(2)
                act.wait_ge(pv_done, 2 * j)
                for half in range(2):
                    stream.evacuate(act, MIX_0 + MIX_CHUNKS * j + 2, half, v[:, 2 * half:2 * half + 2],
                                    proj[:, half].rearrange("p (k n) -> p k n", k=2))
                ahead(3)
                bring(j, 3, 0, conv_done, 2 * j)
                exponentials(j, 0, 0)
                exponentials(j, 0, 1)
                bring(j, 3, 1, conv_done, 2 * j)
                exponentials(j, 0, 2)
                exponentials(j, 0, 3)
                ahead(4)
                bring(j, 4, 0, qk_ready, 4 * j + 2)
                bring_diffT(j, 0, 0)
                bring_diffT(j, 0, 1)
                exponentials(j, 1, 0)
                exponentials(j, 1, 1)
                bring(j, 4, 1, qk_ready, 4 * j + 2)
                bring_diffT(j, 0, 2)
                bring_diffT(j, 0, 3)
                bring_o(j, 0)
                exponentials(j, 1, 2)
                exponentials(j, 1, 3)
                ahead(5)
                bring(j, 5, 0, qk_ready, 4 * j + 4)
                for tile in range(TT):
                    bring_diffT(j, 1, tile)
                bring_o(j, 1)
                bring(j, 5, 1, qk_ready, 4 * j + 4)
                act.wait_ge(sums_ready, j + 1)
                nc.scalar.activation(o_stat[:, 1], o_stat[:, 0], ACT.Sqrt, bias=lam[:, 7:8],
                                     scale=1.0 / P).then_inc(root_ready, 1)

            round_of(0, True)
            with act.Fori(1, MIX_ROUNDS) as j:
                round_of(j, False)
            for head in range(2):
                bring_y_hi(MIX_ROUNDS - 1, head)

        @block.vector
        def _(dve):
            v_ = nc.vector
            chain = Chain(dve, dve_step)
            step = chain.step
            dve.sem_inc(diff_ready, 2)
            for c in range(DT):
                dve.wait_ge(x_hi, c + 1)
                v_.tensor_tensor(xT[1][:, c], raws[:, c], f32(xT[0][:, c]), ALU.subtract).then_inc(x_split, 1)
            step(v_.memset(z[:, 0:2], 0.0))
            step(v_.memset(lam[:, 7:8], LN_EPS))
            dve.wait_ge(const_loaded, 16 * CONSTS)
            step(v_.tensor_copy(part[:], position))
            step(v_.tensor_scalar(y[:], part[:], freq[:, 0:1], None, ALU.mult))
            for to, quarter in ((sinT, 0.0), (cosT, 0.25)):
                step(v_.tensor_scalar(part[:], y[:], 1 / TURN, quarter, ALU.mult, ALU.add))
                step(v_.tensor_scalar(part[:], part[:], MAGIC, None, ALU.add))
                step(v_.tensor_scalar(part[:], part[:], -MAGIC, None, ALU.add))
                step(v_.scalar_tensor_tensor(to[:], part[:], -TURN_1, y[:], ALU.mult, ALU.add))
                step(v_.scalar_tensor_tensor(to[:], part[:], -TURN_2, to[:], ALU.mult, ALU.add))
                step(v_.scalar_tensor_tensor(to[:], part[:], -TURN_3, to[:], ALU.mult, ALU.add))
                step(v_.tensor_scalar(to[:], to[:], quarter * TURN, None, ALU.add))
                step(v_.tensor_scalar(to[:], to[:], HALF_TURN, -HALF_TURN, ALU.min, ALU.max))
            for n in range(2):
                step(v_.tensor_tensor(part[:, 0:HD], lam_in[:, 2 * n], lam_in[:, 2 * n + 1], ALU.mult))
                last = v_.tensor_reduce(lam[:, n:n + 1], part[:, 0:HD], AX.X, ALU.add)
                if n == 0:
                    step(last)
            last.then_inc(tables_ready, 1)
            dve.wait_ge(lam_exp, 1)
            step(v_.tensor_tensor(lam[:, 4:5], lam[:, 3:4], lam[:, 2:3], ALU.subtract))
            step(v_.tensor_scalar(lam[:, 5:6], lam[:, 4:5], -LAM_INIT, None, ALU.add))
            dve.wait_ge(sin_ready, 2)

            def rotate(j, m, half, to):
                dve.wait_ge(swap_done, 4 * j + 2 * m + half + 1)
                dve.wait_ge(score_done, 8 * j)
                step(v_.tensor_tensor(part[:], raws[:, RAW[m] + half], cosT[:], ALU.mult))
                step(v_.tensor_tensor(y[:], turn[:, 0], sinT[:], ALU.mult))
                v_.tensor_tensor(to[:, half], part[:], y[:], ALU.add).then_inc(qk_ready, 1)

            def maximum(j, head, tile):
                u = 8 * j + 4 * head + tile
                both = slice(2 * (tile % 2), 2 * (tile % 2) + 2)
                dve.wait_ge(score_done, u + 1)
                diagonal = scores[:, both, P * tile:P * tile + P]
                step(v_.tensor_tensor(diagonal, diagonal, mask[:, None, :].broadcast_to([P, 2, P]), ALU.add))
                step(v_.tensor_reduce(stat[:, tile % 2, 0:2], scores[:, both, 0:P * (tile + 1)], AX.X, ALU.max))
                v_.tensor_scalar(stat[:, tile % 2, 2:4], stat[:, tile % 2, 0:2], -SCALE, None,
                                 ALU.mult).then_inc(bias_ready, 1)

            def difference(j, head, tile):
                u = 8 * j + 4 * head + tile
                n = P * (tile + 1)
                s = tile % 2
                dve.wait_ge(exp_done, 2 * u + 4)
                dve.wait_ge(turned, u + 1)
                step(v_.reciprocal(stat[:, s, 6:8], stat[:, s, 4:6]))
                step(v_.tensor_tensor(stat[:, s, 8:9], stat[:, s, 7:8], lam[:, 5:6], ALU.mult))
                step(v_.tensor_scalar(diff[:, s, 0:n], probs[:, s, 1, 0:n], stat[:, s, 8:9], None, ALU.mult))
                v_.scalar_tensor_tensor(diff[:, s, 0:n], probs[:, s, 0, 0:n], stat[:, s, 6:7], diff[:, s, 0:n],
                                        ALU.mult, ALU.add).then_inc(diff_ready, 1)

            def short_conv(j, half):
                at = 2 * j + half
                stream.wait_out(dve, MIX_0 + MIX_CHUNKS * j + 5, half)
                step(v_.tensor_tensor(z[:, 2:T + 2], raws[:, RAW[5] + half], raws[:, RAW[3] + half], ALU.mult))
                step(v_.tensor_scalar(y[:], z[:, 2:T + 2], conv_w[:, 2, bass.ds(at, 1)], conv_b[:, bass.ds(at, 1)],
                                      ALU.mult, ALU.add))
                step(v_.scalar_tensor_tensor(y[:], z[:, 1:T + 1], conv_w[:, 1, bass.ds(at, 1)], y[:], ALU.mult,
                                             ALU.add))
                step(v_.scalar_tensor_tensor(y[:], z[:, 0:T], conv_w[:, 0, bass.ds(at, 1)], y[:], ALU.mult, ALU.add))
                step(v_.tensor_tensor(y[:], y[:], raws[:, RAW[4] + half], ALU.mult))
                hi, lo = row(conv[0], at), row(conv[1], at)
                step(v_.tensor_copy(hi, y[:]))
                v_.tensor_tensor(lo, y[:], f32(hi), ALU.subtract).then_inc(conv_done, 1)

            def take_y_lo(j, head):
                dve.wait_ge(y_hi, 2 * j + head + 1)
                at = 2 * j + head
                v_.tensor_tensor(row(attn[1], at), turn[:, 0], f32(row(attn[0], at)),
                                 ALU.subtract).then_inc(y_split, 1)

            def round_of(j, first):
                if not first:
                    take_y_lo(j - 1, 0)
                    take_y_lo(j - 1, 1)
                for m, to in ((0, qT), (1, kT)):
                    for half in range(2):
                        rotate(j, m, half, to)
                for head in range(2):
                    for pair in range(2):
                        for tile in (2 * pair, 2 * pair + 1):
                            maximum(j, head, tile)
                        for tile in (2 * pair, 2 * pair + 1):
                            difference(j, head, tile)
                short_conv(j, 0)
                dve.wait_ge(o_ready, 2 * j + 2)
                step(v_.tensor_tensor(squares, o[:], o[:], ALU.mult))
                v_.tensor_reduce(o_stat[:, 0], squares, AX.X, ALU.add).then_inc(sums_ready, 1)
                short_conv(j, 1)
                dve.wait_ge(root_ready, j + 1)
                step(v_.reciprocal(o_stat[:, 2], o_stat[:, 1]))
                step(v_.scalar_tensor_tensor(o[:], o[:], 1.0 - LAM_INIT,
                                             o_stat[:, 2, :, None].broadcast_to([P, 2 * TT, P]), ALU.mult, ALU.mult))
                v_.tensor_tensor(o[:], o[:], subln[:, None, :].broadcast_to([P, 2 * TT, P]),
                                 ALU.mult).then_inc(y_ready, 1)

            before = chain.n
            round_of(0, True)
            per = chain.n - before
            with dve.Fori(1, MIX_ROUNDS) as j:
                chain.round(j - 1, per)
                round_of(j, False)
            chain.done(MIX_ROUNDS - 1)
            for head in range(2):
                take_y_lo(MIX_ROUNDS - 1, head)


def merge(nc, a, stream, merged, xT, conv, attn):
    with ExitStack() as ctx:
        gate, branch, total, gate_b = tiles(
            nc, ctx, ("gate", [P, 2, 2, T], F32), ("branch", [P, 2, 2, T], F32), ("total", [P, T], F32),
            ("gate_b", [P, 2 * DT], F32))
        proj, = banks(nc, ctx, ("proj_merge", 2))
        bias_loaded, merge_done, step_done = sems(nc, ctx, "bias_loaded merge_done merge_step")
        block = ctx.enter_context(nc.Block())

        @block.sync
        def _(sp):
            sp.dma_start(gate_b[:], a["gate_b_columns"]).then_inc(bias_loaded, 16)
            stream.load_stage(sp, MERGE_0, WO_0)

        @block.gpsimd
        def _(pool):
            take_los(pool, stream, MERGE_0, MERGE_ROUNDS, MERGE_CHUNKS, True)

        @block.tensor
        def _(pe):
            with pe.Fori(0, MERGE_ROUNDS) as j:
                for m, right in enumerate((xT, xT, conv, attn)):
                    for half in range(2):
                        stream.columns(pe, proj[:, half], MERGE_0 + MERGE_CHUNKS * j + m, m, half, *right)

        @block.scalar
        def _(act):
            act.wait_ge(bias_loaded, 16)
            with act.Fori(0, MERGE_ROUNDS) as j:
                for m in range(MERGE_CHUNKS):
                    n = MERGE_0 + MERGE_CHUNKS * j + m
                    stream.take_hi(act, n + 1, m + 1)
                    for half in range(2):
                        if m == 0 and half == 0:
                            act.wait_ge(merge_done, 2 * j + 1)
                        if m < 2:
                            stream.evacuate(act, n, half, gate[:, m, half], proj[:, half], ACT.Sigmoid,
                                            bias=gate_b[:, bass.ds(2 * j + DT * m + half, 1)])
                        else:
                            stream.evacuate(act, n, half, branch[:, m - 2, half], proj[:, half])

        @block.vector
        def _(dve):
            v_ = nc.vector
            chain = Chain(dve, step_done)
            dve.sem_inc(merge_done, 1)
            with dve.Fori(0, MERGE_ROUNDS) as j:
                chain.round(j, 2 * 4)
                for half in range(2):
                    stream.wait_out(dve, MERGE_0 + MERGE_CHUNKS * j + 3, half)
                    at = 2 * j + half
                    hi, lo = row(merged[0], at), row(merged[1], at)
                    chain.step(v_.tensor_tensor(branch[:, 0, half], branch[:, 0, half], gate[:, 0, half], ALU.mult))
                    chain.step(v_.tensor_tensor(branch[:, 1, half], branch[:, 1, half], gate[:, 1, half], ALU.mult))
                    chain.step(v_.tensor_tensor(total[:], branch[:, 0, half], branch[:, 1, half], ALU.add))
                    chain.step(v_.tensor_copy(hi, total[:]))
                    v_.tensor_tensor(lo, total[:], f32(hi), ALU.subtract).then_inc(merge_done, 1)
            chain.done(MERGE_ROUNDS)


class LayerNorm:

    def __init__(self, nc, ctx, name):
        self.nc = nc
        self.stats, self.mv, self.gain, self.shift, self.eps = tiles(
            nc, ctx, (f"{name}_stats", [P, TT, 2, 6], F32), (f"{name}_mv", [P, TT, 4], F32),
            (f"{name}_gain", [P, D], F32), (f"{name}_shift", [P, D], F32), (f"{name}_eps", [P, 1], F32))
        self.loaded, self.var_ready, self.root_ready, self.steps = sems(
            nc, ctx, f"{name}_loaded {name}_var_ready {name}_root_ready {name}_steps")

    def load(self, sp, gain, shift):
        sp.dma_start(self.gain[:], gain.broadcast_to([P, D])).then_inc(self.loaded, 16)
        sp.dma_start(self.shift[:], shift.broadcast_to([P, D])).then_inc(self.loaded, 16)

    def roots(self, act):
        act.wait_ge(self.var_ready, 1)
        self.nc.scalar.activation(self.mv[:, :, 2], self.mv[:, :, 1], ACT.Sqrt,
                                  bias=self.eps[:, 0:1]).then_inc(self.root_ready, 1)

    def statistics(self, dve, z):
        v_ = self.nc.vector
        self.chain = Chain(dve, self.steps)
        step = self.chain.step
        step(v_.memset(self.eps[:], LN_EPS))
        for t in range(TT):
            for g in range(2):
                step(v_.bn_stats(self.stats[:, t, g], z[:, t, 512 * g:512 * g + 512]))
        for t in range(TT):
            last = v_.bn_aggr(self.mv[:, t, 0:2], self.stats[:, t].rearrange("p a b -> p (a b)"))
            if t < TT - 1:
                step(last)
        last.then_inc(self.var_ready, 1)
        dve.wait_ge(self.root_ready, 1)
        step(v_.reciprocal(self.mv[:, :, 3], self.mv[:, :, 2]))
        dve.wait_ge(self.loaded, 32)

    def tile(self, z, t):
        v_, step = self.nc.vector, self.chain.step
        step(v_.tensor_scalar(z[:, t], z[:, t], self.mv[:, t, 0:1], self.mv[:, t, 3:4], ALU.subtract, ALU.mult))
        step(v_.tensor_tensor(z[:, t], z[:, t], self.gain[:], ALU.mult))
        return v_.tensor_tensor(z[:, t], z[:, t], self.shift[:], ALU.add)


def norm1(nc, a, stream, identity, merged, x1_scaled, xT):
    with ExitStack() as ctx:
        z, product = tiles(nc, ctx, ("z1", [P, TT, D], F32), ("product", [P, 2, 2, CW], F32))
        proj, turn = banks(nc, ctx, ("proj_o", 2), ("turn_x1", 2))
        x_loaded, added, normed, x1_turned, x1_hi, x1_split = sems(
            nc, ctx, "x_rows_loaded added normed x1_turned x1_hi x1_split")
        norm = LayerNorm(nc, ctx, "ln1")
        block = ctx.enter_context(nc.Block())
        chunks = WO_ROUNDS * WO_CHUNKS

        @block.sync
        def _(sp):
            sp.dma_start(x1_scaled[:], a["x"][0].rearrange("(t p) d -> p t d", p=P)).then_inc(x_loaded, 16)
            norm.load(sp, a["ln1_g"], a["ln1_b"])
            stream.load_stage(sp, WO_0, PQ_0)

        @block.gpsimd
        def _(pool):
            take_los(pool, stream, WO_0, WO_ROUNDS, WO_CHUNKS, True)

        @block.tensor
        def _(pe):
            for n in range(chunks):
                stream.rows(pe, [proj[:, half] for half in range(2)], WO_0 + n, n, *merged)
            for t in range(TT):
                pe.wait_ge(normed, t + 1)
                for g in range(2):
                    if t:
                        pe.wait_ge(x1_split, 2 * t + g - 1)
                    for c in range(4):
                        d = 4 * g + c
                        last = nc.tensor.transpose(turn[:, g, P * c:P * c + P], z[:, t, P * d:P * d + P], identity[:])
                    last.then_inc(x1_turned, 1)

        @block.scalar
        def _(act):
            for n in range(chunks):
                stream.take_hi(act, WO_0 + n + 1, n + 1)
                for half in range(2):
                    if n:
                        act.wait_ge(added, 2 * n + half - 1)
                    stream.evacuate(act, WO_0 + n, half, product[:, half],
                                    proj[:, half].rearrange("p (k n) -> p k n", k=2))
            norm.roots(act)
            for u in range(2 * TT):
                t, g = u // 2, u % 2
                act.wait_ge(x1_turned, u + 1)
                nc.scalar.activation(xT[0][:, 4 * g:4 * g + 4, P * t:P * t + P],
                                     turn[:, g].rearrange("p (c n) -> p c n", c=4), ACT.Copy).then_inc(x1_hi, 1)

        @block.vector
        def _(dve):
            v_ = nc.vector
            dve.wait_ge(x_loaded, 16)
            for n in range(chunks):
                for half in range(2):
                    stream.wait_out(dve, WO_0 + n, half)
                    at = (slice(None), slice(2 * half, 2 * half + 2), slice(CW * n, CW * n + CW))
                    v_.scalar_tensor_tensor(z[at], x1_scaled[at], ALPHA, product[:, half], ALU.mult,
                                            ALU.add).then_inc(added, 1)
            dve.wait_ge(added, 2 * chunks)
            norm.statistics(dve, z)
            for t in range(TT):
                norm.tile(z, t).then_inc(normed, 1)
            for t in range(TT):
                dve.wait_ge(normed, t + 1)
                v_.tensor_scalar(x1_scaled[:, t], z[:, t], ALPHA, None, ALU.mult)
                for g in range(2):
                    dve.wait_ge(x1_hi, 2 * t + g + 1)
                    at = (slice(None), slice(4 * g, 4 * g + 4), slice(P * t, P * t + P))
                    v_.tensor_tensor(xT[1][at], turn[:, g].rearrange("p (c n) -> p c n", c=4), f32(xT[0][at]),
                                     ALU.subtract).then_inc(x1_split, 1)


def keys(nc, a, stream, identity, xT, picks):
    with ExitStack() as ctx:
        (key_rows, q, s, s_rest, best, best_at, best_at_f, pair, pair_rest, top, top_at, first, second, weight,
         one_hot, small, count16, packed) = tiles(
            nc, ctx,
            ("sub_keys", [P, 2, 2, N_KEYS], F32), ("q", [P, 2, T], F32), ("s", [P, 2, TT, 2, N_KEYS], F32),
            ("s_rest", [P, TT * 2, N_KEYS], F32), ("best", [P, TT, 2, TOPK], F32),
            ("best_at", [P, TT, 2, TOPK], U32), ("best_at_f", [P, TT, 2, TOPK], F32),
            ("pair", [P, TT, TOPK * TOPK], F32), ("pair_rest", [P, TT, TOPK * TOPK], F32),
            ("top", [P, TT, TOPK], F32), ("top_at", [P, TT, TOPK], U32), ("first_at", [P, TT, TOPK], U32),
            ("second_at", [P, TT, TOPK], U32), ("weight", [P, TT, TOPK], F32),
            ("one_hot", [P, TT, TOPK, TOPK], F32), ("small", [P, 4, TT, TOPK], F32),
            ("count16", [P, TOPK], F32), ("packed", [P, 3, TT, P], F32))
        proj, score, turn = banks(nc, ctx, ("proj_q", 2), ("score_k", 2), ("turn_k", 3))
        k_loaded = sems(nc, ctx, "sub_keys_loaded0 sub_keys_loaded1")
        (c_loaded, q_scored, s_out, s_used, exp_asked, exp_done, all_packed, packed_turned, picks_out,
         steps) = sems(nc, ctx, "count16_loaded q_scored s_out s_used k_exp_asked k_exp_done all_packed "
                       "packed_turned picks_out k_steps")
        block = ctx.enter_context(nc.Block())

        @block.sync
        def _(sp):
            sp.dma_start(count16[:], a["count"][:, 0:TOPK]).then_inc(c_loaded, 16)
            for m in range(2):
                sp.dma_start(key_rows[:, m], a["sub_keys_columns"][m]).then_inc(k_loaded[m], 16)
            for i in range(PK_HEADS // 2):
                for m in range(2):
                    h = 2 * i + m
                    if h + 2 < PK_HEADS:
                        stream.load(sp, PQ_0 + h + 2, m)
                        sp.wait_ge(q_scored, 2 * h + 2)
                        sp.dma_start(key_rows[:, m], a["sub_keys_columns"][h + 2]).then_inc(k_loaded[m], 16)

        @block.gpsimd
        def _(pool):
            take_los(pool, stream, PQ_0, PQ_ROUNDS, PQ_CHUNKS, False)

        @block.tensor
        def _(pe):
            with pe.Fori(0, PQ_ROUNDS) as j:
                for m in range(2):
                    h = 2 * j + m
                    for half in range(2):
                        stream.columns(pe, proj[:, half], PQ_0 + h, m, half, *xT)
                    pe.wait_ge(k_loaded[m], 16 * j + 16)
                    for half in range(2):
                        stream.wait_out(pe, PQ_0 + h, half)
                        pe.wait_ge(s_out, 2 * h + half + 1)
                        for t in range(TT):
                            last = nc.tensor.matmul(score[:, half, P * t:P * t + P], q[:, half, P * t:P * t + P],
                                                    key_rows[:, m, half], start=True, stop=True)
                        last.then_inc(q_scored, 1)
            pe.wait_ge(all_packed, 1)
            for n in range(3):
                for t in range(TT):
                    last = nc.tensor.transpose(turn[:, n, P * t:P * t + P], packed[:, n, t], identity[:])
            last.then_inc(packed_turned, 1)

        @block.scalar
        def _(act):
            act.sem_inc(s_used, 2)
            act.sem_inc(s_out, 1)

            def head(j, m, ahead):
                h = 2 * j + m
                if ahead:
                    stream.take_hi(act, PQ_0 + h + 1, m + 1)
                act.wait_ge(q_scored, 2 * h)
                for half in range(2):
                    stream.evacuate(act, PQ_0 + h, half, q[:, half], proj[:, half])
                act.wait_ge(s_used, h + 1)
                for half in range(2):
                    act.wait_ge(q_scored, 2 * h + half + 1)
                    nc.scalar.activation(s[:, m, :, half], score[:, half].rearrange("p (t n) -> p t n", t=TT),
                                         ACT.Copy).then_inc(s_out, 1)

            def exponentials(h):
                act.wait_ge(exp_asked, h + 1)
                nc.scalar.activation(weight[:], small[:, 3], ACT.Exp).then_inc(exp_done, 1)

            head(0, 0, True)
            head(0, 1, True)
            exponentials(0)
            with act.Fori(1, PQ_ROUNDS - 1) as j:
                for m in range(2):
                    head(j, m, True)
                    exponentials(2 * j + m - 1)
            head(PQ_ROUNDS - 1, 0, True)
            exponentials(PK_HEADS - 3)
            head(PQ_ROUNDS - 1, 1, False)
            exponentials(PK_HEADS - 2)
            exponentials(PK_HEADS - 1)
            act.wait_ge(packed_turned, 1)
            for n in range(3):
                nc.scalar.activation(picks[:, n], turn[:, n], ACT.Copy).then_inc(picks_out, 1)
            act.wait_ge(picks_out, 3)

        @block.vector
        def _(dve):
            v_ = nc.vector
            chain = Chain(dve, steps)
            step = chain.step
            dve.wait_ge(c_loaded, 16)

            def top16(values, rest, out, out_at):
                step(v_.max(out[:, 0:8], values))
                step(v_.match_replace(rest, out[:, 0:8], values, NEG))
                step(v_.max(out[:, 8:16], rest))
                step(v_.max_index(out_at[:, 0:8], out[:, 0:8], values))
                step(v_.max_index(out_at[:, 8:16], out[:, 8:16], rest))

            def head(j, m):
                h = 2 * j + m
                dve.wait_ge(s_out, 2 * h + 3)
                for t in range(TT):
                    for half in range(2):
                        top16(s[:, m, t, half], s_rest[:, 2 * t + half], best[:, t, half], best_at[:, t, half])
                dve.sem_inc(s_used, 1)
                step(v_.tensor_copy(best_at_f[:], best_at[:]))
                for t in range(TT):
                    step(v_.tensor_tensor(pair[:, t].rearrange("p (a b) -> p a b", a=TOPK),
                                          best[:, t, 0, :, None].broadcast_to([P, TOPK, TOPK]),
                                          best[:, t, 1, None, :].broadcast_to([P, TOPK, TOPK]), ALU.add))
                for t in range(TT):
                    top16(pair[:, t], pair_rest[:, t], top[:, t], top_at[:, t])
                step(v_.tensor_tensor(small[:, 3], top[:], top[:, :, 0:1].broadcast_to([P, TT, TOPK]), ALU.subtract))
                dve.sem_inc(exp_asked, 1)
                step(v_.tensor_scalar(first[:], top_at[:], 4, None, ALU.logical_shift_right))
                step(v_.tensor_scalar(second[:], top_at[:], 15, None, ALU.bitwise_and))
                for n, at in enumerate((first, second)):
                    step(v_.tensor_copy(small[:, 2], at[:]))
                    step(v_.tensor_tensor(one_hot[:].rearrange("p t a b -> p (t a) b"),
                                          small[:, 2].rearrange("p t a -> p (t a)")[:, :, None]
                                          .broadcast_to([P, TT * TOPK, TOPK]),
                                          count16[:, None, :].broadcast_to([P, TT * TOPK, TOPK]), ALU.is_equal))
                    step(v_.tensor_tensor(one_hot[:], one_hot[:], best_at_f[:, :, n, None, :]
                                          .broadcast_to([P, TT, TOPK, TOPK]), ALU.mult))
                    step(v_.tensor_reduce(packed[:, n, :, TOPK * h:TOPK * h + TOPK], one_hot[:], AX.X, ALU.add))
                dve.wait_ge(exp_done, h + 1)
                step(v_.tensor_reduce(small[:, 0, 0, 0:TT], weight[:], AX.X, ALU.add))
                step(v_.reciprocal(small[:, 1, 0, 0:TT], small[:, 0, 0, 0:TT]))
                step(v_.tensor_tensor(packed[:, 2, :, TOPK * h:TOPK * h + TOPK], weight[:],
                                      small[:, 1, 0, 0:TT, None].broadcast_to([P, TT, TOPK]), ALU.mult))

            for h in range(PK_HEADS):
                head(h // 2, h % 2)
            dve.sem_inc(all_packed, 1)


def experts(nc, a, identity, xT, picks, gelus, gates):
    ROUNDS = N_KEYS // (2 * 8)
    with ExitStack() as ctx:
        u_raw, u_hi, u_lo, gelu, left, right, gate, count = tiles(
            nc, ctx, ("u_raw", [P, 2, DT, P], F32), ("u_hi", [P, 2, DT, P], F32R), ("u_lo", [P, 2, DT, P], F32R),
            ("gelu", [P, 2, T], F32), ("left", [P, 2, PER_TILE, P], F32), ("right", [P, 2, PER_TILE, P], F32),
            ("gate_chunk", [P, 2, N_KEYS, TOK], F32), ("count", [P, N_KEYS], F32))
        dots, built = banks(nc, ctx, ("dots", 2), ("built", 2))
        u_loaded = sems(nc, ctx, "u_loaded0 u_loaded1")
        stored = sems(nc, ctx, "gelu_stored0 gelu_stored1")
        flushed = sems(nc, ctx, "gate_stored0 gate_stored1")
        count_loaded, hi_taken, lo_taken, dot_done, gelu_done, hot_ready, built_done, built_out, hot_step = sems(
            nc, ctx, "count_loaded u_hi_taken u_lo_taken dot_done gelu_done hot_ready built_done built_out hot_step")
        block = ctx.enter_context(nc.Block())

        def tiles_of(engine, body, after=None):
            with engine.Fori(0, ROUNDS) as c:
                for f in range(2):
                    with engine.Fori(0, 4) as k:
                        for r in range(2):
                            body(16 * c + 2 * k + 8 * f + r, c, f, k, r, 8 * c + k + 4 * f)
                    if after:
                        after(c, f)

        @block.sync
        def _(sp):
            sp.dma_start(count[:], a["count"]).then_inc(count_loaded, 16)

            def load(i, c, f, k, r, pair):
                sp.wait_ge(lo_taken, i + 1)
                sp.dma_start(u_raw[:, r], a["u_columns"][i]).then_inc(u_loaded[r], 16)
            tiles_of(sp, load)

        @block.gpsimd
        def _(pool):
            pool.sem_inc(lo_taken, 2)

            def tile(i, c, f, k, r, pair):
                pool.wait_ge(hi_taken, i + 1)
                nc.gpsimd.tensor_tensor(u_lo[:, r], u_raw[:, r], f32(u_hi[:, r]), ALU.subtract).then_inc(lo_taken, 1)
            tiles_of(pool, tile)

        @block.tensor
        def _(pe):
            pe.sem_inc(dot_done, 2)
            pe.sem_inc(built_done, 2)

            def tile(i, c, f, k, r, pair):
                pe.wait_ge(hot_ready, i + 1)
                pe.wait_ge(built_out, i + 1)
                for t in range(PER_TILE):
                    last = nc.tensor.matmul(built[:, r, P * t:P * t + P], left[:, r, t], right[:, r, t],
                                            start=True, stop=True)
                last.then_inc(built_done, 1)
                pe.wait_ge(lo_taken, i + 3)
                pe.wait_ge(gelu_done, i + 1)
                for d in range(DT):
                    nc.tensor.matmul(dots[:, r], u_hi[:, r, d], xT[0][:, d], start=(d == 0), stop=False)
                    nc.tensor.matmul(dots[:, r], u_hi[:, r, d], xT[1][:, d], start=False, stop=False)
                    last = nc.tensor.matmul(dots[:, r], u_lo[:, r, d], xT[0][:, d], start=False,
                                            stop=(d == DT - 1))
                last.then_inc(dot_done, 1)
            tiles_of(pe, tile)

        @block.scalar
        def _(act):
            act.sem_inc(gelu_done, 2)
            act.sem_inc(built_out, 2)
            for n in range(2):
                act.sem_inc(stored[n], 16)
                act.sem_inc(flushed[n], 16)

            def tile(i, c, f, k, r, pair):
                act.wait_ge(built_done, i + 3)
                if r == 0:
                    act.wait_ge(flushed[f], 16 * c + 16)
                nc.scalar.activation(gate[:, f, :, bass.ds(8 * k + 4 * r, PER_TILE)],
                                     built[:, r].rearrange("p (t n) -> p n t", t=PER_TILE),
                                     ACT.Copy).then_inc(built_out, 1)
                act.wait_ge(dot_done, i + 3)
                act.wait_ge(stored[r], 16 * pair + 16)
                nc.scalar.activation(gelu[:, r], dots[:, r], ACT.Gelu).then_inc(gelu_done, 1)
                act.wait_ge(gelu_done, i + 3)
                act.dma_start(gelus[i], gelu[:, r]).then_inc(stored[r], 16)

            def flush(c, f):
                act.wait_ge(built_out, 16 * c + 8 * f + 10)
                act.dma_start(gates[2 * c + f], gate[:, f].rearrange("p n t -> p (n t)")).then_inc(flushed[f], 16)
            tiles_of(act, tile, flush)
            for n in range(2):
                act.wait_ge(stored[n], 16 * (N_KEYS // 2) + 16)
                act.wait_ge(flushed[n], 16 * ROUNDS + 16)

        @block.vector
        def _(dve):
            dve.wait_ge(count_loaded, 16)

            def tile(i, c, f, k, r, pair):
                dve.wait_ge(u_loaded[r], 16 * pair + 16)
                dve.wait_ge(dot_done, i + 1)
                nc.vector.tensor_copy(u_hi[:, r], u_raw[:, r]).then_inc(hi_taken, 1)
                dve.wait_ge(built_done, i + 1)
                for t in range(PER_TILE):
                    at = bass.ds(PER_TILE * i + t, 1)
                    nc.vector.tensor_scalar(left[:, r, t], count[:], picks[:, 1, at], None, ALU.is_equal)
                    last = nc.vector.tensor_scalar(right[:, r, t], count[:], picks[:, 0, at], picks[:, 2, at],
                                                   ALU.is_equal, ALU.mult)
                last.then_inc(hot_ready, 1)
            tiles_of(dve, tile)


def output(nc, a, x1_scaled, gelus, gates, out):
    GROUPS = N_KEYS // GROUP
    BANKS = 4
    with ExitStack() as ctx:
        v_raw, v_hi, v_lo, gelu, gate, w, w_hi, w_lo = tiles(
            nc, ctx, ("v_raw", [P, 2, D], F32), ("v_hi", [P, 2, GROUP, D], F32R), ("v_lo", [P, 2, GROUP, D], F32R),
            ("gelu_in", [P, 2, GROUP, T], F32), ("gate_in", [P, 2, T // TOK, GROUP * TOK], F32),
            ("weights", [P, 2, T], F32), ("weights_hi", [P, 2, GROUP, T], F32R), ("weights_lo", [P, 2, GROUP, T], F32R))
        sums, = banks(nc, ctx, ("sums", BANKS))
        v_loaded = sems(nc, ctx, "v_loaded0 v_loaded1")
        in_loaded = sems(nc, ctx, "gelu_gate_loaded0 gelu_gate_loaded1")
        v_hi_taken, v_lo_taken, w_ready, bank_done, bank_added, steps, tile_normed, out_stored = sems(
            nc, ctx, "v_hi_taken v_lo_taken w_ready bank_done bank_added w_steps tile_normed out_stored")
        norm = LayerNorm(nc, ctx, "ln2")
        block = ctx.enter_context(nc.Block())

        @block.sync
        def _(sp):
            with sp.Fori(0, GROUPS // 2) as jj:
                for s in range(2):
                    j = 2 * jj + s
                    sp.wait_ge(w_ready, GROUP * (j + 1))
                    sp.dma_start(gelu[:, s], gelus[bass.ds(GROUP * j, GROUP)].rearrange("q p t -> p q t")) \
                        .then_inc(in_loaded[s], 16)
                    sp.dma_start(gate[:, s], gates.rearrange("c p n -> p c n")[:, :, bass.ds(GROUP * TOK * j,
                                                                                             GROUP * TOK)]) \
                        .then_inc(in_loaded[s], 16)
                    for q in range(GROUP):
                        sp.wait_ge(v_lo_taken, GROUP * j + q + 1)
                        sp.dma_start(v_raw[:, q % 2], a["v_tab"][0].rearrange("(n p) d -> n p d", p=P)
                                     [GROUP * j + q]).then_inc(v_loaded[q % 2], 16)
            norm.load(sp, a["ln2_g"], a["ln2_b"])

        @block.gpsimd
        def _(pool):
            pool.sem_inc(v_lo_taken, 2)
            with pool.Fori(0, GROUPS // 2) as jj:
                for s in range(2):
                    for q in range(GROUP):
                        i = GROUP * (2 * jj + s) + q
                        pool.wait_ge(v_hi_taken, i + 1)
                        nc.gpsimd.tensor_tensor(v_lo[:, s, q], v_raw[:, q % 2], f32(v_hi[:, s, q]),
                                                ALU.subtract).then_inc(v_lo_taken, 1)

        @block.tensor
        def _(pe):
            pe.sem_inc(bank_done, 2 * 8)
            with pe.Fori(0, GROUPS // 2) as jj:
                for s in range(2):
                    j = 2 * jj + s
                    for b in range(8):
                        t, g = b // 2, b % 2
                        pe.wait_ge(bank_added, 8 * j + b + 1)
                        for q in range(GROUP):
                            if b == 0:
                                pe.wait_ge(v_lo_taken, GROUP * j + q + 3)
                                pe.wait_ge(w_ready, GROUP * j + q + 1 + 2 * GROUP)
                            tokens, columns = slice(P * t, P * t + P), slice(512 * g, 512 * g + 512)
                            to = sums[:, b % BANKS]
                            nc.tensor.matmul(to, w_hi[:, s, q, tokens], v_hi[:, s, q, columns], start=(q == 0),
                                             stop=False)
                            nc.tensor.matmul(to, w_hi[:, s, q, tokens], v_lo[:, s, q, columns], start=False, stop=False)
                            last = nc.tensor.matmul(to, w_lo[:, s, q, tokens], v_hi[:, s, q, columns], start=False,
                                                    stop=(q == GROUP - 1))
                        last.then_inc(bank_done, 1)

        @block.scalar
        def _(act):
            with act.Fori(0, GROUPS // 2) as jj:
                for s in range(2):
                    for q in range(GROUP):
                        i = GROUP * (2 * jj + s) + q
                        act.wait_ge(v_loaded[q % 2], 16 * (2 * (2 * jj + s) + q // 2) + 16)
                        if q == 0:
                            act.wait_ge(bank_done, 8 * (2 * jj + s) + 8)
                        nc.scalar.activation(v_hi[:, s, q], v_raw[:, q % 2], ACT.Copy).then_inc(v_hi_taken, 1)
            norm.roots(act)
            for t in range(TT):
                act.wait_ge(tile_normed, t + 1)
                act.dma_start(out[0].rearrange("(t p) d -> t p d", p=P)[t], x1_scaled[:, t]).then_inc(out_stored, 16)
            act.wait_ge(out_stored, 16 * TT)

        @block.vector
        def _(dve):
            v_ = nc.vector
            chain = Chain(dve, steps)
            dve.sem_inc(w_ready, 2 * GROUP)
            dve.sem_inc(bank_added, BANKS)

            def weigh(j, s, q):
                if q == 0:
                    dve.wait_ge(in_loaded[s], 16 * (j - s) + 32)
                    dve.wait_ge(bank_done, 8 * j + 8)
                chain.step(v_.tensor_tensor(w[:, q % 2].rearrange("p (c t) -> p c t", t=TOK),
                                            gelu[:, s, q].rearrange("p (c t) -> p c t", t=TOK),
                                            gate[:, s, :, TOK * q:TOK * q + TOK], ALU.mult))
                chain.step(v_.tensor_copy(w_hi[:, s, q], w[:, q % 2]))
                v_.tensor_tensor(w_lo[:, s, q], w[:, q % 2], f32(w_hi[:, s, q]), ALU.subtract).then_inc(w_ready, 1)

            def add(j, b):
                t, g = b // 2, b % 2
                to = x1_scaled[:, t, 512 * g:512 * g + 512]
                dve.wait_ge(bank_done, 8 * j + b + 17)
                v_.tensor_tensor(to, to, sums[:, b % BANKS], ALU.add).then_inc(bank_added, 1)

            def group(j, s, then):
                for b in range(8):
                    add(j, b)
                    if then and b % 2 == 1:
                        weigh(j + 1, 1 - s, b // 2)

            for q in range(GROUP):
                weigh(0, 0, q)
            with dve.Fori(0, GROUPS // 2 - 1) as jj:
                chain.round(jj, 2 * GROUP * 2)
                group(2 * jj, 0, True)
                group(2 * jj + 1, 1, True)
            chain.done(GROUPS // 2 - 1)
            group(GROUPS - 2, 0, True)
            group(GROUPS - 1, 1, False)
            dve.wait_ge(bank_added, BANKS + 8 * GROUPS)
            norm.statistics(dve, x1_scaled)
            for t in range(TT):
                norm.tile(x1_scaled, t).then_inc(tile_normed, 1)


def block_program(nc, a, gelus, gates, out):
    with ExitStack() as whole:
        identity, = tiles(nc, whole, ("identity", [P, P], F32))
        xT = tiles(nc, whole, ("xT_hi", [P, DT, T], F32R), ("xT_lo", [P, DT, T], F32R))
        with ExitStack() as front:
            stream = Stream(nc, front, a["w_chunks"])
            with ExitStack() as merging:
                with ExitStack() as mixing:
                    conv = tiles(nc, mixing, ("conv_hi", [P, DT, T], F32R), ("conv_lo", [P, DT, T], F32R))
                    attn = tiles(nc, mixing, ("attn_hi", [P, DT, T], F32R), ("attn_lo", [P, DT, T], F32R))
                    mixers(nc, a, stream, identity, xT, conv, attn)
                    merged = tiles(nc, merging, ("merged_hi", [P, DT, T], F32R), ("merged_lo", [P, DT, T], F32R),
                                   side="right")
                    merge(nc, a, stream, merged, xT, conv, attn)
                x1_scaled, picks = tiles(nc, whole, ("x1_scaled", [P, TT, D], F32), ("picks", [P, 3, T], F32))
                norm1(nc, a, stream, identity, merged, x1_scaled, xT)
            keys(nc, a, stream, identity, xT, picks)
        experts(nc, a, identity, xT, picks, gelus, gates)
        output(nc, a, x1_scaled, gelus, gates, out)


def laid_out(i):
    def chunk(w, first, j):
        at = first + CW * j
        return w[0][:, at:at + CW].reshape(DT, P, CW).transpose(1, 0, 2)

    def columns(v):
        v = v.reshape(*v.shape[:-1], -1, P)
        return np.ascontiguousarray(np.moveaxis(v, -1, 0))

    h, b, c, q, k, v, conv_gate, attn_gate = (D * n for n in range(8))
    w = [chunk(i["w_in"], at, j) for j in range(MIX_ROUNDS) for at in (q, k, v, h, b, c)]
    for j in range(MERGE_ROUNDS):
        w += [chunk(i["w_in"], conv_gate, j), chunk(i["w_in"], attn_gate, j), chunk(i["w_conv_out"], 0, j),
              chunk(i["w_attn_out"], 0, j)]
    w += [chunk(i["w_o"], 0, j) for j in range(D // CW)]
    w += [chunk(i["w_pq"], 0, j) for j in range(PK_HEADS)]

    inverse = ROPE_THETA ** (-np.arange(0, ROT_DIM, 2, dtype=np.float32) / ROT_DIM)
    freq, swap = np.zeros((P, 1), np.float32), np.zeros((P, P), np.float32)
    for n in range(ROT_DIM // 2):
        for component in range(2):
            r1, r2 = HD * component + n, HD * component + ROT_DIM // 2 + n
            freq[r1] = freq[r2] = inverse[n]
            swap[r2, r1], swap[r1, r2] = -1.0, 1.0
    below = np.arange(P)[None, :] <= np.arange(P)[:, None]
    kept = ("x", "positions", "lambda_q1", "lambda_k1", "lambda_q2", "lambda_k2", "subln_g", "ln1_g", "ln1_b",
            "ln2_g", "ln2_b", "v_tab")
    return {n: i[n] for n in kept} | {
        "x_columns": np.ascontiguousarray(i["x"][0].T.reshape(DT, P, T).transpose(1, 0, 2)),
        "w_chunks": np.stack(w),
        "conv_w_columns": columns(i["conv_w"][0]),
        "conv_b_columns": columns(i["conv_b"][0]),
        "gate_b_columns": columns(i["gate_b"][0]),
        "sub_keys_columns": np.ascontiguousarray(i["sub_keys"][0].transpose(0, 3, 1, 2)),
        "u_columns": np.ascontiguousarray(i["u_tab"][0].reshape(N_KEYS, P, DT, P).transpose(0, 3, 2, 1)),
        "identity": np.eye(P, dtype=np.float32),
        "freq": freq,
        "swap": swap,
        "mask": np.where(below, 0.0, NEG).astype(np.float32),
        "count": np.ascontiguousarray(np.broadcast_to(np.arange(P, dtype=np.float32), (P, P))),
    }


def kernel(**inputs):
    import concourse.bacc as bacc
    from concourse.bass_utils import run_bass_kernel_spmd

    nc = bacc.Bacc("TRN2", target_bir_lowering=False, num_devices=1)
    arrays = laid_out({n: np.asarray(v) for n, v in inputs.items()})
    a = {n: nc.dram_tensor(f"in_{n}", v.shape, mybir.dt.from_np(v.dtype), kind="ExternalInput").ap()
         for n, v in arrays.items()}
    gelus = nc.dram_tensor("gelus", [N_KEYS, P, T], F32, kind="Internal").ap()
    gates = nc.dram_tensor("gates", [T // TOK, P, N_KEYS * TOK], F32, kind="Internal").ap()
    out = nc.dram_tensor("out", (1, T, D), F32, kind="ExternalOutput").ap()
    block_program(nc, a, gelus, gates, out)
    r = run_bass_kernel_spmd(nc, [{f"in_{n}": v for n, v in arrays.items()}], core_ids=[0])
    return r.results[0]["out"]
```

```python
import math
from contextlib import ExitStack

import concourse.bass as bass
import numpy as np
from concourse import mybir

F32 = mybir.dt.float32
F32R = mybir.dt.float32r
I32 = mybir.dt.int32
U32 = mybir.dt.uint32
ACT = mybir.ActivationFunctionType
ALU = mybir.AluOpType
AX = mybir.AxisListType

P = 128
D = 1024
T = 512
DT = D // P
TT = T // P
HEADS = 8
HD = 64
CW = 256
SLOTS = 2
PK_HEADS = 8
TOPK = 16
N_KEYS = 128
ALPHA = 2 ** 0.25
LAM_INIT = 0.8 - 0.6 * math.exp(0.0)
LN_EPS = 1e-5
SCALE = HD ** -0.5
ROT_DIM = HD // 4
ROPE_THETA = 500000.0
NEG = -3.0e38
GROUP = 4
TOK = 32
PER_TILE = 8
TILES_BESIDE = 46
TILES_AFTER = 4

MIX_ROUNDS, MIX_CHUNKS = 4, 6
MERGE_ROUNDS, MERGE_CHUNKS = 4, 4
WO_ROUNDS, WO_CHUNKS = 2, 2
PQ_ROUNDS, PQ_CHUNKS = 4, 2
MIX_0 = 0
MERGE_0 = MIX_0 + MIX_ROUNDS * MIX_CHUNKS
WO_0 = MERGE_0 + MERGE_ROUNDS * MERGE_CHUNKS
PQ_0 = WO_0 + WO_ROUNDS * WO_CHUNKS
CHUNKS = PQ_0 + PQ_ROUNDS * PQ_CHUNKS


def f32(ap):
    return ap.bitcast(F32)


def row(ap, at):
    return ap[:, bass.ds(at, 1)].rearrange("p a n -> p (a n)")


class Chain:

    def __init__(self, engine, sem):
        self.engine, self.sem, self.n, self.base = engine, sem, 0, 0

    def step(self, instruction):
        self.n += 1
        instruction.then_inc(self.sem, 1)
        self.engine.wait_ge(self.sem, self.base + self.n)

    def round(self, i, per):
        self.start, self.per = self.base + self.n, per
        self.base, self.n = self.start + i * per, 0

    def done(self, rounds):
        assert self.n == self.per, (self.n, self.per)
        self.base, self.n = self.start + rounds * self.per, 0


class Stream:

    def __init__(self, nc, ctx, source):
        self.nc, self.source = nc, source
        self.raw, self.hi, self.lo = tiles(
            nc, ctx, ("w_raw", [P, SLOTS, DT, CW], F32), ("w_hi", [P, SLOTS, DT, CW], F32R),
            ("w_lo", [P, SLOTS, DT, CW], F32R), side="right")
        self.raw_loaded = [ctx.enter_context(nc.semaphore(f"w_raw_loaded{s}")) for s in range(SLOTS)]
        self.hi_ready = ctx.enter_context(nc.semaphore("w_hi_ready"))
        self.lo_ready = ctx.enter_context(nc.semaphore("w_lo_ready"))
        self.unit_done = ctx.enter_context(nc.semaphore("unit_done"))
        self.bank_free = ctx.enter_context(nc.semaphore("proj_bank_free"))

    def load(self, sp, n, m):
        sp.wait_ge(self.lo_ready, n + 1)
        sp.dma_start(self.raw[:, m], self.source[n]).then_inc(self.raw_loaded[m], 16)

    def load_stage(self, sp, first, last):
        with sp.Fori(0, (min(last, CHUNKS - 2) - first) // 2) as i:
            for m in range(2):
                self.load(sp, 2 * i + first + 2 + m, m)

    def take_hi(self, act, n, m):
        act.wait_ge(self.raw_loaded[m % 2], (n - m % 2) * 8 + 16)
        if not isinstance(n, int) or n >= 2:
            act.wait_ge(self.unit_done, 2 * n - 2)
        self.nc.scalar.activation(self.hi[:, m % 2], self.raw[:, m % 2], ACT.Copy).then_inc(self.hi_ready, 1)

    def take_lo(self, pool, n, m):
        pool.wait_ge(self.hi_ready, n + 1)
        self.nc.gpsimd.tensor_tensor(self.lo[:, m % 2], self.raw[:, m % 2], f32(self.hi[:, m % 2]),
                                     ALU.subtract).then_inc(self.lo_ready, 1)

    def columns(self, pe, out, n, m, half, right_hi, right_lo):
        pe.wait_ge(self.hi_ready, n + 1)
        pe.wait_ge(self.bank_free, 2 * n + half + 1)
        columns = slice(P * half, P * half + P)
        for c in range(DT):
            hi = self.hi[:, m % 2, c, columns]
            self.nc.tensor.matmul(out, hi, right_hi[:, c, :], start=(c == 0), stop=False)
            self.nc.tensor.matmul(out, hi, right_lo[:, c, :], start=False, stop=False)
        pe.wait_ge(self.lo_ready, n + 1 + SLOTS)
        for c in range(DT):
            last = self.nc.tensor.matmul(out, self.lo[:, m % 2, c, columns], right_hi[:, c, :], start=False,
                                         stop=(c == DT - 1))
        last.then_inc(self.unit_done, 1)

    def rows(self, pe, outs, n, m, left_hi, left_lo):
        pe.wait_ge(self.lo_ready, n + 1 + SLOTS)
        for half in range(2):
            pe.wait_ge(self.bank_free, 2 * n + half + 1)
            for k in range(2):
                tokens = slice(P * (2 * half + k), P * (2 * half + k) + P)
                to = outs[half][:, CW * k:CW * k + CW]
                for c in range(DT):
                    hi, lo = self.hi[:, m % 2, c], self.lo[:, m % 2, c]
                    self.nc.tensor.matmul(to, left_hi[:, c, tokens], hi, start=(c == 0), stop=False)
                    self.nc.tensor.matmul(to, left_hi[:, c, tokens], lo, start=False, stop=False)
                    last = self.nc.tensor.matmul(to, left_lo[:, c, tokens], hi, start=False, stop=(c == DT - 1))
            last.then_inc(self.unit_done, 1)

    def evacuate(self, act, n, half, to, bank, func=ACT.Copy, **kw):
        act.wait_ge(self.unit_done, 2 * n + half + 1)
        self.nc.scalar.activation(to, bank, func, **kw).then_inc(self.bank_free, 1)

    def wait_out(self, engine, n, half):
        engine.wait_ge(self.bank_free, SLOTS + 2 * n + half + 1)


def take_los(pool, stream, first, rounds, per, ahead):
    with pool.Fori(0, rounds if ahead else rounds - 1) as j:
        for m in range(per):
            stream.take_lo(pool, first + per * j + m + 1, m + 1)
    if not ahead:
        for m in range(per - 1):
            stream.take_lo(pool, first + per * (rounds - 1) + m + 1, m + 1)


def tiles(nc, ctx, *named, side="left"):
    return [ctx.enter_context(nc.sbuf_tensor(name, shape, dtype, side=side)) for name, shape, dtype in named]


def banks(nc, ctx, *named):
    return [ctx.enter_context(nc.psum_tensor(name, [P, n, 512], F32)) for name, n in named]


def sems(nc, ctx, names):
    return [ctx.enter_context(nc.semaphore(n)) for n in names.split()]


def mixers(nc, a, stream, identity, xT, conv, attn):
    MAGIC = 1.5 * 2.0 ** 23
    TURN = 2 * math.pi
    TURN_1, TURN_2 = 6.28125, float(np.float32(TURN - 6.28125))
    TURN_3 = TURN - TURN_1 - TURN_2
    HALF_TURN = float(np.nextafter(np.float32(math.pi), np.float32(0)))
    CONSTS = 12
    with ExitStack() as ctx:
        (raws, cosT, sinT, part, qT, kT, v, probs, diff, diffT, z, y, o, mask, swap, freq,
         conv_w, conv_b, subln, lam_in, lam, stat, o_stat) = tiles(
            nc, ctx, ("raws", [P, 8, T], F32),
            ("cosT", [P, T], F32), ("sinT", [P, T], F32), ("part", [P, T], F32),
            ("qT", [P, 2, T], F32), ("kT", [P, 2, T], F32), ("v", [P, TT, CW], F32),
            ("probs", [P, 2, 2, T], F32), ("diff", [P, 2, T], F32), ("diffT", [P, 10, P], F32),
            ("z", [P, T + 2], F32), ("y", [P, T], F32),
            ("o", [P, 2 * TT, P], F32), ("mask", [P, P], F32),
            ("swap", [P, P], F32), ("freq", [P, 1], F32), ("conv_w", [P, 3, DT], F32),
            ("conv_b", [P, DT], F32), ("subln", [P, P], F32), ("lam_in", [P, 4, HD], F32),
            ("lam", [P, 8], F32), ("stat", [P, 2, 10], F32), ("o_stat", [P, 3, 2 * TT], F32))
        position = kT[:, 1].bitcast(I32)
        proj, scores, turn, pv = banks(nc, ctx, ("proj", 2), ("scores", 4), ("turn", 1), ("pv", 1))
        (x_loaded, const_loaded, x_hi, x_split, tables_ready, sin_ready, lam_exp, swap_done, qk_ready,
         score_done, bias_ready, exp_done, diff_ready, turned, diffT_ready, pv_done, o_ready, sums_ready,
         root_ready, y_ready, y_turned, y_hi, y_split, conv_done, dve_step) = sems(
            nc, ctx, "x_loaded const_loaded x_hi x_split tables_ready sin_ready lam_exp swap_done "
            "qk_ready score_done bias_ready exp_done diff_ready turned diffT_ready pv_done o_ready "
            "sums_ready root_ready y_ready y_turned y_hi y_split conv_done dve_step")
        squares = raws[:, 6:8, :].rearrange("p a (t n) -> p (a t) n", n=P)
        RAW = {0: 0, 1: 2, 3: 4, 4: 0, 5: 2}
        block = ctx.enter_context(nc.Block())

        @block.sync
        def _(sp):
            sp.dma_start(raws[:], a["x_columns"]).then_inc(x_loaded, 16)
            for m in range(2):
                sp.dma_start(stream.raw[:, m], stream.source[m]).then_inc(stream.raw_loaded[m], 16)
            sp.dma_start(identity[:], a["identity"]).then_inc(const_loaded, 16)
            sp.dma_start(position, a["positions"].broadcast_to([P, T])).then_inc(const_loaded, 16)
            sp.dma_start(freq[:], a["freq"]).then_inc(const_loaded, 16)
            sp.dma_start(mask[:], a["mask"]).then_inc(const_loaded, 16)
            sp.dma_start(swap[:], a["swap"]).then_inc(const_loaded, 16)
            sp.dma_start(subln[:], a["subln_g"].broadcast_to([P, P])).then_inc(const_loaded, 16)
            for n, name in enumerate(("lambda_q1", "lambda_k1", "lambda_q2", "lambda_k2")):
                sp.dma_start(lam_in[:, n], a[name].broadcast_to([P, HD])).then_inc(const_loaded, 16)
            sp.dma_start(conv_b[:], a["conv_b_columns"]).then_inc(const_loaded, 16)
            sp.dma_start(conv_w[:], a["conv_w_columns"]).then_inc(const_loaded, 16)
            stream.load_stage(sp, MIX_0, MERGE_0)

        @block.gpsimd
        def _(pool):
            pool.sem_inc(stream.lo_ready, SLOTS)
            stream.take_lo(pool, 0, 0)
            take_los(pool, stream, MIX_0, MIX_ROUNDS, MIX_CHUNKS, True)

        @block.tensor
        def _(pe):
            pe.sem_inc(turned, 2)
            pe.wait_ge(const_loaded, 16 * CONSTS)
            pe.wait_ge(x_split, DT)

            def project(j, m, half):
                stream.columns(pe, proj[:, half], MIX_0 + MIX_CHUNKS * j + m, m, half, *xT)

            def rotate_halves(j, m):
                for half in range(2):
                    stream.wait_out(pe, MIX_0 + MIX_CHUNKS * j + m, half)
                    if m == 0 and half == 0:
                        pe.wait_ge(y_split, 2 * j)
                    pe.wait_ge(qk_ready, 4 * j + 2 * m + half)
                    nc.tensor.matmul(turn[:, 0], swap[:], raws[:, RAW[m] + half], start=True,
                                     stop=True).then_inc(swap_done, 1)

            def score(j, head, tile):
                u = 8 * j + 4 * head + tile
                n = P * (tile + 1)
                pe.wait_ge(qk_ready, 4 * j + 4)
                pe.wait_ge(exp_done, 2 * u)
                for c in range(2):
                    rows = slice(HD * c, HD * c + HD)
                    last = nc.tensor.matmul(scores[:, 2 * (tile % 2) + c, 0:n],
                                            qT[rows, head, P * tile:P * tile + P], kT[rows, head, 0:n],
                                            start=True, stop=True)
                last.then_inc(score_done, 1)

            def turn_diff(j, head, tile):
                u = 8 * j + 4 * head + tile
                pe.wait_ge(diff_ready, u + 3)
                pe.wait_ge(diffT_ready, u)
                for b in range(tile + 1):
                    last = nc.tensor.transpose(turn[:, 0, P * b:P * b + P], diff[:, tile % 2, P * b:P * b + P],
                                               identity[:])
                last.then_inc(turned, 1)

            def values(j, head):
                pe.wait_ge(diffT_ready, 8 * j + 4 * head + 4)
                stream.wait_out(pe, MIX_0 + MIX_CHUNKS * j + 2, 1)
                pe.wait_ge(o_ready, 2 * j + head)
                for tile in range(TT):
                    at = tile * (tile + 1) // 2
                    for b in range(tile + 1):
                        last = nc.tensor.matmul(pv[:, 0, P * tile:P * tile + P], diffT[:, at + b],
                                                v[:, b, P * head:P * head + P], start=(b == 0), stop=(b == tile))
                last.then_inc(pv_done, 1)

            def turn_y(j, head):
                pe.wait_ge(y_ready, j + 1)
                pe.wait_ge(diffT_ready, 8 * j + 8)
                pe.wait_ge(y_split, 2 * j + head)
                for tile in range(TT):
                    last = nc.tensor.transpose(turn[:, 0, P * tile:P * tile + P], o[:, TT * head + tile],
                                               identity[:])
                last.then_inc(y_turned, 1)

            def round_of(j, first):
                project(j, 0, 0)
                project(j, 0, 1)
                project(j, 1, 0)
                if not first:
                    turn_y(j - 1, 0)
                project(j, 1, 1)
                if not first:
                    turn_y(j - 1, 1)
                rotate_halves(j, 0)
                stream.rows(pe, [proj[:, half] for half in range(2)], MIX_0 + MIX_CHUNKS * j + 2, 2, *xT)
                rotate_halves(j, 1)
                project(j, 3, 0)
                score(j, 0, 0)
                score(j, 0, 1)
                project(j, 3, 1)
                score(j, 0, 2)
                score(j, 0, 3)
                project(j, 4, 0)
                for tile in range(2):
                    turn_diff(j, 0, tile)
                score(j, 1, 0)
                score(j, 1, 1)
                project(j, 4, 1)
                for tile in range(2, TT):
                    turn_diff(j, 0, tile)
                values(j, 0)
                score(j, 1, 2)
                score(j, 1, 3)
                project(j, 5, 0)
                for tile in range(TT):
                    turn_diff(j, 1, tile)
                values(j, 1)
                project(j, 5, 1)

            round_of(0, True)
            with pe.Fori(1, MIX_ROUNDS) as j:
                round_of(j, False)
            turn_y(MIX_ROUNDS - 1, 0)
            turn_y(MIX_ROUNDS - 1, 1)

        @block.scalar
        def _(act):
            act.sem_inc(stream.bank_free, SLOTS)
            act.sem_inc(exp_done, 2)
            stream.take_hi(act, 0, 0)
            act.wait_ge(x_loaded, 16)
            for c in range(DT):
                nc.scalar.activation(xT[0][:, c], raws[:, c], ACT.Copy).then_inc(x_hi, 1)
            act.wait_ge(tables_ready, 1)
            nc.scalar.activation(sinT[:], sinT[:], ACT.Sin).then_inc(sin_ready, 1)
            nc.scalar.activation(cosT[:], cosT[:], ACT.Sin).then_inc(sin_ready, 1)
            nc.scalar.activation(lam[:, 2:4], lam[:, 0:2], ACT.Exp).then_inc(lam_exp, 1)

            def bring(j, m, half, free, value):
                act.wait_ge(free, value)
                stream.evacuate(act, MIX_0 + MIX_CHUNKS * j + m, half, raws[:, RAW[m] + half], proj[:, half])

            def exponentials(j, head, tile):
                n = P * (tile + 1)
                u = 8 * j + 4 * head + tile
                act.wait_ge(bias_ready, u + 1)
                act.wait_ge(diff_ready, u + 1)
                for c in range(2):
                    nc.scalar.activation(probs[:, tile % 2, c, 0:n], scores[:, 2 * (tile % 2) + c, 0:n], ACT.Exp,
                                         bias=stat[:, tile % 2, 2 + c:3 + c], scale=SCALE,
                                         accum_out=stat[:, tile % 2, 4 + c:5 + c]).then_inc(exp_done, 1)

            def bring_diffT(j, head, tile):
                u = 8 * j + 4 * head + tile
                act.wait_ge(turned, u + 3)
                act.wait_ge(pv_done, 2 * j + head)
                at = tile * (tile + 1) // 2
                nc.scalar.activation(diffT[:, at:at + tile + 1],
                                     turn[:, 0, 0:P * (tile + 1)].rearrange("p (b n) -> p b n", n=P),
                                     ACT.Copy).then_inc(diffT_ready, 1)

            def bring_o(j, head):
                act.wait_ge(pv_done, 2 * j + head + 1)
                act.wait_ge(y_turned, 2 * j)
                nc.scalar.activation(o[:, TT * head:TT * head + TT], pv[:, 0].rearrange("p (t n) -> p t n", n=P),
                                     ACT.Copy).then_inc(o_ready, 1)

            def bring_y_hi(j, head):
                act.wait_ge(y_turned, 2 * j + head + 1)
                nc.scalar.activation(row(attn[0], 2 * j + head), turn[:, 0], ACT.Copy).then_inc(y_hi, 1)

            def round_of(j, first):
                def ahead(m):
                    stream.take_hi(act, MIX_0 + MIX_CHUNKS * j + m + 1, m + 1)

                for m in range(2):
                    ahead(m)
                    for half in range(2):
                        bring(j, m, half, conv_done, 2 * j)
                        if m == 1 and not first:
                            bring_y_hi(j - 1, half)
                ahead(2)
                act.wait_ge(pv_done, 2 * j)
                for half in range(2):
                    stream.evacuate(act, MIX_0 + MIX_CHUNKS * j + 2, half, v[:, 2 * half:2 * half + 2],
                                    proj[:, half].rearrange("p (k n) -> p k n", k=2))
                ahead(3)
                bring(j, 3, 0, conv_done, 2 * j)
                exponentials(j, 0, 0)
                exponentials(j, 0, 1)
                bring(j, 3, 1, conv_done, 2 * j)
                exponentials(j, 0, 2)
                exponentials(j, 0, 3)
                ahead(4)
                bring(j, 4, 0, qk_ready, 4 * j + 2)
                bring_diffT(j, 0, 0)
                bring_diffT(j, 0, 1)
                exponentials(j, 1, 0)
                exponentials(j, 1, 1)
                bring(j, 4, 1, qk_ready, 4 * j + 2)
                bring_diffT(j, 0, 2)
                bring_diffT(j, 0, 3)
                bring_o(j, 0)
                exponentials(j, 1, 2)
                exponentials(j, 1, 3)
                ahead(5)
                bring(j, 5, 0, qk_ready, 4 * j + 4)
                for tile in range(TT):
                    bring_diffT(j, 1, tile)
                bring_o(j, 1)
                bring(j, 5, 1, qk_ready, 4 * j + 4)
                act.wait_ge(sums_ready, j + 1)
                nc.scalar.activation(o_stat[:, 1], o_stat[:, 0], ACT.Sqrt, bias=lam[:, 7:8],
                                     scale=1.0 / P).then_inc(root_ready, 1)

            round_of(0, True)
            with act.Fori(1, MIX_ROUNDS) as j:
                round_of(j, False)
            for head in range(2):
                bring_y_hi(MIX_ROUNDS - 1, head)

        @block.vector
        def _(dve):
            v_ = nc.vector
            chain = Chain(dve, dve_step)
            step = chain.step
            dve.sem_inc(diff_ready, 2)
            for c in range(DT):
                dve.wait_ge(x_hi, c + 1)
                v_.tensor_tensor(xT[1][:, c], raws[:, c], f32(xT[0][:, c]), ALU.subtract).then_inc(x_split, 1)
            step(v_.memset(z[:, 0:2], 0.0))
            step(v_.memset(lam[:, 7:8], LN_EPS))
            dve.wait_ge(const_loaded, 16 * CONSTS)
            step(v_.tensor_copy(part[:], position))
            step(v_.tensor_scalar(y[:], part[:], freq[:, 0:1], None, ALU.mult))
            for to, quarter in ((sinT, 0.0), (cosT, 0.25)):
                step(v_.tensor_scalar(part[:], y[:], 1 / TURN, quarter, ALU.mult, ALU.add))
                step(v_.tensor_scalar(part[:], part[:], MAGIC, None, ALU.add))
                step(v_.tensor_scalar(part[:], part[:], -MAGIC, None, ALU.add))
                step(v_.scalar_tensor_tensor(to[:], part[:], -TURN_1, y[:], ALU.mult, ALU.add))
                step(v_.scalar_tensor_tensor(to[:], part[:], -TURN_2, to[:], ALU.mult, ALU.add))
                step(v_.scalar_tensor_tensor(to[:], part[:], -TURN_3, to[:], ALU.mult, ALU.add))
                step(v_.tensor_scalar(to[:], to[:], quarter * TURN, None, ALU.add))
                step(v_.tensor_scalar(to[:], to[:], HALF_TURN, -HALF_TURN, ALU.min, ALU.max))
            for n in range(2):
                step(v_.tensor_tensor(part[:, 0:HD], lam_in[:, 2 * n], lam_in[:, 2 * n + 1], ALU.mult))
                last = v_.tensor_reduce(lam[:, n:n + 1], part[:, 0:HD], AX.X, ALU.add)
                if n == 0:
                    step(last)
            last.then_inc(tables_ready, 1)
            dve.wait_ge(lam_exp, 1)
            step(v_.tensor_tensor(lam[:, 4:5], lam[:, 3:4], lam[:, 2:3], ALU.subtract))
            step(v_.tensor_scalar(lam[:, 5:6], lam[:, 4:5], -LAM_INIT, None, ALU.add))
            dve.wait_ge(sin_ready, 2)

            def rotate(j, m, half, to):
                dve.wait_ge(swap_done, 4 * j + 2 * m + half + 1)
                dve.wait_ge(score_done, 8 * j)
                step(v_.tensor_tensor(part[:], raws[:, RAW[m] + half], cosT[:], ALU.mult))
                step(v_.tensor_tensor(y[:], turn[:, 0], sinT[:], ALU.mult))
                v_.tensor_tensor(to[:, half], part[:], y[:], ALU.add).then_inc(qk_ready, 1)

            def maximum(j, head, tile):
                u = 8 * j + 4 * head + tile
                both = slice(2 * (tile % 2), 2 * (tile % 2) + 2)
                dve.wait_ge(score_done, u + 1)
                diagonal = scores[:, both, P * tile:P * tile + P]
                step(v_.tensor_tensor(diagonal, diagonal, mask[:, None, :].broadcast_to([P, 2, P]), ALU.add))
                step(v_.tensor_reduce(stat[:, tile % 2, 0:2], scores[:, both, 0:P * (tile + 1)], AX.X, ALU.max))
                v_.tensor_scalar(stat[:, tile % 2, 2:4], stat[:, tile % 2, 0:2], -SCALE, None,
                                 ALU.mult).then_inc(bias_ready, 1)

            def difference(j, head, tile):
                u = 8 * j + 4 * head + tile
                n = P * (tile + 1)
                s = tile % 2
                dve.wait_ge(exp_done, 2 * u + 4)
                dve.wait_ge(turned, u + 1)
                step(v_.reciprocal(stat[:, s, 6:8], stat[:, s, 4:6]))
                step(v_.tensor_tensor(stat[:, s, 8:9], stat[:, s, 7:8], lam[:, 5:6], ALU.mult))
                step(v_.tensor_scalar(diff[:, s, 0:n], probs[:, s, 1, 0:n], stat[:, s, 8:9], None, ALU.mult))
                v_.scalar_tensor_tensor(diff[:, s, 0:n], probs[:, s, 0, 0:n], stat[:, s, 6:7], diff[:, s, 0:n],
                                        ALU.mult, ALU.add).then_inc(diff_ready, 1)

            def short_conv(j, half):
                at = 2 * j + half
                stream.wait_out(dve, MIX_0 + MIX_CHUNKS * j + 5, half)
                step(v_.tensor_tensor(z[:, 2:T + 2], raws[:, RAW[5] + half], raws[:, RAW[3] + half], ALU.mult))
                step(v_.tensor_scalar(y[:], z[:, 2:T + 2], conv_w[:, 2, bass.ds(at, 1)], conv_b[:, bass.ds(at, 1)],
                                      ALU.mult, ALU.add))
                step(v_.scalar_tensor_tensor(y[:], z[:, 1:T + 1], conv_w[:, 1, bass.ds(at, 1)], y[:], ALU.mult,
                                             ALU.add))
                step(v_.scalar_tensor_tensor(y[:], z[:, 0:T], conv_w[:, 0, bass.ds(at, 1)], y[:], ALU.mult, ALU.add))
                step(v_.tensor_tensor(y[:], y[:], raws[:, RAW[4] + half], ALU.mult))
                hi, lo = row(conv[0], at), row(conv[1], at)
                step(v_.tensor_copy(hi, y[:]))
                v_.tensor_tensor(lo, y[:], f32(hi), ALU.subtract).then_inc(conv_done, 1)

            def take_y_lo(j, head):
                dve.wait_ge(y_hi, 2 * j + head + 1)
                at = 2 * j + head
                v_.tensor_tensor(row(attn[1], at), turn[:, 0], f32(row(attn[0], at)),
                                 ALU.subtract).then_inc(y_split, 1)

            def round_of(j, first):
                if not first:
                    take_y_lo(j - 1, 0)
                    take_y_lo(j - 1, 1)
                for m, to in ((0, qT), (1, kT)):
                    for half in range(2):
                        rotate(j, m, half, to)
                for head in range(2):
                    for pair in range(2):
                        for tile in (2 * pair, 2 * pair + 1):
                            maximum(j, head, tile)
                        for tile in (2 * pair, 2 * pair + 1):
                            difference(j, head, tile)
                short_conv(j, 0)
                dve.wait_ge(o_ready, 2 * j + 2)
                step(v_.tensor_tensor(squares, o[:], o[:], ALU.mult))
                v_.tensor_reduce(o_stat[:, 0], squares, AX.X, ALU.add).then_inc(sums_ready, 1)
                short_conv(j, 1)
                dve.wait_ge(root_ready, j + 1)
                step(v_.reciprocal(o_stat[:, 2], o_stat[:, 1]))
                step(v_.scalar_tensor_tensor(o[:], o[:], 1.0 - LAM_INIT,
                                             o_stat[:, 2, :, None].broadcast_to([P, 2 * TT, P]), ALU.mult, ALU.mult))
                v_.tensor_tensor(o[:], o[:], subln[:, None, :].broadcast_to([P, 2 * TT, P]),
                                 ALU.mult).then_inc(y_ready, 1)

            before = chain.n
            round_of(0, True)
            per = chain.n - before
            with dve.Fori(1, MIX_ROUNDS) as j:
                chain.round(j - 1, per)
                round_of(j, False)
            chain.done(MIX_ROUNDS - 1)
            for head in range(2):
                take_y_lo(MIX_ROUNDS - 1, head)


def merge(nc, a, stream, merged, xT, conv, attn):
    with ExitStack() as ctx:
        gate, branch, total, gate_b = tiles(
            nc, ctx, ("gate", [P, 2, 2, T], F32), ("branch", [P, 2, 2, T], F32), ("total", [P, T], F32),
            ("gate_b", [P, 2 * DT], F32))
        proj, = banks(nc, ctx, ("proj_merge", 2))
        bias_loaded, merge_done, step_done = sems(nc, ctx, "bias_loaded merge_done merge_step")
        block = ctx.enter_context(nc.Block())

        @block.sync
        def _(sp):
            sp.dma_start(gate_b[:], a["gate_b_columns"]).then_inc(bias_loaded, 16)
            stream.load_stage(sp, MERGE_0, WO_0)

        @block.gpsimd
        def _(pool):
            take_los(pool, stream, MERGE_0, MERGE_ROUNDS, MERGE_CHUNKS, True)

        @block.tensor
        def _(pe):
            with pe.Fori(0, MERGE_ROUNDS) as j:
                for m, right in enumerate((xT, xT, conv, attn)):
                    for half in range(2):
                        stream.columns(pe, proj[:, half], MERGE_0 + MERGE_CHUNKS * j + m, m, half, *right)

        @block.scalar
        def _(act):
            act.wait_ge(bias_loaded, 16)
            with act.Fori(0, MERGE_ROUNDS) as j:
                for m in range(MERGE_CHUNKS):
                    n = MERGE_0 + MERGE_CHUNKS * j + m
                    stream.take_hi(act, n + 1, m + 1)
                    for half in range(2):
                        if m == 0 and half == 0:
                            act.wait_ge(merge_done, 2 * j + 1)
                        if m < 2:
                            stream.evacuate(act, n, half, gate[:, m, half], proj[:, half], ACT.Sigmoid,
                                            bias=gate_b[:, bass.ds(2 * j + DT * m + half, 1)])
                        else:
                            stream.evacuate(act, n, half, branch[:, m - 2, half], proj[:, half])

        @block.vector
        def _(dve):
            v_ = nc.vector
            chain = Chain(dve, step_done)
            dve.sem_inc(merge_done, 1)
            with dve.Fori(0, MERGE_ROUNDS) as j:
                chain.round(j, 2 * 4)
                for half in range(2):
                    stream.wait_out(dve, MERGE_0 + MERGE_CHUNKS * j + 3, half)
                    at = 2 * j + half
                    hi, lo = row(merged[0], at), row(merged[1], at)
                    chain.step(v_.tensor_tensor(branch[:, 0, half], branch[:, 0, half], gate[:, 0, half], ALU.mult))
                    chain.step(v_.tensor_tensor(branch[:, 1, half], branch[:, 1, half], gate[:, 1, half], ALU.mult))
                    chain.step(v_.tensor_tensor(total[:], branch[:, 0, half], branch[:, 1, half], ALU.add))
                    chain.step(v_.tensor_copy(hi, total[:]))
                    v_.tensor_tensor(lo, total[:], f32(hi), ALU.subtract).then_inc(merge_done, 1)
            chain.done(MERGE_ROUNDS)


class LayerNorm:

    def __init__(self, nc, ctx, name, pieces):
        self.nc, self.width = nc, D // pieces
        self.stats, self.mv, self.gain, self.shift, self.eps = tiles(
            nc, ctx, (f"{name}_stats", [P, TT, pieces, 6], F32), (f"{name}_mv", [P, TT, 4], F32),
            (f"{name}_gain", [P, D], F32), (f"{name}_shift", [P, D], F32), (f"{name}_eps", [P, 1], F32))
        self.loaded, self.var_ready, self.root_ready, self.steps = sems(
            nc, ctx, f"{name}_loaded {name}_var_ready {name}_root_ready {name}_steps")

    def load(self, sp, gain, shift):
        sp.dma_start(self.gain[:], gain.broadcast_to([P, D])).then_inc(self.loaded, 16)
        sp.dma_start(self.shift[:], shift.broadcast_to([P, D])).then_inc(self.loaded, 16)

    def root(self, act, t):
        act.wait_ge(self.var_ready, t + 1)
        self.nc.scalar.activation(self.mv[:, t, 2:3], self.mv[:, t, 1:2], ACT.Sqrt,
                                  bias=self.eps[:, 0:1]).then_inc(self.root_ready, 1)

    def begin(self, dve):
        self.dve, self.chain = dve, Chain(dve, self.steps)
        self.chain.step(self.nc.vector.memset(self.eps[:], LN_EPS))
        dve.wait_ge(self.loaded, 32)

    def piece(self, z, t, g):
        self.chain.step(self.nc.vector.bn_stats(self.stats[:, t, g], z[:, t, self.width * g:self.width * g + self.width]))

    def variance(self, t):
        self.nc.vector.bn_aggr(self.mv[:, t, 0:2], self.stats[:, t].rearrange("p a b -> p (a b)")) \
            .then_inc(self.var_ready, 1)

    def tile(self, z, t):
        v_, step = self.nc.vector, self.chain.step
        self.dve.wait_ge(self.root_ready, t + 1)
        step(v_.reciprocal(self.mv[:, t, 3:4], self.mv[:, t, 2:3]))
        step(v_.tensor_scalar(z[:, t], z[:, t], self.mv[:, t, 0:1], self.mv[:, t, 3:4], ALU.subtract, ALU.mult))
        step(v_.tensor_tensor(z[:, t], z[:, t], self.gain[:], ALU.mult))
        return v_.tensor_tensor(z[:, t], z[:, t], self.shift[:], ALU.add)


def norm1(nc, a, stream, identity, merged, x1, xT):
    with ExitStack() as ctx:
        proj, turn = banks(nc, ctx, ("proj_o", 2), ("turn_x1", 4))
        x_loaded, added, normed, x1_turned, x1_hi, x1_split = sems(
            nc, ctx, "x_rows_loaded added normed x1_turned x1_hi x1_split")
        chunks = WO_ROUNDS * WO_CHUNKS
        norm = LayerNorm(nc, ctx, "ln1", chunks)
        block = ctx.enter_context(nc.Block())

        @block.sync
        def _(sp):
            sp.dma_start(x1[:], a["x"][0].rearrange("(t p) d -> p t d", p=P)).then_inc(x_loaded, 16)
            norm.load(sp, a["ln1_g"], a["ln1_b"])
            stream.load_stage(sp, WO_0, PQ_0)

        @block.gpsimd
        def _(pool):
            take_los(pool, stream, WO_0, WO_ROUNDS, WO_CHUNKS, True)

        @block.tensor
        def _(pe):
            for n in range(chunks):
                stream.rows(pe, [proj[:, half] for half in range(2)], WO_0 + n, n, *merged)
            for u in range(2 * TT):
                t, g = u // 2, u % 2
                pe.wait_ge(normed, t + 1)
                if u >= 4:
                    pe.wait_ge(x1_split, u - 3)
                for c in range(4):
                    d = 4 * g + c
                    last = nc.tensor.transpose(turn[:, u % 4, P * c:P * c + P], x1[:, t, P * d:P * d + P], identity[:])
                last.then_inc(x1_turned, 1)

        @block.scalar
        def _(act):
            for n in range(chunks):
                stream.take_hi(act, WO_0 + n + 1, n + 1)
            for t in range(TT):
                norm.root(act, t)
            for u in range(2 * TT):
                t, g = u // 2, u % 2
                act.wait_ge(x1_turned, u + 1)
                nc.scalar.activation(xT[0][:, 4 * g:4 * g + 4, P * t:P * t + P],
                                     turn[:, u % 4].rearrange("p (c n) -> p c n", c=4), ACT.Copy).then_inc(x1_hi, 1)

        @block.vector
        def _(dve):
            v_ = nc.vector
            norm.begin(dve)
            dve.wait_ge(x_loaded, 16)
            for n in range(chunks):
                for half in range(2):
                    dve.wait_ge(stream.unit_done, 2 * (WO_0 + n) + half + 1)
                    at = (slice(None), slice(2 * half, 2 * half + 2), slice(CW * n, CW * n + CW))
                    v_.scalar_tensor_tensor(x1[at], x1[at], ALPHA, proj[:, half].rearrange("p (k n) -> p k n", k=2),
                                            ALU.mult, ALU.add).then_inc(stream.bank_free, 1)
                    stream.wait_out(dve, WO_0 + n, half)
                    for t in (2 * half, 2 * half + 1):
                        norm.piece(x1, t, n)
                        if n == chunks - 1:
                            norm.variance(t)
                    if n == chunks - 1:
                        for t in (2 * half, 2 * half + 1):
                            norm.tile(x1, t).then_inc(normed, 1)
            for u in range(2 * TT):
                t, g = u // 2, u % 2
                dve.wait_ge(x1_hi, u + 1)
                at = (slice(None), slice(4 * g, 4 * g + 4), slice(P * t, P * t + P))
                v_.tensor_tensor(xT[1][at], turn[:, u % 4].rearrange("p (c n) -> p c n", c=4), f32(xT[0][at]),
                                 ALU.subtract).then_inc(x1_split, 1)


class Experts:

    def __init__(self, nc, ctx, source, xT, gelus):
        self.nc, self.source, self.xT, self.gelus = nc, source, xT, gelus
        self.raw, self.hi, self.lo, self.gelu = tiles(
            nc, ctx, ("u_raw", [P, 2, DT, P], F32), ("u_hi", [P, 2, DT, P], F32R), ("u_lo", [P, 2, DT, P], F32R),
            ("gelu", [P, 2, T], F32))
        self.loaded = sems(nc, ctx, "u_loaded0 u_loaded1")
        self.stored = sems(nc, ctx, "gelu_stored0 gelu_stored1")
        self.hi_taken, self.lo_taken, self.dot_done, self.gelu_done = sems(
            nc, ctx, "u_hi_taken u_lo_taken dot_done gelu_done")

    def load(self, sp, i, r):
        sp.wait_ge(self.lo_taken, i + 1)
        sp.dma_start(self.raw[:, r], self.source[i]).then_inc(self.loaded[r], 16)

    def take_hi(self, act, i, r):
        act.wait_ge(self.loaded[r], 8 * (i - r) + 16)
        act.wait_ge(self.dot_done, i + 1)
        self.nc.scalar.activation(self.hi[:, r], self.raw[:, r], ACT.Copy).then_inc(self.hi_taken, 1)

    def take_lo(self, pool, i, r):
        pool.wait_ge(self.hi_taken, i + 1)
        self.nc.gpsimd.tensor_tensor(self.lo[:, r], self.raw[:, r], f32(self.hi[:, r]),
                                     ALU.subtract).then_inc(self.lo_taken, 1)

    def product(self, pe, i, r, dots):
        hi, lo, right = self.hi[:, r], self.lo[:, r], self.xT
        pe.wait_ge(self.hi_taken, i + 1)
        pe.wait_ge(self.gelu_done, i + 1)
        for d in range(DT):
            self.nc.tensor.matmul(dots[:, r], hi[:, d], right[0][:, d], start=(d == 0), stop=False)
            self.nc.tensor.matmul(dots[:, r], hi[:, d], right[1][:, d], start=False, stop=False)
        pe.wait_ge(self.lo_taken, i + 3)
        for d in range(DT):
            last = self.nc.tensor.matmul(dots[:, r], lo[:, d], right[0][:, d], start=False, stop=(d == DT - 1))
        last.then_inc(self.dot_done, 1)

    def finish(self, act, i, r, dots):
        act.wait_ge(self.dot_done, i + 3)
        act.wait_ge(self.stored[r], 8 * (i - r) + 16)
        self.nc.scalar.activation(self.gelu[:, r], dots[:, r], ACT.Gelu).then_inc(self.gelu_done, 1)
        act.wait_ge(self.gelu_done, i + 3)
        act.dma_start(self.gelus[i], self.gelu[:, r]).then_inc(self.stored[r], 16)


def pairs_of(engine, first, last, body):
    with engine.Fori(first // 2, last // 2) as k:
        for r in range(2):
            body(2 * k + r, r)


def keys(nc, a, stream, experts, identity, xT, x1, picks):
    with ExitStack() as ctx:
        (key_rows, q, s, s_rest, best, best_at, best_at_f, pair, pair_rest, top, top_at, first, second, number,
         one_hot, count16, packed, sums, weight) = tiles(
            nc, ctx,
            ("sub_keys", [P, 2, 2, N_KEYS], F32), ("q", [P, 2, T], F32), ("s", [P, PK_HEADS, TT, 2, N_KEYS], F32),
            ("s_rest", [P, TT * 2, N_KEYS], F32), ("best", [P, TT, 2, TOPK], F32),
            ("best_at", [P, TT, 2, TOPK], U32), ("best_at_f", [P, TT, 2, TOPK], F32),
            ("pair", [P, TT, TOPK * TOPK], F32), ("pair_rest", [P, TT, TOPK * TOPK], F32),
            ("top", [P, TT, TOPK], F32), ("top_at", [P, TT, TOPK], U32), ("first_at", [P, TT, TOPK], U32),
            ("second_at", [P, TT, TOPK], U32), ("number", [P, TT, TOPK], F32),
            ("one_hot", [P, TT, TOPK, TOPK], F32), ("count16", [P, TOPK], F32),
            ("packed", [P, 3, TT, PK_HEADS, TOPK], F32), ("weight_sums", [P, 2, TT, PK_HEADS], F32),
            ("weight", [P, TT, PK_HEADS, TOPK], F32))
        proj, score, dots = banks(nc, ctx, ("proj_q", 2), ("score_k", 2), ("dots_keys", 2))
        turn = [proj[:, 0], proj[:, 1], score[:, 0]]
        k_loaded = sems(nc, ctx, "sub_keys_loaded0 sub_keys_loaded1")
        (x1_scaled, c_loaded, q_scored, s_out, exp_asked, exp_done, all_packed, packed_turned, picks_out,
         steps) = sems(nc, ctx, "x1_scaled_done count16_loaded q_scored s_out k_exp_asked k_exp_done all_packed "
                       "packed_turned picks_out k_steps")
        block = ctx.enter_context(nc.Block())

        @block.sync
        def _(sp):
            sp.dma_start(count16[:], a["count"][:, 0:TOPK]).then_inc(c_loaded, 16)
            for m in range(2):
                sp.dma_start(key_rows[:, m], a["sub_keys_columns"][m]).then_inc(k_loaded[m], 16)
            for h in range(PK_HEADS - 2):
                m = h % 2
                stream.load(sp, PQ_0 + h + 2, m)
                sp.wait_ge(q_scored, 2 * h + 2)
                sp.dma_start(key_rows[:, m], a["sub_keys_columns"][h + 2]).then_inc(k_loaded[m], 16)
            pairs_of(sp, 0, TILES_BESIDE + 2, lambda i, r: experts.load(sp, i, r))

        @block.gpsimd
        def _(pool):
            pool.sem_inc(experts.lo_taken, 2)
            for t in range(TT):
                nc.gpsimd.tensor_scalar(x1[:, t], x1[:, t], ALPHA, None, ALU.mult).then_inc(x1_scaled, 1)
            pool.wait_ge(x1_scaled, TT)
            take_los(pool, stream, PQ_0, PQ_ROUNDS, PQ_CHUNKS, False)
            experts.take_lo(pool, 0, 0)
            with pool.Fori(0, TILES_BESIDE // 2) as k:
                for r in range(2):
                    experts.take_lo(pool, 2 * k + r + 1, 1 - r)

        @block.tensor
        def _(pe):
            pe.sem_inc(experts.dot_done, 2)
            with pe.Fori(0, PQ_ROUNDS) as j:
                for m in range(2):
                    h = 2 * j + m
                    for half in range(2):
                        stream.columns(pe, proj[:, half], PQ_0 + h, m, half, *xT)
                    pe.wait_ge(k_loaded[m], 16 * j + 16)
                    for half in range(2):
                        stream.wait_out(pe, PQ_0 + h, half)
                        pe.wait_ge(s_out, 2 * h + half + 1)
                        for t in range(TT):
                            last = nc.tensor.matmul(score[:, half, P * t:P * t + P], q[:, half, P * t:P * t + P],
                                                    key_rows[:, m, half], start=True, stop=True)
                        last.then_inc(q_scored, 1)
            pairs_of(pe, 0, TILES_BESIDE - 2, lambda i, r: experts.product(pe, i, r, dots))
            pe.wait_ge(s_out, 2 * PK_HEADS + 1)
            pe.wait_ge(all_packed, 1)
            for n in range(3):
                for t in range(TT):
                    last = nc.tensor.transpose(turn[n][:, P * t:P * t + P],
                                               packed[:, n, t].rearrange("p h k -> p (h k)"), identity[:])
            last.then_inc(packed_turned, 1)
            for i in range(TILES_BESIDE - 2, TILES_BESIDE):
                experts.product(pe, i, i % 2, dots)

        @block.scalar
        def _(act):
            act.sem_inc(s_out, 1)
            act.sem_inc(experts.gelu_done, 2)
            for r in range(2):
                act.sem_inc(experts.stored[r], 16)

            def head(j, m, ahead):
                h = 2 * j + m
                if ahead:
                    stream.take_hi(act, PQ_0 + h + 1, m + 1)
                act.wait_ge(q_scored, 2 * h)
                for half in range(2):
                    stream.evacuate(act, PQ_0 + h, half, q[:, half], proj[:, half])
                for half in range(2):
                    act.wait_ge(q_scored, 2 * h + half + 1)
                    nc.scalar.activation(s_of(h)[:, :, half], score[:, half].rearrange("p (t n) -> p t n", t=TT),
                                         ACT.Copy).then_inc(s_out, 1)

            def s_of(h):
                return s[:, h] if isinstance(h, int) else \
                    s[:, bass.ds(h, 1)].rearrange("p h t c n -> p (h t) c n")

            def tile(i, r):
                experts.take_hi(act, i + 1, 1 - r)
                experts.finish(act, i, r, dots)

            head(0, 0, True)
            head(0, 1, True)
            with act.Fori(1, PQ_ROUNDS - 1) as j:
                for m in range(2):
                    head(j, m, True)
            head(PQ_ROUNDS - 1, 0, True)
            experts.take_hi(act, 0, 0)
            head(PQ_ROUNDS - 1, 1, False)
            pairs_of(act, 0, TILES_BESIDE - 4, tile)
            act.wait_ge(exp_asked, 1)
            nc.scalar.activation(weight[:], packed[:, 2], ACT.Exp).then_inc(exp_done, 1)
            pairs_of(act, TILES_BESIDE - 4, TILES_BESIDE - 2, tile)
            act.wait_ge(packed_turned, 1)
            for n in range(3):
                nc.scalar.activation(picks[:, n], turn[n], ACT.Copy).then_inc(picks_out, 1)
            pairs_of(act, TILES_BESIDE - 2, TILES_BESIDE, tile)
            act.wait_ge(picks_out, 3)

        @block.vector
        def _(dve):
            v_ = nc.vector
            chain = Chain(dve, steps)
            step = chain.step
            dve.wait_ge(c_loaded, 16)

            def top16(values, rest, out, out_at):
                step(v_.max(out[:, 0:8], values))
                step(v_.match_replace(rest, out[:, 0:8], values, NEG))
                step(v_.max(out[:, 8:16], rest))
                step(v_.max_index(out_at[:, 0:8], out[:, 0:8], values))
                step(v_.max_index(out_at[:, 8:16], out[:, 8:16], rest))

            for h in range(PK_HEADS):
                dve.wait_ge(s_out, 2 * h + 3)
                for t in range(TT):
                    for half in range(2):
                        top16(s[:, h, t, half], s_rest[:, 2 * t + half], best[:, t, half], best_at[:, t, half])
                step(v_.tensor_copy(best_at_f[:], best_at[:]))
                for t in range(TT):
                    step(v_.tensor_tensor(pair[:, t].rearrange("p (a b) -> p a b", a=TOPK),
                                          best[:, t, 0, :, None].broadcast_to([P, TOPK, TOPK]),
                                          best[:, t, 1, None, :].broadcast_to([P, TOPK, TOPK]), ALU.add))
                for t in range(TT):
                    top16(pair[:, t], pair_rest[:, t], top[:, t], top_at[:, t])
                step(v_.tensor_tensor(packed[:, 2, :, h], top[:], top[:, :, 0:1].broadcast_to([P, TT, TOPK]),
                                      ALU.subtract))
                if h == PK_HEADS - 1:
                    dve.sem_inc(exp_asked, 1)
                step(v_.tensor_scalar(first[:], top_at[:], 4, None, ALU.logical_shift_right))
                step(v_.tensor_scalar(second[:], top_at[:], 15, None, ALU.bitwise_and))
                for n, at in enumerate((first, second)):
                    step(v_.tensor_copy(number[:], at[:]))
                    step(v_.tensor_tensor(one_hot[:].rearrange("p t a b -> p (t a) b"),
                                          number[:].rearrange("p t a -> p (t a)")[:, :, None]
                                          .broadcast_to([P, TT * TOPK, TOPK]),
                                          count16[:, None, :].broadcast_to([P, TT * TOPK, TOPK]), ALU.is_equal))
                    step(v_.tensor_tensor(one_hot[:], one_hot[:], best_at_f[:, :, n, None, :]
                                          .broadcast_to([P, TT, TOPK, TOPK]), ALU.mult))
                    step(v_.tensor_reduce(packed[:, n, :, h], one_hot[:], AX.X, ALU.add))
            dve.wait_ge(exp_done, 1)
            step(v_.tensor_reduce(sums[:, 0], weight[:], AX.X, ALU.add))
            step(v_.reciprocal(sums[:, 1], sums[:, 0]))
            v_.tensor_tensor(packed[:, 2], weight[:], sums[:, 1, :, :, None]
                             .broadcast_to([P, TT, PK_HEADS, TOPK]), ALU.mult).then_inc(all_packed, 1)


def gate_matrix(nc, a, experts, picks, gates):
    TILES = T // PER_TILE
    PER_CHUNK = TOK // PER_TILE
    with ExitStack() as ctx:
        left, right, gate, count = tiles(
            nc, ctx, ("left", [P, 2, PER_TILE, P], F32), ("right", [P, 2, PER_TILE, P], F32),
            ("gate_chunk", [P, 2, N_KEYS, TOK], F32), ("count", [P, N_KEYS], F32))
        dots, built = banks(nc, ctx, ("dots_gate", 2), ("built", 4))
        flushed = sems(nc, ctx, "gate_stored0 gate_stored1")
        count_loaded, hot_ready, built_done, built_out, steps = sems(
            nc, ctx, "count_loaded hot_ready built_done built_out hot_steps")
        AFTER = TILES_BESIDE + TILES
        END = AFTER + TILES_AFTER
        block = ctx.enter_context(nc.Block())

        def built_of(r):
            return built[:, 2 * r:2 * r + 2].rearrange("p b (t n) -> p (b t) n", n=P)

        @block.sync
        def _(sp):
            sp.dma_start(count[:], a["count"]).then_inc(count_loaded, 16)
            pairs_of(sp, TILES_BESIDE + 2, END + 2, lambda i, r: experts.load(sp, i, r))

        @block.gpsimd
        def _(pool):
            with pool.Fori(TILES_BESIDE // 2, END // 2) as k:
                for r in range(2):
                    experts.take_lo(pool, 2 * k + r + 1, 1 - r)

        @block.tensor
        def _(pe):
            pe.sem_inc(built_done, 2)
            with pe.Fori(0, TILES // 2) as k:
                for r in range(2):
                    n = 2 * k + r
                    experts.product(pe, TILES_BESIDE + n, r, dots)
                    pe.wait_ge(hot_ready, n + 1)
                    pe.wait_ge(built_out, n + 1)
                    for t in range(PER_TILE):
                        last = nc.tensor.matmul(built_of(r)[:, t], left[:, r, t], right[:, r, t],
                                                start=True, stop=True)
                    last.then_inc(built_done, 1)
            pairs_of(pe, AFTER, END, lambda i, r: experts.product(pe, i, r, dots))

        @block.scalar
        def _(act):
            act.sem_inc(built_out, 2)
            for f in range(2):
                act.sem_inc(flushed[f], 16)
            with act.Fori(0, TILES // (2 * PER_CHUNK)) as c:
                for f in range(2):
                    with act.Fori(0, PER_CHUNK // 2) as k:
                        for r in range(2):
                            n = 2 * PER_CHUNK * c + 2 * k + PER_CHUNK * f + r
                            experts.take_hi(act, TILES_BESIDE + 1 + n, 1 - r)
                            experts.finish(act, TILES_BESIDE + n, r, dots)
                            act.wait_ge(built_done, n + 3)
                            if r == 0:
                                act.wait_ge(flushed[f], 16 * c + 16)
                            nc.scalar.activation(gate[:, f, :, bass.ds(2 * PER_TILE * k + PER_TILE * r, PER_TILE)],
                                                 built_of(r).rearrange("p t n -> p n t"),
                                                 ACT.Copy).then_inc(built_out, 1)
                    act.wait_ge(built_out, 2 * PER_CHUNK * c + PER_CHUNK * (f + 1) + 2)
                    act.dma_start(gates[2 * c + f], gate[:, f].rearrange("p n t -> p (n t)")) \
                        .then_inc(flushed[f], 16)

            def tile(i, r):
                experts.take_hi(act, i + 1, 1 - r)
                experts.finish(act, i, r, dots)
            pairs_of(act, AFTER, END, tile)
            for f in range(2):
                act.wait_ge(flushed[f], 16 * (TILES // (2 * PER_CHUNK)) + 16)

        @block.vector
        def _(dve):
            chain = Chain(dve, steps)
            dve.wait_ge(count_loaded, 16)
            with dve.Fori(0, TILES // 2) as k:
                chain.round(k, 2)
                for r in range(2):
                    n = 2 * k + r
                    dve.wait_ge(built_done, n + 1)
                    at = bass.ds(PER_TILE * n, PER_TILE)
                    first, second, weight = (picks[:, m, at][:, :, None].broadcast_to([P, PER_TILE, P])
                                             for m in range(3))
                    numbers = count[:, None, :].broadcast_to([P, PER_TILE, P])
                    chain.step(nc.vector.tensor_tensor(right[:, r], numbers, first, ALU.is_equal))
                    nc.vector.tensor_tensor(left[:, r], numbers, second, ALU.is_equal)
                    nc.vector.tensor_tensor(right[:, r], right[:, r], weight, ALU.mult).then_inc(hot_ready, 1)


class Sources:

    def __init__(self, nc, ctx, v_tab, gelus, gates):
        self.nc, self.gelus, self.gates = nc, gelus, gates
        self.v_tab = v_tab[0].rearrange("(n p) d -> n p d", p=P)
        self.raw, self.hi, self.lo, self.gelu, self.gate = tiles(
            nc, ctx, ("v_raw", [P, 2, D], F32), ("v_hi", [P, 2, GROUP, D], F32R), ("v_lo", [P, 2, GROUP, D], F32R),
            ("gelu_in", [P, 2, GROUP, T], F32), ("gate_in", [P, 2, T // TOK, GROUP * TOK], F32), side="right")
        self.v_loaded = sems(nc, ctx, "v_loaded0 v_loaded1")
        self.in_loaded = sems(nc, ctx, "gelu_gate_loaded0 gelu_gate_loaded1")
        self.hi_taken, self.lo_taken = sems(nc, ctx, "v_hi_taken v_lo_taken")

    def load_in(self, sp, j, s):
        self.load_gelu(sp, j, s)
        self.load_gate(sp, j, s)

    def load_gelu(self, sp, j, s):
        sp.dma_start(self.gelu[:, s], self.gelus[bass.ds(GROUP * j, GROUP)].rearrange("q p t -> p q t")) \
            .then_inc(self.in_loaded[s], 16)

    def load_gate(self, sp, j, s):
        sp.dma_start(self.gate[:, s], self.gates.rearrange("c p n -> p c n")
                     [:, :, bass.ds(GROUP * TOK * j, GROUP * TOK)]).then_inc(self.in_loaded[s], 16)

    def load_v(self, sp, j, q):
        i = GROUP * j + q
        if not isinstance(i, int) or i >= 2:
            sp.wait_ge(self.lo_taken, i - 1)
        sp.dma_start(self.raw[:, q % 2], self.v_tab[i]).then_inc(self.v_loaded[q % 2], 16)

    def take_hi(self, act, j, s, q):
        act.wait_ge(self.v_loaded[q % 2], 16 * (2 * j + q // 2) + 16)
        self.nc.scalar.activation(self.hi[:, s, q], self.raw[:, q % 2], ACT.Copy).then_inc(self.hi_taken, 1)

    def take_lo(self, pool, j, s, q):
        pool.wait_ge(self.hi_taken, GROUP * j + q + 1)
        self.nc.gpsimd.tensor_tensor(self.lo[:, s, q], self.raw[:, q % 2], f32(self.hi[:, s, q]),
                                     ALU.subtract).then_inc(self.lo_taken, 1)


def last_experts(nc, experts, sources):
    FIRST = TILES_BESIDE + T // PER_TILE + TILES_AFTER
    V_TILES = 2 * GROUP
    assert N_KEYS - FIRST >= V_TILES + 4
    with ExitStack() as ctx:
        dots, = banks(nc, ctx, ("dots_last", 2))
        block = ctx.enter_context(nc.Block())

        @block.sync
        def _(sp):
            for n in range(V_TILES):
                experts.load(sp, FIRST + n + 2, n % 2)
                if n < 4:
                    (sources.load_gelu, sources.load_gate)[n % 2](sp, n // 2, n // 2)
                sources.load_v(sp, n // GROUP, n % GROUP)
            pairs_of(sp, FIRST + V_TILES + 2, N_KEYS, lambda i, r: experts.load(sp, i, r))

        @block.gpsimd
        def _(pool):
            for n in range(V_TILES):
                experts.take_lo(pool, FIRST + n + 1, 1 - n % 2)
                sources.take_lo(pool, n // GROUP, n // GROUP, n % GROUP)
            pairs_of(pool, FIRST + V_TILES, N_KEYS - 2, lambda i, r: experts.take_lo(pool, i + 1, 1 - r))
            experts.take_lo(pool, N_KEYS - 1, 1)

        @block.tensor
        def _(pe):
            pairs_of(pe, FIRST, N_KEYS, lambda i, r: experts.product(pe, i, r, dots))

        @block.scalar
        def _(act):
            def tile(i, r):
                experts.take_hi(act, i + 1, 1 - r)
                experts.finish(act, i, r, dots)

            for n in range(V_TILES):
                experts.take_hi(act, FIRST + n + 1, 1 - n % 2)
                experts.finish(act, FIRST + n, n % 2, dots)
                sources.take_hi(act, n // GROUP, n // GROUP, n % GROUP)
            pairs_of(act, FIRST + V_TILES, N_KEYS - 2, tile)
            tile(N_KEYS - 2, 0)
            experts.finish(act, N_KEYS - 1, 1, dots)
            for r in range(2):
                act.wait_ge(experts.stored[r], 8 * N_KEYS + 16)


def output(nc, a, sources, x1_scaled, out):
    GROUPS = N_KEYS // GROUP
    BANKS = 8
    with ExitStack() as ctx:
        w, w_hi, w_lo = tiles(
            nc, ctx, ("weights", [P, 2, T], F32), ("weights_hi", [P, 2, GROUP, T], F32R),
            ("weights_lo", [P, 2, GROUP, T], F32R))
        sums, = banks(nc, ctx, ("sums", BANKS))
        w_ready, bank_done, bank_added, steps, tile_normed, out_stored = sems(
            nc, ctx, "w_ready bank_done bank_added w_steps tile_normed out_stored")
        norm = LayerNorm(nc, ctx, "ln2", 2)
        block = ctx.enter_context(nc.Block())

        def groups_of(engine, body):
            with engine.Fori(1, GROUPS // 2) as jj:
                for s in range(2):
                    body(2 * jj + s, s)

        @block.sync
        def _(sp):
            norm.load(sp, a["ln2_g"], a["ln2_b"])

            def group(j, s):
                sp.wait_ge(w_ready, GROUP * (j + 1))
                sources.load_in(sp, j, s)
                for q in range(GROUP):
                    sources.load_v(sp, j, q)
            groups_of(sp, group)
            for t in range(TT):
                sp.wait_ge(tile_normed, t + 1)
                sp.dma_start(out[0].rearrange("(t p) d -> t p d", p=P)[t], x1_scaled[:, t]).then_inc(out_stored, 16)
            sp.wait_ge(out_stored, 16 * TT)

        @block.gpsimd
        def _(pool):
            def group(j, s):
                for q in range(GROUP):
                    sources.take_lo(pool, j, s, q)
            groups_of(pool, group)

        @block.tensor
        def _(pe):
            pe.sem_inc(bank_done, 2 * 8)
            with pe.Fori(0, GROUPS // 2) as jj:
                for s in range(2):
                    j = 2 * jj + s
                    for b in range(8):
                        t, g = b // 2, b % 2
                        pe.wait_ge(bank_added, 8 * j + b + 1)
                        for q in range(GROUP):
                            if b == 0:
                                pe.wait_ge(sources.lo_taken, GROUP * j + q + 1)
                                pe.wait_ge(w_ready, GROUP * j + q + 1 + 2 * GROUP)
                            tokens, columns = slice(P * t, P * t + P), slice(512 * g, 512 * g + 512)
                            to = sums[:, b % BANKS]
                            v_hi, v_lo = sources.hi[:, s, q, columns], sources.lo[:, s, q, columns]
                            nc.tensor.matmul(to, w_hi[:, s, q, tokens], v_hi, start=(q == 0), stop=False)
                            nc.tensor.matmul(to, w_hi[:, s, q, tokens], v_lo, start=False, stop=False)
                            last = nc.tensor.matmul(to, w_lo[:, s, q, tokens], v_hi, start=False,
                                                    stop=(q == GROUP - 1))
                        last.then_inc(bank_done, 1)

        @block.scalar
        def _(act):
            def group(j, s):
                act.wait_ge(bank_done, 8 * j + 8)
                for q in range(GROUP):
                    sources.take_hi(act, j, s, q)
            groups_of(act, group)
            for t in range(TT):
                norm.root(act, t)

        @block.vector
        def _(dve):
            v_ = nc.vector
            chain = Chain(dve, steps)
            dve.sem_inc(w_ready, 2 * GROUP)
            dve.sem_inc(bank_added, BANKS)

            def weigh(j, s, q):
                if q == 0:
                    dve.wait_ge(sources.in_loaded[s], 16 * (j - s) + 32)
                    dve.wait_ge(bank_done, 8 * j + 8)
                chain.step(v_.tensor_tensor(w[:, q % 2].rearrange("p (c t) -> p c t", t=TOK),
                                            sources.gelu[:, s, q].rearrange("p (c t) -> p c t", t=TOK),
                                            sources.gate[:, s, :, TOK * q:TOK * q + TOK], ALU.mult))
                chain.step(v_.tensor_copy(w_hi[:, s, q], w[:, q % 2]))
                v_.tensor_tensor(w_lo[:, s, q], w[:, q % 2], f32(w_hi[:, s, q]), ALU.subtract).then_inc(w_ready, 1)

            def add(j, b):
                t, g = b // 2, b % 2
                to = x1_scaled[:, t, 512 * g:512 * g + 512]
                dve.wait_ge(bank_done, 8 * j + b + 17)
                v_.tensor_tensor(to, to, sums[:, b % BANKS], ALU.add).then_inc(bank_added, 1)

            def group(j, s):
                for b in range(8):
                    add(j, b)
                    if b in (0, 1, 3, 5):
                        weigh(j + 1, 1 - s, (b + 1) // 2)

            for q in range(GROUP):
                weigh(0, 0, q)
            with dve.Fori(0, GROUPS // 2 - 1) as jj:
                chain.round(jj, 2 * GROUP * 2)
                group(2 * jj, 0)
                group(2 * jj + 1, 1)
            chain.done(GROUPS // 2 - 1)
            group(GROUPS - 2, 0)
            norm.begin(dve)
            for t in range(TT):
                for g in range(2):
                    add(GROUPS - 1, 2 * t + g)
                    dve.wait_ge(bank_added, BANKS + 8 * (GROUPS - 1) + 2 * t + g + 1)
                    norm.piece(x1_scaled, t, g)
                norm.variance(t)
                norm.tile(x1_scaled, t).then_inc(tile_normed, 1)


def block_program(nc, a, gelus, gates, out):
    with ExitStack() as whole:
        identity, = tiles(nc, whole, ("identity", [P, P], F32))
        xT = tiles(nc, whole, ("xT_hi", [P, DT, T], F32R), ("xT_lo", [P, DT, T], F32R))
        with ExitStack() as front:
            stream = Stream(nc, front, a["w_chunks"])
            with ExitStack() as merging:
                with ExitStack() as mixing:
                    conv = tiles(nc, mixing, ("conv_hi", [P, DT, T], F32R), ("conv_lo", [P, DT, T], F32R))
                    attn = tiles(nc, mixing, ("attn_hi", [P, DT, T], F32R), ("attn_lo", [P, DT, T], F32R))
                    mixers(nc, a, stream, identity, xT, conv, attn)
                    merged = tiles(nc, merging, ("merged_hi", [P, DT, T], F32R), ("merged_lo", [P, DT, T], F32R),
                                   side="right")
                    merge(nc, a, stream, merged, xT, conv, attn)
                x1, picks = tiles(nc, whole, ("x1", [P, TT, D], F32), ("picks", [P, 3, T], F32))
                norm1(nc, a, stream, identity, merged, x1, xT)
            dotting = whole.enter_context(ExitStack())
            experts = Experts(nc, dotting, a["u_columns"], xT, gelus)
            keys(nc, a, stream, experts, identity, xT, x1, picks)
        gate_matrix(nc, a, experts, picks, gates)
        sources = Sources(nc, whole, a["v_tab"], gelus, gates)
        last_experts(nc, experts, sources)
        dotting.close()
        output(nc, a, sources, x1, out)


def laid_out(i):
    def chunk(w, first, j):
        at = first + CW * j
        return w[0][:, at:at + CW].reshape(DT, P, CW).transpose(1, 0, 2)

    def columns(v):
        v = v.reshape(*v.shape[:-1], -1, P)
        return np.ascontiguousarray(np.moveaxis(v, -1, 0))

    h, b, c, q, k, v, conv_gate, attn_gate = (D * n for n in range(8))
    w = [chunk(i["w_in"], at, j) for j in range(MIX_ROUNDS) for at in (q, k, v, h, b, c)]
    for j in range(MERGE_ROUNDS):
        w += [chunk(i["w_in"], conv_gate, j), chunk(i["w_in"], attn_gate, j), chunk(i["w_conv_out"], 0, j),
              chunk(i["w_attn_out"], 0, j)]
    w += [chunk(i["w_o"], 0, j) for j in range(D // CW)]
    w += [chunk(i["w_pq"], 0, j) for j in range(PK_HEADS)]

    inverse = ROPE_THETA ** (-np.arange(0, ROT_DIM, 2, dtype=np.float32) / ROT_DIM)
    freq, swap = np.zeros((P, 1), np.float32), np.zeros((P, P), np.float32)
    for n in range(ROT_DIM // 2):
        for component in range(2):
            r1, r2 = HD * component + n, HD * component + ROT_DIM // 2 + n
            freq[r1] = freq[r2] = inverse[n]
            swap[r2, r1], swap[r1, r2] = -1.0, 1.0
    below = np.arange(P)[None, :] <= np.arange(P)[:, None]
    kept = ("x", "positions", "lambda_q1", "lambda_k1", "lambda_q2", "lambda_k2", "subln_g", "ln1_g", "ln1_b",
            "ln2_g", "ln2_b", "v_tab")
    return {n: i[n] for n in kept} | {
        "x_columns": np.ascontiguousarray(i["x"][0].T.reshape(DT, P, T).transpose(1, 0, 2)),
        "w_chunks": np.stack(w),
        "conv_w_columns": columns(i["conv_w"][0]),
        "conv_b_columns": columns(i["conv_b"][0]),
        "gate_b_columns": columns(i["gate_b"][0]),
        "sub_keys_columns": np.ascontiguousarray(i["sub_keys"][0].transpose(0, 3, 1, 2)),
        "u_columns": np.ascontiguousarray(i["u_tab"][0].reshape(N_KEYS, P, DT, P).transpose(0, 3, 2, 1)),
        "identity": np.eye(P, dtype=np.float32),
        "freq": freq,
        "swap": swap,
        "mask": np.where(below, 0.0, NEG).astype(np.float32),
        "count": np.ascontiguousarray(np.broadcast_to(np.arange(P, dtype=np.float32), (P, P))),
    }


def kernel(**inputs):
    import concourse.bacc as bacc
    from concourse.bass_utils import run_bass_kernel_spmd

    nc = bacc.Bacc("TRN2", target_bir_lowering=False, num_devices=1)
    arrays = laid_out({n: np.asarray(v) for n, v in inputs.items()})
    a = {n: nc.dram_tensor(f"in_{n}", v.shape, mybir.dt.from_np(v.dtype), kind="ExternalInput").ap()
         for n, v in arrays.items()}
    gelus = nc.dram_tensor("gelus", [N_KEYS, P, T], F32, kind="Internal").ap()
    gates = nc.dram_tensor("gates", [T // TOK, P, N_KEYS * TOK], F32, kind="Internal").ap()
    out = nc.dram_tensor("out", (1, T, D), F32, kind="ExternalOutput").ap()
    block_program(nc, a, gelus, gates, out)
    r = run_bass_kernel_spmd(nc, [{f"in_{n}": v for n, v in arrays.items()}], core_ids=[0])
    return r.results[0]["out"]
```

```python
import math
from contextlib import ExitStack

import concourse.bass as bass
import numpy as np
from concourse import mybir

F32 = mybir.dt.float32
F32R = mybir.dt.float32r
BF16 = mybir.dt.bfloat16
I32 = mybir.dt.int32
U32 = mybir.dt.uint32
ACT = mybir.ActivationFunctionType
ALU = mybir.AluOpType
AX = mybir.AxisListType

P = 128
D = 1024
T = 512
DT = D // P
TT = T // P
HEADS = 8
HD = 64
CW = 256
SLOTS = 2
PK_HEADS = 8
TOPK = 16
N_KEYS = 128
ALPHA = 2 ** 0.25
LAM_INIT = 0.8 - 0.6 * math.exp(0.0)
LN_EPS = 1e-5
SCALE = HD ** -0.5
ROT_DIM = HD // 4
HALF_ROT = ROT_DIM // 2
ROPE_THETA = 500000.0
NEG = -3.0e38
GROUP = 4
TOK = 32
PER_TILE = 8
TILES_BESIDE = 50
TILES_AFTER = 4

MIX_ROUNDS, MIX_CHUNKS = 4, 6
MERGE_ROUNDS, MERGE_CHUNKS = 4, 4
WO_ROUNDS, WO_CHUNKS = 2, 2
PQ_ROUNDS, PQ_CHUNKS = 4, 2
MIX_0 = 0
MERGE_0 = MIX_0 + MIX_ROUNDS * MIX_CHUNKS
WO_0 = MERGE_0 + MERGE_ROUNDS * MERGE_CHUNKS
PQ_0 = WO_0 + WO_ROUNDS * WO_CHUNKS
CHUNKS = PQ_0 + PQ_ROUNDS * PQ_CHUNKS


def f32(ap):
    return ap.bitcast(F32)


def row(ap, at):
    return ap[:, bass.ds(at, 1)].rearrange("p a n -> p (a n)")


class Chain:

    def __init__(self, engine, sem):
        self.engine, self.sem, self.n, self.base = engine, sem, 0, 0

    def step(self, instruction):
        self.n += 1
        instruction.then_inc(self.sem, 1)
        self.engine.wait_ge(self.sem, self.base + self.n)

    def round(self, i, per):
        self.start, self.per = self.base + self.n, per
        self.base, self.n = self.start + i * per, 0

    def done(self, rounds):
        assert self.n == self.per, (self.n, self.per)
        self.base, self.n = self.start + rounds * self.per, 0


class Stream:

    def __init__(self, nc, ctx, source):
        self.nc, self.source = nc, source
        self.raw, self.hi, self.lo = tiles(
            nc, ctx, ("w_raw", [P, SLOTS, DT, CW], F32), ("w_hi", [P, SLOTS, DT, CW], F32R),
            ("w_lo", [P, SLOTS, DT, CW], F32R), side="right")
        self.raw_loaded = [ctx.enter_context(nc.semaphore(f"w_raw_loaded{s}")) for s in range(SLOTS)]
        self.hi_ready = ctx.enter_context(nc.semaphore("w_hi_ready"))
        self.lo_ready = ctx.enter_context(nc.semaphore("w_lo_ready"))
        self.unit_done = ctx.enter_context(nc.semaphore("unit_done"))
        self.bank_free = ctx.enter_context(nc.semaphore("proj_bank_free"))

    def load(self, sp, n, m):
        sp.wait_ge(self.lo_ready, n + 1)
        sp.dma_start(self.raw[:, m], self.source[n]).then_inc(self.raw_loaded[m], 16)

    def load_stage(self, sp, first, last):
        with sp.Fori(0, (min(last, CHUNKS - 2) - first) // 2) as i:
            for m in range(2):
                self.load(sp, 2 * i + first + 2 + m, m)

    def take_hi(self, act, n, m):
        act.wait_ge(self.raw_loaded[m % 2], (n - m % 2) * 8 + 16)
        if not isinstance(n, int) or n >= 2:
            act.wait_ge(self.unit_done, 2 * n - 2)
        self.nc.scalar.activation(self.hi[:, m % 2], self.raw[:, m % 2], ACT.Copy).then_inc(self.hi_ready, 1)

    def take_lo(self, pool, n, m):
        pool.wait_ge(self.hi_ready, n + 1)
        self.nc.gpsimd.tensor_tensor(self.lo[:, m % 2], self.raw[:, m % 2], f32(self.hi[:, m % 2]),
                                     ALU.subtract).then_inc(self.lo_ready, 1)

    def columns(self, pe, out, n, m, half, right_hi, right_lo, before=lambda c: None):
        pe.wait_ge(self.hi_ready, n + 1)
        pe.wait_ge(self.bank_free, 2 * n + half + 1)
        columns = slice(P * half, P * half + P)
        for c in range(DT):
            before(c)
            hi = self.hi[:, m % 2, c, columns]
            self.nc.tensor.matmul(out, hi, right_hi[:, c, :], start=(c == 0), stop=False)
            self.nc.tensor.matmul(out, hi, right_lo[:, c, :], start=False, stop=False)
        pe.wait_ge(self.lo_ready, n + 1 + SLOTS)
        for c in range(DT):
            last = self.nc.tensor.matmul(out, self.lo[:, m % 2, c, columns], right_hi[:, c, :], start=False,
                                         stop=(c == DT - 1))
        last.then_inc(self.unit_done, 1)

    def rows(self, pe, outs, n, m, left_hi, left_lo):
        for half in range(2):
            self.rows_half(pe, outs[half], 2 * n + half, n, m, half, left_hi, left_lo)

    def rows_half(self, pe, out, unit, n, m, half, left_hi, left_lo, between=None):
        pe.wait_ge(self.hi_ready, n + 1)
        pe.wait_ge(self.bank_free, unit + 1)
        for k in range(2):
            tokens = slice(P * (2 * half + k), P * (2 * half + k) + P)
            to = out[:, CW * k:CW * k + CW]
            for c in range(DT):
                hi = self.hi[:, m % 2, c]
                self.nc.tensor.matmul(to, left_hi[:, c, tokens], hi, start=(c == 0), stop=False)
                self.nc.tensor.matmul(to, left_lo[:, c, tokens], hi, start=False, stop=False)
            if k == 0:
                pe.wait_ge(self.lo_ready, n + 1 + SLOTS)
            for c in range(DT):
                last = self.nc.tensor.matmul(to, left_hi[:, c, tokens], self.lo[:, m % 2, c], start=False,
                                             stop=(c == DT - 1))
            if k == 0 and between:
                between()
        last.then_inc(self.unit_done, 1)

    def evacuate(self, act, n, half, to, bank, func=ACT.Copy, **kw):
        act.wait_ge(self.unit_done, 2 * n + half + 1)
        self.nc.scalar.activation(to, bank, func, **kw).then_inc(self.bank_free, 1)

    def wait_out(self, engine, n, half):
        engine.wait_ge(self.bank_free, SLOTS + 2 * n + half + 1)


def take_los(pool, stream, first, rounds, per):
    with pool.Fori(0, rounds) as j:
        for m in range(per):
            stream.take_lo(pool, first + per * j + m + 1, m + 1)


def tiles(nc, ctx, *named, side="left"):
    return [ctx.enter_context(nc.sbuf_tensor(name, shape, dtype, side=side)) for name, shape, dtype in named]


def banks(nc, ctx, *named):
    return [ctx.enter_context(nc.psum_tensor(name, [P, n, 512], F32)) for name, n in named]


def sems(nc, ctx, names):
    return [ctx.enter_context(nc.semaphore(n)) for n in names.split()]


def mixers(nc, a, stream, identity, xT, conv, attn, gate, gate_b):
    MAGIC = 1.5 * 2.0 ** 23
    TURN = 2 * math.pi
    TURN_1, TURN_2 = 6.28125, float(np.float32(TURN - 6.28125))
    TURN_3 = TURN - TURN_1 - TURN_2
    HALF_TURN = float(np.nextafter(np.float32(math.pi), np.float32(0)))
    CONSTS = 11
    with ExitStack() as ctx:
        (raws, cosT, sinT, part, qT, kT, v, diff, diffT, z, y, o, mask, freq,
         conv_w, conv_b, subln, lam_in, lam, stat, o_stat) = tiles(
            nc, ctx, ("raws", [P, 8, T], F32),
            ("cosT", [P, T], F32), ("sinT", [P, T], F32), ("part", [P, T], F32),
            ("qT", [P, 2, T], F32), ("kT", [P, 2, T], F32), ("v", [P, TT, CW], F32),
            ("diff", [P, 10, P], F32), ("diffT", [P, 10, P], F32),
            ("z", [P, T + 2], F32), ("y", [P, T], F32),
            ("o", [P, 2 * TT, P], F32), ("mask", [P, P], F32),
            ("freq", [P, 2], F32), ("conv_w", [P, 3, DT], F32),
            ("conv_b", [P, DT], F32), ("subln", [P, P], F32), ("lam_in", [P, 4, HD], F32),
            ("lam", [P, 8], F32), ("stat", [P, 2, 10], F32), ("o_stat", [P, 3, 2 * TT], F32))
        probs = gate
        position = kT[:, 1].bitcast(I32)
        proj, scores, turn, pv = banks(nc, ctx, ("proj", 2), ("scores", 4), ("turn", 1), ("pv", 1))
        x_loaded = sems(nc, ctx, "x_loaded0 x_loaded1 x_loaded2 x_loaded3")
        (const_loaded, gate_b_loaded, partner_clear, x_hi, x_split, tables_ready, sin_ready, lam_exp, partner_loaded, qk_ready,
         score_done, bias_ready, exp_done, diff_ready, turned, diffT_ready, pv_done, o_ready, sums_ready,
         root_ready, y_ready, y_turned, y_hi, y_split, conv_done, dve_step) = sems(
            nc, ctx, "const_loaded gate_b_loaded partner_clear x_hi x_split tables_ready sin_ready lam_exp partner_loaded "
            "qk_ready score_done bias_ready exp_done diff_ready turned diffT_ready pv_done o_ready "
            "sums_ready root_ready y_ready y_turned y_hi y_split conv_done dve_step")
        partner = raws[:, 6:8]
        squares = gate[:, 1].rearrange("p a (t n) -> p (a t) n", n=P)
        y_turn = turn[:, 0], scores[:, 3]

        def turn_of(tile):
            return (turn if tile % 2 == 0 else pv)[:, 0]

        RAW = {0: 0, 1: 2, 3: 4, 4: 0, 5: 2}
        block = ctx.enter_context(nc.Block())

        @block.sync
        def _(sp):
            sp.dma_start(stream.raw[:, 0], stream.source[0]).then_inc(stream.raw_loaded[0], 16)
            for n, loaded in enumerate(x_loaded):
                sp.dma_start(raws[:, 2 * n:2 * n + 2], a["x_columns"][:, 2 * n:2 * n + 2]).then_inc(loaded, 16)
            sp.dma_start(stream.raw[:, 1], stream.source[1]).then_inc(stream.raw_loaded[1], 16)
            sp.dma_start(gate_b[:], a["gate_b_columns"]).then_inc(gate_b_loaded, 16)
            sp.dma_start(identity[:], a["identity"]).then_inc(const_loaded, 16)
            sp.dma_start(position, a["positions"].broadcast_to([P, T])).then_inc(const_loaded, 16)
            sp.dma_start(freq[:], a["freq"]).then_inc(const_loaded, 16)
            sp.dma_start(mask[:], a["mask"]).then_inc(const_loaded, 16)
            sp.dma_start(subln[:], a["subln_g"].broadcast_to([P, P])).then_inc(const_loaded, 16)
            for n, name in enumerate(("lambda_q1", "lambda_k1", "lambda_q2", "lambda_k2")):
                sp.dma_start(lam_in[:, n], a[name].broadcast_to([P, HD])).then_inc(const_loaded, 16)
            sp.dma_start(conv_b[:], a["conv_b_columns"]).then_inc(const_loaded, 16)
            sp.dma_start(conv_w[:], a["conv_w_columns"]).then_inc(const_loaded, 16)

            def partners(j, m, first):
                if not first:
                    sp.wait_ge(qk_ready, 4 * j + 2 * m)
                stream.wait_out(sp, MIX_0 + MIX_CHUNKS * j + m, 1)
                for component in range(2):
                    for to, source in ((0, HALF_ROT), (HALF_ROT, 0)):
                        to, source = (slice(HD * component + at, HD * component + at + HALF_ROT)
                                      for at in (to, source))
                        sp.dma_start(partner[to], raws[source, RAW[m]:RAW[m] + 2]).then_inc(partner_loaded, 16)

            def round_of(j, first):
                for m in range(MIX_CHUNKS):
                    stream.load(sp, MIX_0 + MIX_CHUNKS * j + m + 2, m % 2)
                    if m in (1, 2):
                        partners(j, m - 1, first and m == 1)

            sp.wait_ge(partner_clear, 1)
            round_of(0, True)
            with sp.Fori(1, MIX_ROUNDS) as j:
                round_of(j, False)
            for m in range(2):
                stream.load(sp, MERGE_0 + 2 + m, m)

        @block.gpsimd
        def _(pool):
            pool.sem_inc(stream.lo_ready, SLOTS)
            stream.take_lo(pool, 0, 0)
            take_los(pool, stream, MIX_0, MIX_ROUNDS, MIX_CHUNKS)
            take_los(pool, stream, MERGE_0, 1, 2)

        @block.tensor
        def _(pe):
            pe.sem_inc(turned, 2)

            def project(j, m, half):
                stream.columns(pe, proj[:, half], MIX_0 + MIX_CHUNKS * j + m, m, half, *xT)

            def score(j, head, tile):
                u = 8 * j + 4 * head + tile
                n = P * (tile + 1)
                pe.wait_ge(qk_ready, 4 * j + 4)
                pe.wait_ge(exp_done, 2 * u)
                if (head, tile) == (0, 1) and (not isinstance(j, int) or j):
                    pe.wait_ge(y_split, 2 * j)
                for c in range(2):
                    rows = slice(HD * c, HD * c + HD)
                    last = nc.tensor.matmul(scores[:, 2 * (tile % 2) + c, 0:n],
                                            qT[rows, head, P * tile:P * tile + P], kT[rows, head, 0:n],
                                            start=True, stop=True)
                last.then_inc(score_done, 1)

            def turn_diff(j, head, tile):
                u = 8 * j + 4 * head + tile
                at = tile * (tile + 1) // 2
                pe.wait_ge(diff_ready, u + 3)
                if tile == 0 and (not isinstance(j, int) or j) and head == 0:
                    pe.wait_ge(y_split, 2 * j)
                pe.wait_ge(diffT_ready, u + 1)
                if tile == 1:
                    pe.wait_ge(o_ready, 2 * j + head)
                for b in range(tile + 1):
                    last = nc.tensor.transpose(turn_of(tile)[:, P * b:P * b + P], diff[:, at + b], identity[:])
                last.then_inc(turned, 1)

            def values(j, head):
                pe.wait_ge(diffT_ready, 8 * j + 4 * head + 6)
                stream.wait_out(pe, MIX_0 + MIX_CHUNKS * j + 2, 1)
                for tile in range(TT):
                    at = tile * (tile + 1) // 2
                    for b in range(tile + 1):
                        last = nc.tensor.matmul(pv[:, 0, P * tile:P * tile + P], diffT[:, at + b],
                                                v[:, b, P * head:P * head + P], start=(b == 0), stop=(b == tile))
                last.then_inc(pv_done, 1)

            def turn_y(j, head):
                pe.wait_ge(y_ready, j + 1)
                pe.wait_ge(diffT_ready, 8 * j + 10)
                for tile in range(TT):
                    last = nc.tensor.transpose(y_turn[head][:, P * tile:P * tile + P], o[:, TT * head + tile],
                                               identity[:])
                last.then_inc(y_turned, 1)

            def round_of(j, first):
                if first:
                    pe.wait_ge(x_split, 1)
                    stream.columns(pe, proj[:, 0], MIX_0, 0, 0, *xT, before=lambda c: pe.wait_ge(x_split, c + 1))
                else:
                    project(j, 0, 0)
                project(j, 0, 1)
                project(j, 1, 0)
                if not first:
                    turn_y(j - 1, 0)
                project(j, 1, 1)
                if not first:
                    turn_y(j - 1, 1)
                stream.rows(pe, [proj[:, half] for half in range(2)], MIX_0 + MIX_CHUNKS * j + 2, 2, *xT)
                project(j, 3, 0)
                score(j, 0, 0)
                score(j, 0, 1)
                project(j, 3, 1)
                score(j, 0, 2)
                score(j, 0, 3)
                project(j, 4, 0)
                turn_diff(j, 0, 0)
                turn_diff(j, 0, 1)
                score(j, 1, 0)
                score(j, 1, 1)
                project(j, 4, 1)
                turn_diff(j, 0, 2)
                turn_diff(j, 0, 3)
                score(j, 1, 2)
                score(j, 1, 3)
                values(j, 0)
                turn_diff(j, 1, 0)
                project(j, 5, 0)
                turn_diff(j, 1, 1)
                turn_diff(j, 1, 2)
                project(j, 5, 1)
                turn_diff(j, 1, 3)
                values(j, 1)

            round_of(0, True)
            with pe.Fori(1, MIX_ROUNDS) as j:
                round_of(j, False)
            for half in range(2):
                stream.columns(pe, proj[:, half], MERGE_0, 0, half, *xT)
            stream.columns(pe, proj[:, 0], MERGE_0 + 1, 1, 0, *xT)
            turn_y(MIX_ROUNDS - 1, 0)
            turn_y(MIX_ROUNDS - 1, 1)
            stream.columns(pe, proj[:, 1], MERGE_0 + 1, 1, 1, *xT)

        @block.scalar
        def _(act):
            act.sem_inc(stream.bank_free, SLOTS)
            act.sem_inc(exp_done, 2)
            act.sem_inc(diffT_ready, 2)
            stream.take_hi(act, 0, 0)
            for c in range(DT):
                act.wait_ge(x_loaded[c // 2], 16)
                nc.scalar.activation(xT[0][:, c], raws[:, c], ACT.Copy).then_inc(x_hi, 1)

            def bring(j, m, half, free, value):
                act.wait_ge(free, value)
                stream.evacuate(act, MIX_0 + MIX_CHUNKS * j + m, half, raws[:, RAW[m] + half], proj[:, half])

            def exponentials(j, head, tile):
                n = P * (tile + 1)
                u = 8 * j + 4 * head + tile
                act.wait_ge(bias_ready, u + 1)
                act.wait_ge(diff_ready, u + 1)
                for c in range(2):
                    nc.scalar.activation(probs[:, tile % 2, c, 0:n], scores[:, 2 * (tile % 2) + c, 0:n], ACT.Exp,
                                         bias=stat[:, tile % 2, 2 + c:3 + c], scale=SCALE,
                                         accum_out=stat[:, tile % 2, 4 + c:5 + c]).then_inc(exp_done, 1)

            def bring_diffT(j, head, tile):
                u = 8 * j + 4 * head + tile
                act.wait_ge(turned, u + 3)
                act.wait_ge(pv_done, 2 * j + head)
                at = tile * (tile + 1) // 2
                nc.scalar.activation(diffT[:, at:at + tile + 1],
                                     turn_of(tile)[:, 0:P * (tile + 1)].rearrange("p (b n) -> p b n", n=P),
                                     ACT.Copy).then_inc(diffT_ready, 1)

            def bring_o(j, head):
                act.wait_ge(pv_done, 2 * j + head + 1)
                act.wait_ge(y_turned, 2 * j)
                nc.scalar.activation(o[:, TT * head:TT * head + TT], pv[:, 0].rearrange("p (t n) -> p t n", n=P),
                                     ACT.Copy).then_inc(o_ready, 1)

            def bring_y_hi(j, head):
                act.wait_ge(y_turned, 2 * j + head + 1)
                nc.scalar.activation(row(attn[0], 2 * j + head), y_turn[head], ACT.Copy).then_inc(y_hi, 1)

            def tables():
                act.wait_ge(tables_ready, 1)
                nc.scalar.activation(sinT[:], sinT[:], ACT.Sin, scale=freq[:, 1:2]).then_inc(sin_ready, 1)
                nc.scalar.activation(cosT[:], cosT[:], ACT.Sin).then_inc(sin_ready, 1)
                nc.scalar.activation(lam[:, 2:4], lam[:, 0:2], ACT.Exp).then_inc(lam_exp, 1)

            def round_of(j, first):
                def ahead(m):
                    stream.take_hi(act, MIX_0 + MIX_CHUNKS * j + m + 1, m + 1)

                for m in range(2):
                    ahead(m)
                    for half in range(2):
                        bring(j, m, half, conv_done, 2 * j)
                        if first and (m, half) == (1, 0):
                            tables()
                        if m == 1 and not first:
                            bring_y_hi(j - 1, half)
                ahead(2)
                act.wait_ge(pv_done, 2 * j)
                for half in range(2):
                    stream.evacuate(act, MIX_0 + MIX_CHUNKS * j + 2, half, v[:, 2 * half:2 * half + 2],
                                    proj[:, half].rearrange("p (k n) -> p k n", k=2))
                ahead(3)
                bring(j, 3, 0, conv_done, 2 * j)
                exponentials(j, 0, 0)
                exponentials(j, 0, 1)
                bring(j, 3, 1, conv_done, 2 * j)
                exponentials(j, 0, 2)
                exponentials(j, 0, 3)
                bring(j, 4, 0, qk_ready, 4 * j + 2)
                bring_diffT(j, 0, 0)
                bring_diffT(j, 0, 1)
                ahead(4)
                exponentials(j, 1, 0)
                exponentials(j, 1, 1)
                bring(j, 4, 1, qk_ready, 4 * j + 2)
                bring_diffT(j, 0, 2)
                bring_diffT(j, 0, 3)
                bring_o(j, 0)
                bring_diffT(j, 1, 0)
                exponentials(j, 1, 2)
                exponentials(j, 1, 3)
                bring(j, 5, 0, qk_ready, 4 * j + 4)
                bring_diffT(j, 1, 1)
                bring_diffT(j, 1, 2)
                ahead(5)
                bring(j, 5, 1, qk_ready, 4 * j + 4)
                bring_diffT(j, 1, 3)
                bring_o(j, 1)
                act.wait_ge(sums_ready, j + 1)
                nc.scalar.activation(o_stat[:, 1], o_stat[:, 0], ACT.Sqrt, bias=lam[:, 7:8],
                                     scale=1.0 / P).then_inc(root_ready, 1)

            round_of(0, True)
            with act.Fori(1, MIX_ROUNDS) as j:
                round_of(j, False)
            act.wait_ge(gate_b_loaded, 16)
            for m in range(2):
                stream.take_hi(act, MERGE_0 + m + 1, m + 1)
                for half in range(2):
                    stream.evacuate(act, MERGE_0 + m, half, gate[:, m, half], proj[:, half], ACT.Sigmoid,
                                    bias=gate_b[:, DT * m + half:DT * m + half + 1])
                    if (m, half) == (1, 0):
                        for head in range(2):
                            bring_y_hi(MIX_ROUNDS - 1, head)

        @block.vector
        def _(dve):
            v_ = nc.vector
            chain = Chain(dve, dve_step)
            step = chain.step
            dve.sem_inc(diff_ready, 2)
            for c in range(DT):
                dve.wait_ge(x_hi, c + 1)
                v_.tensor_tensor(xT[1][:, c], raws[:, c], f32(xT[0][:, c]), ALU.subtract).then_inc(x_split, 1)
            dve.wait_ge(x_split, DT)
            v_.memset(partner, 0.0).then_inc(partner_clear, 1)
            step(v_.memset(z[:, 0:2], 0.0))
            step(v_.memset(lam[:, 7:8], LN_EPS))
            dve.wait_ge(const_loaded, 16 * CONSTS)
            step(v_.tensor_copy(part[:], position))
            step(v_.tensor_scalar(y[:], part[:], freq[:, 0:1], None, ALU.mult))
            for to, quarter in ((sinT, 0.0), (cosT, 0.25)):
                step(v_.tensor_scalar(part[:], y[:], 1 / TURN, quarter, ALU.mult, ALU.add))
                step(v_.tensor_scalar(part[:], part[:], MAGIC, None, ALU.add))
                step(v_.tensor_scalar(part[:], part[:], -MAGIC, None, ALU.add))
                step(v_.scalar_tensor_tensor(to[:], part[:], -TURN_1, y[:], ALU.mult, ALU.add))
                step(v_.scalar_tensor_tensor(to[:], part[:], -TURN_2, to[:], ALU.mult, ALU.add))
                step(v_.scalar_tensor_tensor(to[:], part[:], -TURN_3, to[:], ALU.mult, ALU.add))
                step(v_.tensor_scalar(to[:], to[:], quarter * TURN, None, ALU.add))
                step(v_.tensor_scalar(to[:], to[:], HALF_TURN, -HALF_TURN, ALU.min, ALU.max))
            for n in range(2):
                step(v_.tensor_tensor(part[:, 0:HD], lam_in[:, 2 * n], lam_in[:, 2 * n + 1], ALU.mult))
                last = v_.tensor_reduce(lam[:, n:n + 1], part[:, 0:HD], AX.X, ALU.add)
                if n == 0:
                    step(last)
            last.then_inc(tables_ready, 1)
            dve.wait_ge(lam_exp, 1)
            step(v_.tensor_tensor(lam[:, 4:5], lam[:, 3:4], lam[:, 2:3], ALU.subtract))
            step(v_.tensor_scalar(lam[:, 5:6], lam[:, 4:5], -LAM_INIT, None, ALU.add))
            dve.wait_ge(sin_ready, 2)

            def rotate(j, m, half, to):
                dve.wait_ge(partner_loaded, 64 * (2 * j + m) + 64)
                dve.wait_ge(score_done, 8 * j)
                if not isinstance(j, int) or 2 * m + half:
                    dve.wait_ge(qk_ready, 4 * j + 2 * m + half)
                step(v_.tensor_tensor(part[:], raws[:, RAW[m] + half], cosT[:], ALU.mult))
                step(v_.tensor_tensor(y[:], partner[:, half], sinT[:], ALU.mult))
                v_.tensor_tensor(to[:, half], part[:], y[:], ALU.add).then_inc(qk_ready, 1)

            def maximum(j, head, tile):
                u = 8 * j + 4 * head + tile
                both = slice(2 * (tile % 2), 2 * (tile % 2) + 2)
                dve.wait_ge(score_done, u + 1)
                diagonal = scores[:, both, P * tile:P * tile + P]
                step(v_.tensor_tensor(diagonal, diagonal, mask[:, None, :].broadcast_to([P, 2, P]), ALU.add))
                step(v_.tensor_reduce(stat[:, tile % 2, 0:2], scores[:, both, 0:P * (tile + 1)], AX.X, ALU.max))
                v_.tensor_scalar(stat[:, tile % 2, 2:4], stat[:, tile % 2, 0:2], -SCALE, None,
                                 ALU.mult).then_inc(bias_ready, 1)

            def difference(j, head, tile):
                u = 8 * j + 4 * head + tile
                n = P * (tile + 1)
                s = tile % 2
                dve.wait_ge(exp_done, 2 * u + 4)
                if head or not isinstance(j, int) or j:
                    dve.wait_ge(turned, u - 1)
                part_of = diff[:, tile * (tile + 1) // 2:(tile + 1) * (tile + 2) // 2].rearrange("p b n -> p (b n)")
                step(v_.reciprocal(stat[:, s, 6:8], stat[:, s, 4:6]))
                step(v_.tensor_tensor(stat[:, s, 8:9], stat[:, s, 7:8], lam[:, 5:6], ALU.mult))
                step(v_.tensor_scalar(part_of, probs[:, s, 1, 0:n], stat[:, s, 8:9], None, ALU.mult))
                v_.scalar_tensor_tensor(part_of, probs[:, s, 0, 0:n], stat[:, s, 6:7], part_of, ALU.mult,
                                        ALU.add).then_inc(diff_ready, 1)

            def short_conv(j, half):
                at = 2 * j + half
                stream.wait_out(dve, MIX_0 + MIX_CHUNKS * j + 5, half)
                step(v_.tensor_tensor(z[:, 2:T + 2], raws[:, RAW[5] + half], raws[:, RAW[3] + half], ALU.mult))
                step(v_.tensor_scalar(y[:], z[:, 2:T + 2], conv_w[:, 2, bass.ds(at, 1)], conv_b[:, bass.ds(at, 1)],
                                      ALU.mult, ALU.add))
                step(v_.scalar_tensor_tensor(y[:], z[:, 1:T + 1], conv_w[:, 1, bass.ds(at, 1)], y[:], ALU.mult,
                                             ALU.add))
                step(v_.scalar_tensor_tensor(y[:], z[:, 0:T], conv_w[:, 0, bass.ds(at, 1)], y[:], ALU.mult, ALU.add))
                step(v_.tensor_tensor(y[:], y[:], raws[:, RAW[4] + half], ALU.mult))
                hi, lo = row(conv[0], at), row(conv[1], at)
                step(v_.tensor_copy(hi, y[:]))
                v_.tensor_tensor(lo, y[:], f32(hi), ALU.subtract).then_inc(conv_done, 1)

            def take_y_lo(j, head):
                dve.wait_ge(y_hi, 2 * j + head + 1)
                at = 2 * j + head
                v_.tensor_tensor(row(attn[1], at), y_turn[head], f32(row(attn[0], at)),
                                 ALU.subtract).then_inc(y_split, 1)

            def round_of(j, first):
                if not first:
                    take_y_lo(j - 1, 0)
                for half in range(2):
                    rotate(j, 0, half, qT)
                if not first:
                    take_y_lo(j - 1, 1)
                for half in range(2):
                    rotate(j, 1, half, kT)
                for head in range(2):
                    for pair in range(2):
                        for tile in (2 * pair, 2 * pair + 1):
                            maximum(j, head, tile)
                        for tile in (2 * pair, 2 * pair + 1):
                            difference(j, head, tile)
                short_conv(j, 0)
                short_conv(j, 1)
                dve.wait_ge(o_ready, 2 * j + 2)
                step(v_.tensor_tensor(squares, o[:], o[:], ALU.mult))
                v_.tensor_reduce(o_stat[:, 0], squares, AX.X, ALU.add).then_inc(sums_ready, 1)
                dve.wait_ge(root_ready, j + 1)
                step(v_.reciprocal(o_stat[:, 2], o_stat[:, 1]))
                step(v_.scalar_tensor_tensor(o[:], o[:], 1.0 - LAM_INIT,
                                             o_stat[:, 2, :, None].broadcast_to([P, 2 * TT, P]), ALU.mult, ALU.mult))
                v_.tensor_tensor(o[:], o[:], subln[:, None, :].broadcast_to([P, 2 * TT, P]),
                                 ALU.mult).then_inc(y_ready, 1)

            before = chain.n
            round_of(0, True)
            per = chain.n - before
            with dve.Fori(1, MIX_ROUNDS) as j:
                chain.round(j - 1, per)
                round_of(j, False)
            chain.done(MIX_ROUNDS - 1)
            for head in range(2):
                take_y_lo(MIX_ROUNDS - 1, head)


def merge(nc, a, stream, merged, xT, conv, attn, gate, gate_b):
    with ExitStack() as ctx:
        branch, total = tiles(nc, ctx, ("branch", [P, 2, 2, T], F32), ("total", [P, 2, T], F32))
        proj, = banks(nc, ctx, ("proj_merge", 2))
        half_merged, step_done = sems(nc, ctx, "half_merged merge_step")
        block = ctx.enter_context(nc.Block())
        FIRST = MERGE_0 + 2

        @block.sync
        def _(sp):
            stream.load_stage(sp, FIRST, WO_0)

        @block.gpsimd
        def _(pool):
            take_los(pool, stream, FIRST, MERGE_ROUNDS - 1, MERGE_CHUNKS)
            take_los(pool, stream, WO_0 - 2, 1, 2)

        @block.tensor
        def _(pe):
            def chunk(j, m, right):
                for half in range(2):
                    stream.columns(pe, proj[:, half], FIRST + MERGE_CHUNKS * j + m, m, half, *right)

            with pe.Fori(0, MERGE_ROUNDS - 1) as j:
                for m, right in enumerate((conv, attn, xT, xT)):
                    chunk(j, m, right)
            for m, right in enumerate((conv, attn)):
                chunk(MERGE_ROUNDS - 1, m, right)

        @block.scalar
        def _(act):
            def branches(j):
                for m in range(2):
                    n = FIRST + MERGE_CHUNKS * j + m
                    stream.take_hi(act, n + 1, m + 1)
                    for half in range(2):
                        if not isinstance(j, int) or j:
                            act.wait_ge(half_merged, 2 * j + half - 1)
                        stream.evacuate(act, n, half, branch[:, m, half], proj[:, half])

            def gates(j):
                for m in range(2, 4):
                    n = FIRST + MERGE_CHUNKS * j + m
                    stream.take_hi(act, n + 1, m + 1)
                    for half in range(2):
                        act.wait_ge(half_merged, 2 * j + half + 1)
                        stream.evacuate(act, n, half, gate[:, m - 2, half], proj[:, half], ACT.Sigmoid,
                                        bias=gate_b[:, bass.ds(2 * j + 2 + DT * (m - 2) + half, 1)])

            branches(0)
            gates(0)
            with act.Fori(1, MERGE_ROUNDS - 1) as j:
                branches(j)
                gates(j)
            branches(MERGE_ROUNDS - 1)

        @block.vector
        def _(dve):
            v_ = nc.vector
            chain = Chain(dve, step_done)
            with dve.Fori(0, MERGE_ROUNDS) as j:
                chain.round(j, 2 * 4)
                for half in range(2):
                    n = FIRST + MERGE_CHUNKS * j
                    at = 2 * j + half
                    hi, lo = row(merged[0], at), row(merged[1], at)
                    stream.wait_out(dve, n, half)
                    chain.step(v_.tensor_tensor(branch[:, 0, half], branch[:, 0, half], gate[:, 0, half], ALU.mult))
                    stream.wait_out(dve, n + 1, half)
                    chain.step(v_.tensor_tensor(branch[:, 1, half], branch[:, 1, half], gate[:, 1, half], ALU.mult))
                    chain.step(v_.tensor_tensor(total[:, half], branch[:, 0, half], branch[:, 1, half], ALU.add))
                    chain.step(v_.tensor_copy(hi, total[:, half]))
                    v_.tensor_tensor(lo, total[:, half], f32(hi), ALU.subtract).then_inc(half_merged, 1)
            chain.done(MERGE_ROUNDS)


class LayerNorm:

    def __init__(self, nc, ctx, name, pieces):
        self.nc, self.width = nc, D // pieces
        self.stats, self.mv, self.gain, self.shift, self.eps = tiles(
            nc, ctx, (f"{name}_stats", [P, TT, pieces, 6], F32), (f"{name}_mv", [P, TT, 4], F32),
            (f"{name}_gain", [P, D], F32), (f"{name}_shift", [P, D], F32), (f"{name}_eps", [P, 1], F32))
        self.loaded, self.var_ready, self.centred, self.root_ready, self.steps = sems(
            nc, ctx, f"{name}_loaded {name}_var_ready {name}_centred {name}_root_ready {name}_steps")

    def load(self, sp, gain, shift):
        sp.dma_start(self.gain[:], gain.broadcast_to([P, D])).then_inc(self.loaded, 16)
        sp.dma_start(self.shift[:], shift.broadcast_to([P, D])).then_inc(self.loaded, 16)

    def root(self, act, t):
        act.wait_ge(self.var_ready, t + 1)
        self.nc.scalar.activation(self.mv[:, t, 2:3], self.mv[:, t, 1:2], ACT.Sqrt,
                                  bias=self.eps[:, 0:1]).then_inc(self.root_ready, 1)

    def begin(self, dve):
        self.dve, self.chain = dve, Chain(dve, self.steps)
        self.chain.step(self.nc.vector.memset(self.eps[:], LN_EPS))
        dve.wait_ge(self.loaded, 32)

    def piece(self, z, t, g):
        self.chain.step(self.nc.vector.bn_stats(self.stats[:, t, g], z[:, t, self.width * g:self.width * g + self.width]))

    def variance(self, t):
        self.nc.vector.bn_aggr(self.mv[:, t, 0:2], self.stats[:, t].rearrange("p a b -> p (a b)")) \
            .then_inc(self.var_ready, 1)

    def centre(self, z, t):
        self.dve.wait_ge(self.var_ready, t + 1)
        self.nc.vector.scalar_tensor_tensor(z[:, t], z[:, t], self.mv[:, t, 0:1], self.gain[:], ALU.subtract,
                                            ALU.mult).then_inc(self.centred, 1)

    def finish(self, z, t, parts, done):
        self.dve.wait_ge(self.root_ready, t + 1)
        self.chain.step(self.nc.vector.reciprocal(self.mv[:, t, 3:4], self.mv[:, t, 2:3]))
        self.dve.wait_ge(self.centred, t + 1)
        for g in range(parts):
            at = slice(D // parts * g, D // parts * g + D // parts)
            self.nc.vector.scalar_tensor_tensor(z[:, t, at], z[:, t, at], self.mv[:, t, 3:4], self.shift[:, at],
                                                ALU.mult, ALU.add).then_inc(done, 1)


def norm1(nc, a, stream, identity, merged, x1, xT):
    with ExitStack() as ctx:
        proj, turn = banks(nc, ctx, ("proj_o", 2), ("turn_x1", 6))
        turns = [turn[:, u] for u in range(6)] + [proj[:, u] for u in range(2)]
        x_loaded, normed, x1_turned, x1_hi = sems(nc, ctx, "x_rows_loaded normed x1_turned x1_hi")
        chunks = WO_ROUNDS * WO_CHUNKS
        norm = LayerNorm(nc, ctx, "ln1", chunks)
        units = [(n, half) for n in range(chunks - 2) for half in range(2)] + \
                [(n, half) for half in range(2) for n in (chunks - 2, chunks - 1)]
        block = ctx.enter_context(nc.Block())

        @block.sync
        def _(sp):
            sp.dma_start(x1[:], a["x"][0].rearrange("(t p) d -> p t d", p=P)).then_inc(x_loaded, 16)
            norm.load(sp, a["ln1_g"], a["ln1_b"])
            stream.load_stage(sp, WO_0, PQ_0)

        @block.gpsimd
        def _(pool):
            take_los(pool, stream, WO_0, WO_ROUNDS, WO_CHUNKS)

        @block.tensor
        def _(pe):
            def turn_x1(tiles_of_tokens):
                for t in tiles_of_tokens:
                    pe.wait_ge(normed, t + 1)
                    for g in range(2):
                        for c in range(4):
                            d = 4 * g + c
                            last = nc.tensor.transpose(turns[2 * t + g][:, P * c:P * c + P],
                                                       x1[:, t, P * d:P * d + P], identity[:])
                        last.then_inc(x1_turned, 1)

            for u, (n, half) in enumerate(units):
                stream.rows_half(pe, proj[:, u % 2], 2 * WO_0 + u, WO_0 + n, n, half, *merged,
                                 between=(lambda: turn_x1((0, 1))) if u == len(units) - 1 else None)
            turn_x1((2, 3))

        @block.scalar
        def _(act):
            def halves_of(t):
                for u in (2 * t, 2 * t + 1):
                    g = u % 2
                    act.wait_ge(x1_turned, u + 1)
                    nc.scalar.activation(xT[0][:, 4 * g:4 * g + 4, P * t:P * t + P],
                                         turns[u].rearrange("p (c n) -> p c n", c=4), ACT.Copy).then_inc(x1_hi, 1)

            for n in range(chunks - 1):
                stream.take_hi(act, WO_0 + n + 1, n + 1)
            for t in range(2):
                norm.root(act, t)
            act.wait_ge(stream.unit_done, 2 * WO_0 + 2 * chunks - 1)
            stream.take_hi(act, WO_0 + chunks, chunks)
            for t in range(2):
                halves_of(t)
            for t in range(2, TT):
                norm.root(act, t)
            for t in range(2, TT):
                halves_of(t)

        @block.vector
        def _(dve):
            v_ = nc.vector
            norm.begin(dve)
            dve.wait_ge(x_loaded, 16)
            def residual(u):
                n, half = units[u]
                dve.wait_ge(stream.unit_done, 2 * WO_0 + u + 1)
                at = (slice(None), slice(2 * half, 2 * half + 2), slice(CW * n, CW * n + CW))
                v_.scalar_tensor_tensor(x1[at], x1[at], ALPHA, proj[:, u % 2].rearrange("p (k n) -> p k n", k=2),
                                        ALU.mult, ALU.add).then_inc(stream.bank_free, 1)
                dve.wait_ge(stream.bank_free, SLOTS + 2 * WO_0 + u + 1)
                for t in (2 * half, 2 * half + 1):
                    norm.piece(x1, t, n)

            def normed_half(half):
                for t in (2 * half, 2 * half + 1):
                    norm.variance(t)
                for t in (2 * half, 2 * half + 1):
                    norm.centre(x1, t)
                for t in (2 * half, 2 * half + 1):
                    norm.finish(x1, t, 1, normed)

            def rests(half):
                for u in range(4 * half, 4 * half + 4):
                    t, g = u // 2, u % 2
                    dve.wait_ge(x1_hi, u + 1)
                    at = (slice(None), slice(4 * g, 4 * g + 4), slice(P * t, P * t + P))
                    v_.tensor_tensor(xT[1][at], turns[u].rearrange("p (c n) -> p c n", c=4), f32(xT[0][at]),
                                     ALU.subtract)

            for u in range(len(units) - 2):
                residual(u)
            normed_half(0)
            residual(len(units) - 2)
            rests(0)
            residual(len(units) - 1)
            normed_half(1)
            rests(1)


class Experts:

    def __init__(self, nc, ctx, longer, source, xT, gelus):
        self.nc, self.source, self.xT, self.gelus = nc, source, xT, gelus
        self.gelu, = tiles(nc, longer, ("gelu", [P, 2, T], F32))
        self.raw, self.hi, self.lo = tiles(
            nc, ctx, ("u_raw", [P, 2, DT, P], F32), ("u_hi", [P, 2, DT, P], F32R), ("u_lo", [P, 2, DT, P], F32R))
        self.loaded = sems(nc, ctx, "u_loaded0 u_loaded1")
        self.stored = sems(nc, ctx, "gelu_stored0 gelu_stored1")
        self.hi_taken, self.lo_taken, self.dot_done, self.gelu_done = sems(
            nc, ctx, "u_hi_taken u_lo_taken dot_done gelu_done")

    def load(self, sp, i, r):
        sp.wait_ge(self.lo_taken, i + 1)
        sp.dma_start(self.raw[:, r], self.source[i]).then_inc(self.loaded[r], 16)

    def take_hi(self, act, i, r):
        act.wait_ge(self.loaded[r], 8 * (i - r) + 16)
        act.wait_ge(self.dot_done, i + 1)
        self.nc.scalar.activation(self.hi[:, r], self.raw[:, r], ACT.Copy).then_inc(self.hi_taken, 1)

    def take_lo(self, pool, i, r):
        pool.wait_ge(self.hi_taken, i + 1)
        self.nc.gpsimd.tensor_tensor(self.lo[:, r], self.raw[:, r], f32(self.hi[:, r]),
                                     ALU.subtract).then_inc(self.lo_taken, 1)

    def product(self, pe, i, r, dots):
        hi, lo, right = self.hi[:, r], self.lo[:, r], self.xT
        pe.wait_ge(self.hi_taken, i + 1)
        pe.wait_ge(self.gelu_done, i + 1)
        for d in range(DT):
            self.nc.tensor.matmul(dots[:, r], hi[:, d], right[0][:, d], start=(d == 0), stop=False)
            self.nc.tensor.matmul(dots[:, r], hi[:, d], right[1][:, d], start=False, stop=False)
        pe.wait_ge(self.lo_taken, i + 3)
        for d in range(DT):
            last = self.nc.tensor.matmul(dots[:, r], lo[:, d], right[0][:, d], start=False, stop=(d == DT - 1))
        last.then_inc(self.dot_done, 1)

    def finish(self, act, i, r, dots):
        act.wait_ge(self.dot_done, i + 3)
        act.wait_ge(self.stored[r], 8 * (i - r) + 16)
        self.nc.scalar.activation(self.gelu[:, r], dots[:, r], ACT.Gelu).then_inc(self.gelu_done, 1)
        act.wait_ge(self.gelu_done, i + 3)
        act.dma_start(self.gelus[i], self.gelu[:, r]).then_inc(self.stored[r], 16)


def pairs_of(engine, first, last, body):
    with engine.Fori(first // 2, last // 2) as k:
        for r in range(2):
            body(2 * k + r, r)


def keys(nc, a, stream, experts, identity, xT, x1, numbers, parts):
    with ExitStack() as ctx:
        (key_rows, q, s, s_rest, best, best_at, best_at_f, pair, pair_rest, top, top_at, first, second, number,
         one_hot, count16, packed, sums, weight, whole) = tiles(
            nc, ctx,
            ("sub_keys", [P, 2, 2, N_KEYS], F32), ("q", [P, 2, T], F32), ("s", [P, PK_HEADS, TT, 2, N_KEYS], F32),
            ("s_rest", [P, TT * 2, N_KEYS], F32), ("best", [P, TT, 2, TOPK], F32),
            ("best_at", [P, TT, 2, TOPK], U32), ("best_at_f", [P, TT, 2, TOPK], F32),
            ("pair", [P, TT, TOPK * TOPK], F32), ("pair_rest", [P, TT, TOPK * TOPK], F32),
            ("top", [P, TT, TOPK], F32), ("top_at", [P, TT, TOPK], U32), ("first_at", [P, TT, TOPK], U32),
            ("second_at", [P, TT, TOPK], U32), ("number", [P, TT, TOPK], F32),
            ("one_hot", [P, TT, TOPK, TOPK], F32), ("count16", [P, TOPK], F32),
            ("packed", [P, 3, TT, PK_HEADS, TOPK], F32), ("weight_sums", [P, 2, TT, PK_HEADS], F32),
            ("weight", [P, TT, PK_HEADS, TOPK], F32), ("whole_weight", [P, T], F32))
        proj, score, dots = banks(nc, ctx, ("proj_q", 2), ("score_k", 2), ("dots_keys", 2))
        turn = [proj[:, 0], proj[:, 1], score[:, 0]]
        k_loaded = sems(nc, ctx, "sub_keys_loaded0 sub_keys_loaded1")
        (x1_scaled, c_loaded, q_scored, s_out, exp_asked, exp_done, all_packed, packed_turned, picks_out,
         steps) = sems(nc, ctx, "x1_scaled_done count16_loaded q_scored s_out k_exp_asked k_exp_done all_packed "
                       "packed_turned picks_out k_steps")
        block = ctx.enter_context(nc.Block())

        @block.sync
        def _(sp):
            sp.dma_start(count16[:], a["count"][:, 0:TOPK]).then_inc(c_loaded, 16)
            for m in range(2):
                sp.dma_start(key_rows[:, m], a["sub_keys_columns"][m]).then_inc(k_loaded[m], 16)
            for h in range(PK_HEADS - 2):
                m = h % 2
                stream.load(sp, PQ_0 + h + 2, m)
                sp.wait_ge(q_scored, 2 * h + 2)
                sp.dma_start(key_rows[:, m], a["sub_keys_columns"][h + 2]).then_inc(k_loaded[m], 16)
            pairs_of(sp, 0, TILES_BESIDE + 2, lambda i, r: experts.load(sp, i, r))

        @block.gpsimd
        def _(pool):
            pool.sem_inc(experts.lo_taken, 2)
            for n in range(1, PK_HEADS):
                stream.take_lo(pool, PQ_0 + n, n)
                if n <= TT:
                    nc.gpsimd.tensor_scalar(x1[:, n - 1], x1[:, n - 1], ALPHA, None,
                                            ALU.mult).then_inc(x1_scaled, 1)
            pool.wait_ge(x1_scaled, TT)
            experts.take_lo(pool, 0, 0)
            with pool.Fori(0, TILES_BESIDE // 2) as k:
                for r in range(2):
                    experts.take_lo(pool, 2 * k + r + 1, 1 - r)

        @block.tensor
        def _(pe):
            pe.sem_inc(experts.dot_done, 2)

            def query(h, m, half):
                stream.columns(pe, proj[:, half], PQ_0 + h, m, half, *xT)

            def scores(h, m, half):
                if half == 0:
                    pe.wait_ge(k_loaded[m], 8 * (h - m) + 16)
                stream.wait_out(pe, PQ_0 + h, half)
                pe.wait_ge(s_out, 2 * h + half + 1)
                for t in range(TT):
                    last = nc.tensor.matmul(score[:, half, P * t:P * t + P], q[:, half, P * t:P * t + P],
                                            key_rows[:, m, half], start=True, stop=True)
                last.then_inc(q_scored, 1)

            def head(h, m, first):
                query(h, m, 0)
                if not first:
                    scores(h - 1, 1 - m, 1)
                query(h, m, 1)
                scores(h, m, 0)

            head(0, 0, True)
            head(1, 1, False)
            with pe.Fori(1, PQ_ROUNDS) as j:
                for m in range(2):
                    head(2 * j + m, m, False)
            scores(PK_HEADS - 1, 1, 1)
            pairs_of(pe, 0, TILES_BESIDE - 2, lambda i, r: experts.product(pe, i, r, dots))
            pe.wait_ge(s_out, 2 * PK_HEADS + 1)
            pe.wait_ge(all_packed, 1)
            for n in range(3):
                for t in range(TT):
                    last = nc.tensor.transpose(turn[n][:, P * t:P * t + P],
                                               packed[:, n, t].rearrange("p h k -> p (h k)"), identity[:])
            last.then_inc(packed_turned, 1)
            for i in range(TILES_BESIDE - 2, TILES_BESIDE):
                experts.product(pe, i, i % 2, dots)

        @block.scalar
        def _(act):
            act.sem_inc(s_out, 1)
            act.sem_inc(experts.gelu_done, 2)
            for r in range(2):
                act.sem_inc(experts.stored[r], 16)

            def bring_q(h, half):
                if not isinstance(h, int) or h:
                    act.wait_ge(q_scored, 2 * h + half - 1)
                stream.evacuate(act, PQ_0 + h, half, q[:, half], proj[:, half])

            def bring_s(h, half):
                act.wait_ge(q_scored, 2 * h + half + 1)
                nc.scalar.activation(s_of(h)[:, :, half], score[:, half].rearrange("p (t n) -> p t n", t=TT),
                                     ACT.Copy).then_inc(s_out, 1)

            def head(j, m, ahead, first=False):
                h = 2 * j + m
                if ahead:
                    stream.take_hi(act, PQ_0 + h + 1, m + 1)
                bring_q(h, 0)
                if not first:
                    bring_s(h - 1, 1)
                bring_q(h, 1)
                bring_s(h, 0)

            def s_of(h):
                return s[:, h] if isinstance(h, int) else \
                    s[:, bass.ds(h, 1)].rearrange("p h t c n -> p (h t) c n")

            def tile(i, r):
                experts.take_hi(act, i + 1, 1 - r)
                experts.finish(act, i, r, dots)

            head(0, 0, True, first=True)
            head(0, 1, True)
            with act.Fori(1, PQ_ROUNDS - 1) as j:
                for m in range(2):
                    head(j, m, True)
            head(PQ_ROUNDS - 1, 0, True)
            experts.take_hi(act, 0, 0)
            head(PQ_ROUNDS - 1, 1, False)
            bring_s(PK_HEADS - 1, 1)
            pairs_of(act, 0, TILES_BESIDE - 4, tile)
            act.wait_ge(exp_asked, 1)
            nc.scalar.activation(weight[:], packed[:, 2], ACT.Exp).then_inc(exp_done, 1)
            pairs_of(act, TILES_BESIDE - 4, TILES_BESIDE - 2, tile)
            act.wait_ge(packed_turned, 1)
            for to, n in ((whole[:], 2), (numbers[:, 0], 0), (numbers[:, 1], 1)):
                nc.scalar.activation(to, turn[n], ACT.Copy).then_inc(picks_out, 1)
            pairs_of(act, TILES_BESIDE - 2, TILES_BESIDE, tile)
            act.wait_ge(picks_out, 3)

        @block.vector
        def _(dve):
            v_ = nc.vector
            chain = Chain(dve, steps)
            step = chain.step
            dve.wait_ge(c_loaded, 16)

            def top16(values, rest, out, out_at):
                step(v_.max(out[:, 0:8], values))
                step(v_.match_replace(rest, out[:, 0:8], values, NEG))
                step(v_.max(out[:, 8:16], rest))
                step(v_.max_index(out_at[:, 0:8], out[:, 0:8], values))
                step(v_.max_index(out_at[:, 8:16], out[:, 8:16], rest))

            for h in range(PK_HEADS):
                dve.wait_ge(s_out, 2 * h + 3)
                for t in range(TT):
                    for half in range(2):
                        top16(s[:, h, t, half], s_rest[:, 2 * t + half], best[:, t, half], best_at[:, t, half])
                step(v_.tensor_copy(best_at_f[:], best_at[:]))
                for t in range(TT):
                    step(v_.tensor_tensor(pair[:, t].rearrange("p (a b) -> p a b", a=TOPK),
                                          best[:, t, 0, :, None].broadcast_to([P, TOPK, TOPK]),
                                          best[:, t, 1, None, :].broadcast_to([P, TOPK, TOPK]), ALU.add))
                for t in range(TT):
                    top16(pair[:, t], pair_rest[:, t], top[:, t], top_at[:, t])
                step(v_.tensor_tensor(packed[:, 2, :, h], top[:], top[:, :, 0:1].broadcast_to([P, TT, TOPK]),
                                      ALU.subtract))
                if h == PK_HEADS - 1:
                    dve.sem_inc(exp_asked, 1)
                step(v_.tensor_scalar(first[:], top_at[:], 4, None, ALU.logical_shift_right))
                step(v_.tensor_scalar(second[:], top_at[:], 15, None, ALU.bitwise_and))
                for n, at in enumerate((first, second)):
                    step(v_.tensor_copy(number[:], at[:]))
                    step(v_.tensor_tensor(one_hot[:].rearrange("p t a b -> p (t a) b"),
                                          number[:].rearrange("p t a -> p (t a)")[:, :, None]
                                          .broadcast_to([P, TT * TOPK, TOPK]),
                                          count16[:, None, :].broadcast_to([P, TT * TOPK, TOPK]), ALU.is_equal))
                    step(v_.tensor_tensor(one_hot[:], one_hot[:], best_at_f[:, :, n, None, :]
                                          .broadcast_to([P, TT, TOPK, TOPK]), ALU.mult))
                    step(v_.tensor_reduce(packed[:, n, :, h], one_hot[:], AX.X, ALU.add))
            dve.wait_ge(exp_done, 1)
            step(v_.tensor_reduce(sums[:, 0], weight[:], AX.X, ALU.add))
            step(v_.reciprocal(sums[:, 1], sums[:, 0]))
            v_.tensor_tensor(packed[:, 2], weight[:], sums[:, 1, :, :, None]
                             .broadcast_to([P, TT, PK_HEADS, TOPK]), ALU.mult).then_inc(all_packed, 1)
            dve.wait_ge(picks_out, 1)
            step(v_.tensor_copy(parts[0][:], whole[:]))
            step(v_.tensor_tensor(parts[1][:], whole[:], f32(parts[0][:]), ALU.subtract))


def gate_matrix(nc, a, experts, numbers, parts, gates):
    TILES = T // PER_TILE
    PER_CHUNK = TOK // PER_TILE
    with ExitStack() as ctx:
        left, right, hot, gate, count, low = tiles(
            nc, ctx, ("left", [P, 2, PER_TILE, P], F32R), ("right", [P, 2, PER_TILE, 2, P], F32R),
            ("hot", [P, 2, PER_TILE, P], F32), ("gate_chunk", [P, 2, N_KEYS, TOK], F32), ("count", [P, N_KEYS], F32),
            ("low_half", [P, N_KEYS, PER_TILE], F32))
        dots, built = banks(nc, ctx, ("dots_gate", 2), ("built", 4))
        flushed = sems(nc, ctx, "gate_stored0 gate_stored1")
        count_loaded, hot_ready, high_ready, low_ready, built_done, low_out, built_out = sems(
            nc, ctx, "count_loaded hot_ready high_ready low_ready built_done low_out built_out")
        AFTER = TILES_BESIDE + TILES
        END = AFTER + TILES_AFTER
        block = ctx.enter_context(nc.Block())

        def built_of(part):
            return built.rearrange("p b (t q n) -> p (b t) q n", t=2, q=2)[:, :, part].rearrange("p t n -> p n t")

        def one_hots(n, m):
            at = bass.ds(PER_TILE * n, PER_TILE)
            return (count[:, None, :].broadcast_to([P, PER_TILE, P]),
                    numbers[:, m, at][:, :, None].broadcast_to([P, PER_TILE, P]))

        def weights(n, part):
            weight = (f32(parts[0]) if part == 0 else parts[1])[:, bass.ds(PER_TILE * n, PER_TILE)]
            return weight[:, :, None].broadcast_to([P, PER_TILE, P])

        @block.sync
        def _(sp):
            sp.dma_start(count[:], a["count"]).then_inc(count_loaded, 16)
            pairs_of(sp, TILES_BESIDE + 2, END + 2, lambda i, r: experts.load(sp, i, r))

        @block.gpsimd
        def _(pool):
            with pool.Fori(0, TILES // 2) as k:
                for r in range(2):
                    n = 2 * k + r
                    experts.take_lo(pool, TILES_BESIDE + n + 1, 1 - r)
                    pool.wait_ge(hot_ready, n + 1)
                    nc.gpsimd.tensor_tensor(right[:, r, :, 1], hot[:, r], weights(n, 1),
                                            ALU.mult).then_inc(low_ready, 1)
            for i in range(AFTER, END):
                experts.take_lo(pool, i + 1, (i + 1) % 2)

        @block.tensor
        def _(pe):
            pe.sem_inc(built_done, 2)
            experts.product(pe, TILES_BESIDE, 0, dots)
            with pe.Fori(0, TILES // 2) as k:
                for r in range(2):
                    n = 2 * k + r
                    experts.product(pe, TILES_BESIDE + n + 1, 1 - r, dots)
                    pe.wait_ge(high_ready, n + 1)
                    pe.wait_ge(low_ready, n + 1)
                    pe.wait_ge(built_out, n + 1)
                    for t in range(PER_TILE):
                        last = nc.tensor.matmul(built[:, t // 2, 2 * P * (t % 2):2 * P * (t % 2) + 2 * P],
                                                left[:, r, t], right[:, r, t].rearrange("p q n -> p (q n)"),
                                                start=True, stop=True)
                    last.then_inc(built_done, 1)
            for i in range(AFTER + 1, END):
                experts.product(pe, i, i % 2, dots)

        @block.scalar
        def _(act):
            for f in range(2):
                act.sem_inc(flushed[f], 16)

            def tile(i, r):
                experts.take_hi(act, i + 1, 1 - r)
                experts.finish(act, i, r, dots)

            tile(TILES_BESIDE, 0)
            with act.Fori(0, TILES // (2 * PER_CHUNK)) as c:
                for f in range(2):
                    with act.Fori(0, PER_CHUNK // 2) as k:
                        for r in range(2):
                            n = 2 * PER_CHUNK * c + 2 * k + PER_CHUNK * f + r
                            tile(TILES_BESIDE + n + 1, 1 - r)
                            act.wait_ge(built_done, n + 3)
                            act.wait_ge(built_out, n + 1)
                            nc.scalar.activation(low[:], built_of(1), ACT.Copy).then_inc(low_out, 1)
                    act.wait_ge(built_out, 2 * PER_CHUNK * c + PER_CHUNK * (f + 1) + 1)
                    act.dma_start(gates[2 * c + f], gate[:, f].rearrange("p n t -> p (n t)")) \
                        .then_inc(flushed[f], 16)
            for i in range(AFTER + 1, END):
                tile(i, i % 2)
            for f in range(2):
                act.wait_ge(flushed[f], 16 * (TILES // (2 * PER_CHUNK)) + 16)

        @block.vector
        def _(dve):
            v_ = nc.vector
            dve.wait_ge(count_loaded, 16)
            dve.sem_inc(built_out, 1)

            def one_hot_sides(n, r):
                dve.wait_ge(built_done, n + 1)
                v_.tensor_tensor(hot[:, r], *one_hots(n, 0), ALU.is_equal).then_inc(hot_ready, 1)
                v_.tensor_tensor(left[:, r], *one_hots(n, 1), ALU.is_equal)
                dve.wait_ge(hot_ready, n + 1)
                v_.tensor_tensor(right[:, r, :, 0], hot[:, r], weights(n, 0), ALU.mult).then_inc(high_ready, 1)

            def add(n, c, f, q):
                dve.wait_ge(low_out, n + 1)
                if q == 0:
                    dve.wait_ge(flushed[f], 16 * c + 16)
                v_.tensor_tensor(gate[:, f, :, PER_TILE * q:PER_TILE * q + PER_TILE], built_of(0), low[:],
                                 ALU.add).then_inc(built_out, 1)

            def chunk_pair(c, last):
                for f in range(2):
                    for q in range(PER_CHUNK):
                        n = 2 * PER_CHUNK * c + PER_CHUNK * f + q
                        if not (last and f == 1 and q == PER_CHUNK - 1):
                            one_hot_sides(n + 1, (q + 1) % 2)
                        add(n, c, f, q)

            one_hot_sides(0, 0)
            PAIRS = TILES // (2 * PER_CHUNK)
            with dve.Fori(0, PAIRS - 1) as c:
                chunk_pair(c, False)
            chunk_pair(PAIRS - 1, True)


class Sources:

    def __init__(self, nc, ctx, v_tab, gelus, gates):
        self.nc, self.gelus, self.gates = nc, gelus, gates
        self.v_tab = v_tab[0].rearrange("(n p) d -> n p d", p=P)
        self.raw, self.hi, self.lo, self.gelu, self.gate = tiles(
            nc, ctx, ("v_raw", [P, 2, D], F32), ("v_hi", [P, 2, GROUP, D], F32R), ("v_lo", [P, 2, GROUP, D], F32R),
            ("gelu_in", [P, 2, GROUP, T], F32), ("gate_in", [P, 2, T // TOK, GROUP * TOK], F32), side="right")
        self.w, w_hi, w_lo = tiles(
            nc, ctx, ("weights", [P, 2, T], F32), ("weights_hi0", [P, GROUP, T], F32R),
            ("weights_lo0", [P, GROUP, T], F32R), side="right")
        self.w_hi, self.w_lo = [w_hi], [w_lo]
        self.w_ready, self.steps = sems(nc, ctx, "w_ready w_steps")
        self.v_loaded = sems(nc, ctx, "v_loaded0 v_loaded1")
        self.in_loaded = sems(nc, ctx, "gelu_gate_loaded0 gelu_gate_loaded1")
        self.hi_taken, self.lo_taken = sems(nc, ctx, "v_hi_taken v_lo_taken")

    def load_in(self, sp, j, s):
        self.load_gelu(sp, j, s)
        self.load_gate(sp, j, s)

    def load_gelu(self, sp, j, s):
        sp.dma_start(self.gelu[:, s], self.gelus[bass.ds(GROUP * j, GROUP)].rearrange("q p t -> p q t")) \
            .then_inc(self.in_loaded[s], 16)

    def load_gate(self, sp, j, s):
        sp.dma_start(self.gate[:, s], self.gates.rearrange("c p n -> p c n")
                     [:, :, bass.ds(GROUP * TOK * j, GROUP * TOK)]).then_inc(self.in_loaded[s], 16)

    def load_v(self, sp, j, q):
        i = GROUP * j + q
        if not isinstance(i, int) or i >= 2:
            sp.wait_ge(self.lo_taken, i - 1)
        sp.dma_start(self.raw[:, q % 2], self.v_tab[i]).then_inc(self.v_loaded[q % 2], 16)

    def take_hi(self, act, j, s, q):
        act.wait_ge(self.v_loaded[q % 2], 16 * (2 * j + q // 2) + 16)
        self.nc.scalar.activation(self.hi[:, s, q], self.raw[:, q % 2], ACT.Copy).then_inc(self.hi_taken, 1)

    def take_lo(self, pool, j, s, q):
        pool.wait_ge(self.hi_taken, GROUP * j + q + 1)
        self.nc.gpsimd.tensor_tensor(self.lo[:, s, q], self.raw[:, q % 2], f32(self.hi[:, s, q]),
                                     ALU.subtract).then_inc(self.lo_taken, 1)

    def more(self, ctx):
        w_hi, w_lo = tiles(self.nc, ctx, ("weights_hi1", [P, GROUP, T], F32R), ("weights_lo1", [P, GROUP, T], F32R))
        self.w_hi.append(w_hi)
        self.w_lo.append(w_lo)

    def weigh(self, chain, s, q):
        v_ = self.nc.vector
        chain.step(v_.tensor_tensor(self.w[:, q % 2].rearrange("p (c t) -> p c t", t=TOK),
                                    self.gelu[:, s, q].rearrange("p (c t) -> p c t", t=TOK),
                                    self.gate[:, s, :, TOK * q:TOK * q + TOK], ALU.mult))
        chain.step(v_.tensor_copy(self.w_hi[s][:, q], self.w[:, q % 2]))
        v_.tensor_tensor(self.w_lo[s][:, q], self.w[:, q % 2], f32(self.w_hi[s][:, q]),
                         ALU.subtract).then_inc(self.w_ready, 1)


def last_experts(nc, experts, sources):
    FIRST = TILES_BESIDE + T // PER_TILE + TILES_AFTER
    TILES = N_KEYS - FIRST
    assert TILES > GROUP + 4
    with ExitStack() as ctx:
        dots, = banks(nc, ctx, ("dots_last", 2))
        block = ctx.enter_context(nc.Block())

        INPUTS = {GROUP + 1: (sources.load_gelu, 0), GROUP + 2: (sources.load_gate, 0),
                  GROUP + 3: (sources.load_gelu, 1), GROUP + 4: (sources.load_gate, 1)}
        V_TILE = {n + 1: n for n in range(GROUP)}

        @block.sync
        def _(sp):
            for n in range(TILES):
                if n + 2 < TILES:
                    experts.load(sp, FIRST + n + 2, n % 2)
                if n in INPUTS:
                    load, group = INPUTS[n]
                    load(sp, group, group)
                if n in V_TILE:
                    sources.load_v(sp, 0, V_TILE[n])

        @block.gpsimd
        def _(pool):
            for n in range(TILES):
                if n + 1 < TILES:
                    experts.take_lo(pool, FIRST + n + 1, 1 - n % 2)
                if n in V_TILE:
                    sources.take_lo(pool, 0, 0, V_TILE[n])

        @block.tensor
        def _(pe):
            pairs_of(pe, FIRST, N_KEYS, lambda i, r: experts.product(pe, i, r, dots))

        @block.scalar
        def _(act):
            for n in range(TILES):
                if n + 1 < TILES:
                    experts.take_hi(act, FIRST + n + 1, 1 - n % 2)
                experts.finish(act, FIRST + n, n % 2, dots)
                if n in V_TILE:
                    sources.take_hi(act, 0, 0, V_TILE[n])

        @block.vector
        def _(dve):
            sources.chain = Chain(dve, sources.steps)
            dve.sem_inc(sources.w_ready, 2 * GROUP)
            dve.wait_ge(sources.in_loaded[0], 32)
            for q in range(GROUP):
                if q >= 2:
                    dve.wait_ge(sources.w_ready, 2 * GROUP + q - 1)
                sources.weigh(sources.chain, 0, q)


def output(nc, a, experts, sources, x1_scaled, out):
    GROUPS = N_KEYS // GROUP
    BANKS = 8
    with ExitStack() as ctx:
        sources.more(ctx)
        sums, = banks(nc, ctx, ("sums", BANKS))
        w_ready = sources.w_ready
        bank_done, bank_added, half_normed, out_stored = sems(
            nc, ctx, "bank_done bank_added half_normed out_stored")
        norm = LayerNorm(nc, ctx, "ln2", 2)
        block = ctx.enter_context(nc.Block())

        def groups_of(engine, body):
            body(1, 1, True)
            with engine.Fori(1, GROUPS // 2) as jj:
                for s in range(2):
                    body(2 * jj + s, s, False)

        @block.sync
        def _(sp):
            norm.load(sp, a["ln2_g"], a["ln2_b"])
            for r in range(2):
                sp.wait_ge(experts.stored[r], 8 * N_KEYS + 16)

            def group(j, s, first):
                if not first:
                    sp.wait_ge(w_ready, GROUP * (j + 1))
                    sources.load_in(sp, j, s)
                for q in range(GROUP):
                    sources.load_v(sp, j, q)
            groups_of(sp, group)
            for u in range(2 * TT):
                t, columns = u // 2, slice(D // 2 * (u % 2), D // 2 * (u % 2) + D // 2)
                sp.wait_ge(half_normed, u + 1)
                sp.dma_start(out[0].rearrange("(t p) d -> t p d", p=P)[t][:, columns],
                             x1_scaled[:, t, columns]).then_inc(out_stored, 16)
            sp.wait_ge(out_stored, 16 * 2 * TT)

        @block.gpsimd
        def _(pool):
            def group(j, s, first):
                for q in range(GROUP):
                    sources.take_lo(pool, j, s, q)
            groups_of(pool, group)

        @block.tensor
        def _(pe):
            pe.sem_inc(bank_done, 2 * 8)
            with pe.Fori(0, GROUPS // 2) as jj:
                for s in range(2):
                    j = 2 * jj + s
                    for b in range(8):
                        t, g = b // 2, b % 2
                        pe.wait_ge(bank_added, 8 * j + b + 1)
                        for q in range(GROUP):
                            if b == 0:
                                pe.wait_ge(sources.lo_taken, GROUP * j + q + 1)
                                pe.wait_ge(w_ready, GROUP * j + q + 1 + 2 * GROUP)
                            tokens, columns = slice(P * t, P * t + P), slice(512 * g, 512 * g + 512)
                            to = sums[:, b % BANKS]
                            v_hi, v_lo = sources.hi[:, s, q, columns], sources.lo[:, s, q, columns]
                            w_hi, w_lo = sources.w_hi[s][:, q, tokens], sources.w_lo[s][:, q, tokens]
                            nc.tensor.matmul(to, w_hi, v_hi, start=(q == 0), stop=False)
                            nc.tensor.matmul(to, w_hi, v_lo, start=False, stop=False)
                            last = nc.tensor.matmul(to, w_lo, v_hi, start=False, stop=(q == GROUP - 1))
                        last.then_inc(bank_done, 1)

        @block.scalar
        def _(act):
            def group(j, s, first):
                if not first:
                    act.wait_ge(bank_done, 8 * j + 8)
                for q in range(GROUP):
                    sources.take_hi(act, j, s, q)
            groups_of(act, group)
            for t in range(TT):
                norm.root(act, t)

        @block.vector
        def _(dve):
            v_ = nc.vector
            chain = sources.chain
            chain.engine = dve
            dve.sem_inc(bank_added, BANKS)

            def weigh(j, s, q):
                if q == 0:
                    dve.wait_ge(sources.in_loaded[s], 16 * (j - s) + 32)
                    dve.wait_ge(bank_done, 8 * j + 8)
                dve.wait_ge(w_ready, GROUP * j + q - 1 + 2 * GROUP)
                sources.weigh(chain, s, q)

            def add(j, b):
                t, g = b // 2, b % 2
                to = x1_scaled[:, t, 512 * g:512 * g + 512]
                dve.wait_ge(bank_done, 8 * j + b + 17)
                v_.tensor_tensor(to, to, sums[:, b % BANKS], ALU.add).then_inc(bank_added, 1)

            def group(j, s):
                for b in range(8):
                    add(j, b)
                    if b in (0, 1, 3, 5):
                        weigh(j + 1, 1 - s, (b + 1) // 2)

            with dve.Fori(0, GROUPS // 2 - 1) as jj:
                chain.round(jj, 2 * GROUP * 2)
                group(2 * jj, 0)
                group(2 * jj + 1, 1)
            chain.done(GROUPS // 2 - 1)
            group(GROUPS - 2, 0)
            norm.begin(dve)
            def add_last(b):
                add(GROUPS - 1, b)
                return BANKS + 8 * (GROUPS - 1) + b + 1

            for t in range(TT):
                added = add_last(2 * t)
                if t:
                    norm.finish(x1_scaled, t - 1, 2, half_normed)
                dve.wait_ge(bank_added, added)
                norm.piece(x1_scaled, t, 0)
                dve.wait_ge(bank_added, add_last(2 * t + 1))
                norm.piece(x1_scaled, t, 1)
                norm.variance(t)
                norm.centre(x1_scaled, t)
            norm.finish(x1_scaled, TT - 1, 2, half_normed)


def block_program(nc, a, gelus, gates, out):
    with ExitStack() as whole:
        identity, = tiles(nc, whole, ("identity", [P, P], F32))
        xT = tiles(nc, whole, ("xT_hi", [P, DT, T], F32R), ("xT_lo", [P, DT, T], F32R))
        with ExitStack() as front:
            stream = Stream(nc, front, a["w_chunks"])
            with ExitStack() as merging:
                with ExitStack() as mixing:
                    conv = tiles(nc, mixing, ("conv_hi", [P, DT, T], F32R), ("conv_lo", [P, DT, T], F32R))
                    attn = tiles(nc, mixing, ("attn_hi", [P, DT, T], F32R), ("attn_lo", [P, DT, T], F32R))
                    gate, gate_b = tiles(nc, mixing, ("gate", [P, 2, 2, T], F32), ("gate_b", [P, 2 * DT], F32))
                    mixers(nc, a, stream, identity, xT, conv, attn, gate, gate_b)
                    merged = tiles(nc, merging, ("merged_hi", [P, DT, T], F32R), ("merged_lo", [P, DT, T], F32R),
                                   side="right")
                    merge(nc, a, stream, merged, xT, conv, attn, gate, gate_b)
                x1, = tiles(nc, whole, ("x1", [P, TT, D], F32))
                norm1(nc, a, stream, identity, merged, x1, xT)
            dotting = whole.enter_context(ExitStack())
            experts = Experts(nc, dotting, whole, a["u_columns"], xT, gelus)
            numbers, *parts = tiles(nc, dotting, ("numbers", [P, 2, T], BF16), ("weight_hi", [P, T], F32R),
                                    ("weight_lo", [P, T], F32))
            keys(nc, a, stream, experts, identity, xT, x1, numbers, parts)
        gate_matrix(nc, a, experts, numbers, parts, gates)
        sources = Sources(nc, whole, a["v_tab"], gelus, gates)
        last_experts(nc, experts, sources)
        dotting.close()
        output(nc, a, experts, sources, x1, out)


def laid_out(i):
    def chunk(w, first, j):
        at = first + CW * j
        return w[0][:, at:at + CW].reshape(DT, P, CW).transpose(1, 0, 2)

    def columns(v):
        v = v.reshape(*v.shape[:-1], -1, P)
        return np.ascontiguousarray(np.moveaxis(v, -1, 0))

    h, b, c, q, k, v, conv_gate, attn_gate = (D * n for n in range(8))
    w = [chunk(i["w_in"], at, j) for j in range(MIX_ROUNDS) for at in (q, k, v, h, b, c)]
    for j in range(MERGE_ROUNDS):
        w += [chunk(i["w_in"], conv_gate, j), chunk(i["w_in"], attn_gate, j), chunk(i["w_conv_out"], 0, j),
              chunk(i["w_attn_out"], 0, j)]
    w += [chunk(i["w_o"], 0, j) for j in range(D // CW)]
    w += [chunk(i["w_pq"], 0, j) for j in range(PK_HEADS)]

    inverse = ROPE_THETA ** (-np.arange(0, ROT_DIM, 2, dtype=np.float32) / ROT_DIM)
    freq = np.stack([np.zeros(P, np.float32), np.ones(P, np.float32)], axis=1)
    for n in range(HALF_ROT):
        for component in range(2):
            r1, r2 = HD * component + n, HD * component + HALF_ROT + n
            freq[r1, 0] = freq[r2, 0] = inverse[n]
            freq[r1, 1] = -1.0
    below = np.arange(P)[None, :] <= np.arange(P)[:, None]
    kept = ("x", "positions", "lambda_q1", "lambda_k1", "lambda_q2", "lambda_k2", "subln_g", "ln1_g", "ln1_b",
            "ln2_g", "ln2_b", "v_tab")
    return {n: i[n] for n in kept} | {
        "x_columns": np.ascontiguousarray(i["x"][0].T.reshape(DT, P, T).transpose(1, 0, 2)),
        "w_chunks": np.stack(w),
        "conv_w_columns": columns(i["conv_w"][0]),
        "conv_b_columns": columns(i["conv_b"][0]),
        "gate_b_columns": columns(i["gate_b"][0]),
        "sub_keys_columns": np.ascontiguousarray(i["sub_keys"][0].transpose(0, 3, 1, 2)),
        "u_columns": np.ascontiguousarray(i["u_tab"][0].reshape(N_KEYS, P, DT, P).transpose(0, 3, 2, 1)),
        "identity": np.eye(P, dtype=np.float32),
        "freq": freq,
        "mask": np.where(below, 0.0, NEG).astype(np.float32),
        "count": np.ascontiguousarray(np.broadcast_to(np.arange(P, dtype=np.float32), (P, P))),
    }


def kernel(**inputs):
    import concourse.bacc as bacc
    from concourse.bass_utils import run_bass_kernel_spmd

    nc = bacc.Bacc("TRN2", target_bir_lowering=False, num_devices=1)
    arrays = laid_out({n: np.asarray(v) for n, v in inputs.items()})
    a = {n: nc.dram_tensor(f"in_{n}", v.shape, mybir.dt.from_np(v.dtype), kind="ExternalInput").ap()
         for n, v in arrays.items()}
    gelus = nc.dram_tensor("gelus", [N_KEYS, P, T], F32, kind="Internal").ap()
    gates = nc.dram_tensor("gates", [T // TOK, P, N_KEYS * TOK], F32, kind="Internal").ap()
    out = nc.dram_tensor("out", (1, T, D), F32, kind="ExternalOutput").ap()
    block_program(nc, a, gelus, gates, out)
    r = run_bass_kernel_spmd(nc, [{f"in_{n}": v for n, v in arrays.items()}], core_ids=[0])
    return r.results[0]["out"]
```
